# Optimizing a Trainium2 kernel written in Bass

```python
import jax, jax.numpy as jnp
from jax import lax
import numpy as np

D_MODEL = 1024
BATCH = 1
SEQ = 256
DEPTH = 2

HEAD_DIM = 64
ROPE_THETA = 10000.0
RMS_EPS = 1e-6
QBLK = 128
NEG_INF = -1e30

GRID_W = 64
NA_HEADS = 8
NA_ROWS = 8
NA_COLS = 16
NA_WIDTH = NA_HEADS * HEAD_DIM

MLA_HEADS = 8
MLA_Q_RANK = 256
MLA_KV_RANK = 128
MLA_NOPE = 64
MLA_ROPE = 32
MLA_V = 64

DIL_PAIRS = ((128, 1), (512, 4), (2048, 16))
DIL_GROUPS = len(DIL_PAIRS)
DIL_HEADS = D_MODEL // HEAD_DIM

D_FF = 4 * D_MODEL
N_EVEN = (DEPTH + 1) // 2
N_ODD = DEPTH // 2

EVEN_IN = 3 * NA_WIDTH + MLA_Q_RANK + MLA_KV_RANK + MLA_ROPE
EVEN_MIX = NA_WIDTH + MLA_HEADS * MLA_V
ODD_IN = DIL_GROUPS * 3 * DIL_HEADS * HEAD_DIM
ODD_MIX = DIL_HEADS * HEAD_DIM


def rms_norm(x, g):
    xf = x.astype(jnp.float32)
    y = xf * lax.rsqrt(jnp.mean(xf * xf, axis=-1, keepdims=True) + RMS_EPS)
    return (y * g.astype(jnp.float32)).astype(x.dtype)

def rope_tables(seq_len, dim):
    inv = 1.0 / (ROPE_THETA ** (jnp.arange(0, dim, 2, dtype=jnp.float32) / dim))
    ang = jnp.arange(seq_len, dtype=jnp.float32)[:, None] * inv[None, :]
    return jnp.cos(ang), jnp.sin(ang)

def apply_rope(x, cos, sin):
    half = x.shape[-1] // 2
    shp = (1, cos.shape[0]) + (1,) * (x.ndim - 3) + (cos.shape[1],)
    c = cos.reshape(shp).astype(x.dtype)
    s = sin.reshape(shp).astype(x.dtype)
    x1, x2 = x[..., :half], x[..., half:]
    return jnp.concatenate([x1 * c - x2 * s, x2 * c + x1 * s], axis=-1)

def neighbourhood_attention(q, k, v, rpb):
    b, s, h, dh = q.shape
    rows = s // GRID_W
    wr = min(NA_ROWS, rows)
    wc = NA_COLS
    qg = q.reshape(b, rows, GRID_W, h, dh)
    kg = k.reshape(b, rows, GRID_W, h, dh)
    vg = v.reshape(b, rows, GRID_W, h, dh)
    cols = jnp.arange(GRID_W)
    col_start = jnp.clip(cols - wc // 2, 0, GRID_W - wc)
    col_idx = col_start[:, None] + jnp.arange(wc)[None, :]
    col_rel = col_idx - cols[:, None] + (NA_COLS - 1)
    scale = dh ** -0.5

    def row_fn(r):
        r_start = jnp.clip(r - wr // 2, 0, rows - wr)
        row_rel = r_start + jnp.arange(wr) - r + (NA_ROWS - 1)
        q_row = lax.dynamic_index_in_dim(qg, r, axis=1, keepdims=False)
        k_rows = lax.dynamic_slice_in_dim(kg, r_start, wr, axis=1)
        v_rows = lax.dynamic_slice_in_dim(vg, r_start, wr, axis=1)
        k_win = k_rows[:, :, col_idx]
        v_win = v_rows[:, :, col_idx]
        sc = jnp.einsum('bchd,bicjhd->bhcij', q_row, k_win,
                        preferred_element_type=jnp.float32) * scale
        bias = rpb[:, row_rel[:, None, None], col_rel[None, :, :]]
        sc = sc + bias.transpose(0, 2, 1, 3).astype(jnp.float32)[None]
        p = jax.nn.softmax(sc.reshape(b, h, GRID_W, wr * wc), axis=-1).reshape(sc.shape)
        return jnp.einsum('bhcij,bicjhd->bchd', p.astype(v.dtype), v_win)

    out = lax.map(row_fn, jnp.arange(rows))
    return out.transpose(1, 0, 2, 3, 4).reshape(b, s, h * dh)

def dense_attention(q, k, v, scale):
    b, s, h, dq = q.shape
    nblk = s // QBLK
    qb = q.reshape(b, nblk, QBLK, h, dq).transpose(1, 0, 2, 3, 4)

    def blk(qi):
        sc = jnp.einsum('bqhd,bkhd->bhqk', qi, k, preferred_element_type=jnp.float32) * scale
        p = jax.nn.softmax(sc, axis=-1)
        return jnp.einsum('bhqk,bkhd->bqhd', p.astype(v.dtype), v)

    out = lax.map(blk, qb)
    return out.transpose(1, 0, 2, 3, 4).reshape(b, s, h * v.shape[-1])

def dilated_attention(q, k, v):
    b, s, g, h, dh = q.shape
    nblk = s // QBLK
    scale = dh ** -0.5
    offsets = [jnp.arange(-(w // 2), w // 2 + 1, d) for (w, d) in DIL_PAIRS]
    ks = [k[:, :, gi] for gi in range(g)]
    vs = [v[:, :, gi] for gi in range(g)]

    def blk(bi):
        start = bi * QBLK
        qpos = start + jnp.arange(QBLK)
        q_blk = lax.dynamic_slice_in_dim(q, start, QBLK, axis=1)
        outs, lses = [], []
        for gi in range(g):
            kpos = qpos[:, None] + offsets[gi][None, :]
            valid = (kpos >= 0) & (kpos < s)
            kidx = jnp.clip(kpos, 0, s - 1)
            k_sel = ks[gi][:, kidx]
            v_sel = vs[gi][:, kidx]
            sc = jnp.einsum('bqhd,bqjhd->bhqj', q_blk[:, :, gi], k_sel,
                            preferred_element_type=jnp.float32) * scale
            sc = jnp.where(valid[None, None], sc, NEG_INF)
            m = jnp.max(sc, axis=-1, keepdims=True)
            e = jnp.exp(sc - m)
            z = jnp.sum(e, axis=-1, keepdims=True)
            o = jnp.einsum('bhqj,bqjhd->bqhd', (e / z).astype(v.dtype), v_sel)
            outs.append(o.astype(jnp.float32))
            lses.append((m + jnp.log(z))[..., 0])
        lse = jnp.stack(lses, axis=0)
        wgt = jax.nn.softmax(lse, axis=0).transpose(0, 1, 3, 2)[..., None]
        out = jnp.sum(wgt * jnp.stack(outs, axis=0), axis=0)
        return out.astype(v.dtype)

    out = lax.map(blk, jnp.arange(nblk))
    return out.transpose(1, 0, 2, 3, 4).reshape(b, s, h * dh)

def even_mixer(xn, w_in, rpb, q_norm, w_uq, kv_norm, w_ukv, w_o, cos_r, sin_r):
    b, s, _ = xn.shape
    hcat = xn @ w_in
    o0 = 3 * NA_WIDTH
    o1 = o0 + MLA_Q_RANK
    o2 = o1 + MLA_KV_RANK
    a_qkv = hcat[..., :o0].reshape(b, s, 3, NA_HEADS, HEAD_DIM)
    out_a = neighbourhood_attention(a_qkv[:, :, 0], a_qkv[:, :, 1], a_qkv[:, :, 2], rpb)
    c_q = rms_norm(hcat[..., o0:o1], q_norm)
    c_kv = rms_norm(hcat[..., o1:o2], kv_norm)
    k_pe = apply_rope(hcat[..., o2:][:, :, None, :], cos_r, sin_r)
    q = (c_q @ w_uq).reshape(b, s, MLA_HEADS, MLA_NOPE + MLA_ROPE)
    q = jnp.concatenate([q[..., :MLA_NOPE], apply_rope(q[..., MLA_NOPE:], cos_r, sin_r)], axis=-1)
    kv = (c_kv @ w_ukv).reshape(b, s, MLA_HEADS, MLA_NOPE + MLA_V)
    k = jnp.concatenate([kv[..., :MLA_NOPE],
                         jnp.broadcast_to(k_pe, (b, s, MLA_HEADS, MLA_ROPE))], axis=-1)
    v = kv[..., MLA_NOPE:]
    out_b = dense_attention(q, k, v, (MLA_NOPE + MLA_ROPE) ** -0.5)
    return jnp.concatenate([out_a, out_b], axis=-1) @ w_o

def odd_mixer(xn, w_in, w_o, cos_f, sin_f):
    b, s, _ = xn.shape
    hcat = (xn @ w_in).reshape(b, s, DIL_GROUPS, 3, DIL_HEADS, HEAD_DIM)
    q = apply_rope(hcat[:, :, :, 0], cos_f, sin_f)
    k = apply_rope(hcat[:, :, :, 1], cos_f, sin_f)
    v = hcat[:, :, :, 2]
    return dilated_attention(q, k, v) @ w_o

def sq_relu_mlp(xn, w1, w2):
    return jnp.square(jax.nn.relu(xn @ w1)) @ w2

def first_inputs(seed: int = 0) -> dict:
    key = jax.random.key(seed)
    ks = jax.random.split(key, 16)
    f32 = jnp.float32

    def nrm(k, shape, scale):
        return jax.random.normal(k, shape, f32) * scale

    return {
        "x": nrm(ks[0], (BATCH, SEQ, D_MODEL), 1.0),
        "norm_mix": 1.0 + nrm(ks[1], (DEPTH, D_MODEL), 0.1),
        "norm_mlp": 1.0 + nrm(ks[2], (DEPTH, D_MODEL), 0.1),
        "norm_final": 1.0 + nrm(ks[3], (D_MODEL,), 0.1),
        "ev_w_in": nrm(ks[4], (N_EVEN, D_MODEL, EVEN_IN), D_MODEL ** -0.5),
        "ev_rpb": nrm(ks[5], (N_EVEN, NA_HEADS, 2 * NA_ROWS - 1, 2 * NA_COLS - 1), 0.5),
        "ev_q_norm": 1.0 + nrm(ks[6], (N_EVEN, MLA_Q_RANK), 0.1),
        "ev_w_uq": nrm(ks[7], (N_EVEN, MLA_Q_RANK, MLA_HEADS * (MLA_NOPE + MLA_ROPE)), MLA_Q_RANK ** -0.5),
        "ev_kv_norm": 1.0 + nrm(ks[8], (N_EVEN, MLA_KV_RANK), 0.1),
        "ev_w_ukv": nrm(ks[9], (N_EVEN, MLA_KV_RANK, MLA_HEADS * (MLA_NOPE + MLA_V)), MLA_KV_RANK ** -0.5),
        "ev_w_o": nrm(ks[10], (N_EVEN, EVEN_MIX, D_MODEL), EVEN_MIX ** -0.5),
        "od_w_in": nrm(ks[11], (N_ODD, D_MODEL, ODD_IN), D_MODEL ** -0.5),
        "od_w_o": nrm(ks[12], (N_ODD, ODD_MIX, D_MODEL), ODD_MIX ** -0.5),
        "mlp_w1": nrm(ks[13], (DEPTH, D_MODEL, D_FF), D_MODEL ** -0.5),
        "mlp_w2": nrm(ks[14], (DEPTH, D_FF, D_MODEL), D_FF ** -0.5),
    }

def first_block(x, norm_mix, norm_mlp, norm_final, ev_w_in, ev_rpb, ev_q_norm, ev_w_uq,
              ev_kv_norm, ev_w_ukv, ev_w_o, od_w_in, od_w_o, mlp_w1, mlp_w2):
    s = x.shape[1]
    cos_r, sin_r = rope_tables(s, MLA_ROPE)
    cos_f, sin_f = rope_tables(s, HEAD_DIM)
    for layer in range(DEPTH):
        xn = rms_norm(x, norm_mix[layer])
        if layer % 2 == 0:
            e = layer // 2
            x = x + even_mixer(xn, ev_w_in[e], ev_rpb[e], ev_q_norm[e], ev_w_uq[e],
                               ev_kv_norm[e], ev_w_ukv[e], ev_w_o[e], cos_r, sin_r)
        else:
            o = layer // 2
            x = x + odd_mixer(xn, od_w_in[o], od_w_o[o], cos_f, sin_f)
        x = x + sq_relu_mlp(rms_norm(x, norm_mlp[layer]), mlp_w1[layer], mlp_w2[layer])
    return rms_norm(x, norm_final)


N_A = DEPTH // 2
N_B = DEPTH - N_A
MEM_LEN = 256
MEM_HEADS = 4
MEM_HEAD_DIM = D_MODEL // 8
MEM_WIDTH = MEM_HEADS * MEM_HEAD_DIM
CONV_DIM = D_MODEL
CONV_WIDTH = 3
FOX_HEADS = 8
FOX_HEAD_DIM = D_MODEL // FOX_HEADS
FOX_WIDTH = FOX_HEADS * FOX_HEAD_DIM
D_FF_2 = ((8 * D_MODEL // 3 + 255) // 256) * 256
Q_BLOCK = 128
NEG_INF_2 = float(np.finfo(np.float32).min)


def rmsnorm(x, g):
    xf = x.astype(jnp.float32)
    y = xf * lax.rsqrt(jnp.mean(xf * xf, axis=-1, keepdims=True) + RMS_EPS)
    return (y * g.astype(jnp.float32)).astype(x.dtype)

def swiglu(h, w_gate_up, w_down):
    gu = h @ w_gate_up
    gate, up = gu[..., :D_FF_2], gu[..., D_FF_2:]
    return (jax.nn.silu(gate) * up) @ w_down

def causal_depthwise_conv(u, w):
    c = u.shape[-1]
    return lax.conv_general_dilated(
        u, w[:, None, :].astype(u.dtype), window_strides=(1,),
        padding=[(CONV_WIDTH - 1, 0)],
        dimension_numbers=('NWC', 'WIO', 'NWC'),
        feature_group_count=c)

def memory_attention(q, mk, mv):
    b, s, h, dh = q.shape
    logits = jnp.einsum('bshd,bmhd->bhsm', q, mk,
                        preferred_element_type=jnp.float32) * (dh ** -0.5)
    p = jax.nn.softmax(logits, axis=-1).astype(mv.dtype)
    return jnp.einsum('bhsm,bmhd->bshd', p, mv).reshape(b, s, h * dh)

def forgetting_attention(q, k, v, logf_cum):
    b, s, h, dh = q.shape
    nb = s // Q_BLOCK
    qb = q.reshape(b, nb, Q_BLOCK, h, dh).transpose(1, 0, 2, 3, 4)
    cb = logf_cum.reshape(b, h, nb, Q_BLOCK).transpose(2, 0, 1, 3)
    k_pos = jnp.arange(s)
    scale = dh ** -0.5

    def block(args):
        q_blk, c_blk, i = args
        q_pos = i * Q_BLOCK + jnp.arange(Q_BLOCK)
        logits = jnp.einsum('bqhd,bkhd->bhqk', q_blk, k,
                            preferred_element_type=jnp.float32) * scale
        logits = logits + c_blk[..., :, None] - logf_cum[:, :, None, :]
        causal = k_pos[None, :] <= q_pos[:, None]
        logits = jnp.where(causal, logits, NEG_INF_2)
        p = jax.nn.softmax(logits, axis=-1).astype(v.dtype)
        return jnp.einsum('bhqk,bkhd->bqhd', p, v)

    out = lax.map(block, (qb, cb, jnp.arange(nb)))
    return out.transpose(1, 0, 2, 3, 4).reshape(b, s, h * dh)

def second_inputs(seed: int = 0) -> dict:
    key = jax.random.key(seed)
    ks = jax.random.split(key, 20)
    f32 = jnp.float32

    def w(k, shape, fan_in):
        return jax.random.normal(k, shape, f32) * (fan_in ** -0.5)

    def gain(k, shape):
        return 1.0 + 0.02 * jax.random.normal(k, shape, f32)

    a_in_cols = 3 * CONV_DIM + MEM_WIDTH
    b_in_cols = FOX_WIDTH + MEM_WIDTH
    return {
        'x': jax.random.normal(ks[0], (BATCH, SEQ, D_MODEL), f32),
        'mem': jax.random.normal(ks[1], (BATCH, MEM_LEN, D_MODEL), f32),
        'ffn_norm': gain(ks[2], (DEPTH, 2, D_MODEL)),
        'ffn_w_gate_up': w(ks[3], (DEPTH, 2, D_MODEL, 2 * D_FF_2), D_MODEL),
        'ffn_w_down': w(ks[4], (DEPTH, 2, D_FF_2, D_MODEL), D_FF_2),
        'mix_norm': gain(ks[5], (DEPTH, D_MODEL)),
        'mem_norm': gain(ks[6], (D_MODEL,)),
        'mem_w_kv': w(ks[7], (DEPTH, D_MODEL, 2 * MEM_WIDTH), D_MODEL),
        'a_w_in': w(ks[8], (N_A, D_MODEL, a_in_cols), D_MODEL),
        'a_conv_w': w(ks[9], (N_A, CONV_WIDTH, CONV_DIM), CONV_WIDTH),
        'a_w_out': w(ks[10], (N_A, CONV_DIM + MEM_WIDTH, D_MODEL), CONV_DIM + MEM_WIDTH),
        'kv_norm': gain(ks[11], (D_MODEL,)),
        'w_kvf': w(ks[12], (D_MODEL, 2 * FOX_WIDTH + FOX_HEADS), D_MODEL),
        'b_f': jax.random.uniform(ks[13], (FOX_HEADS,), f32, minval=1.0, maxval=6.0),
        'b_w_q': w(ks[14], (N_B, D_MODEL, b_in_cols), D_MODEL),
        'b_w_out': w(ks[15], (N_B, FOX_WIDTH + MEM_WIDTH, D_MODEL), FOX_WIDTH + MEM_WIDTH),
        'final_norm': gain(ks[16], (D_MODEL,)),
    }

def second_block(x, mem, ffn_norm, ffn_w_gate_up, ffn_w_down, mix_norm, mem_norm,
              mem_w_kv, a_w_in, a_conv_w, a_w_out, kv_norm, w_kvf, b_f,
              b_w_q, b_w_out, final_norm):
    b, s, _ = x.shape
    m = mem.shape[1]
    mem_n = rmsnorm(mem, mem_norm)
    k_sh = v_sh = c_sh = None

    for l in range(DEPTH):
        if l == N_A:
            hkv = rmsnorm(x, kv_norm)
            kvf = hkv @ w_kvf
            k_sh = kvf[..., :FOX_WIDTH].reshape(b, s, FOX_HEADS, FOX_HEAD_DIM)
            v_sh = kvf[..., FOX_WIDTH:2 * FOX_WIDTH].reshape(b, s, FOX_HEADS, FOX_HEAD_DIM)
            f_logit = (kvf[..., 2 * FOX_WIDTH:] + b_f).astype(jnp.float32)
            c_sh = jnp.cumsum(jax.nn.log_sigmoid(f_logit), axis=1).transpose(0, 2, 1)

        x = x + 0.5 * swiglu(rmsnorm(x, ffn_norm[l, 0]), ffn_w_gate_up[l, 0], ffn_w_down[l, 0])

        h = rmsnorm(x, mix_norm[l])
        mkv = mem_n @ mem_w_kv[l]
        mk = mkv[..., :MEM_WIDTH].reshape(b, m, MEM_HEADS, MEM_HEAD_DIM)
        mv = mkv[..., MEM_WIDTH:].reshape(b, m, MEM_HEADS, MEM_HEAD_DIM)
        if l < N_A:
            i = l
            proj = h @ a_w_in[i]
            gate_b = proj[..., :CONV_DIM]
            gate_c = proj[..., CONV_DIM:2 * CONV_DIM]
            u = proj[..., 2 * CONV_DIM:3 * CONV_DIM]
            qm = proj[..., 3 * CONV_DIM:].reshape(b, s, MEM_HEADS, MEM_HEAD_DIM)
            y_tok = gate_b * causal_depthwise_conv(gate_c * u, a_conv_w[i])
            y_mem = memory_attention(qm, mk, mv)
            x = x + jnp.concatenate([y_tok, y_mem], axis=-1) @ a_w_out[i]
        else:
            j = l - N_A
            proj = h @ b_w_q[j]
            q = proj[..., :FOX_WIDTH].reshape(b, s, FOX_HEADS, FOX_HEAD_DIM)
            qm = proj[..., FOX_WIDTH:].reshape(b, s, MEM_HEADS, MEM_HEAD_DIM)
            y_tok = forgetting_attention(q, k_sh, v_sh, c_sh)
            y_mem = memory_attention(qm, mk, mv)
            x = x + jnp.concatenate([y_tok, y_mem], axis=-1) @ b_w_out[j]

        x = x + 0.5 * swiglu(rmsnorm(x, ffn_norm[l, 1]), ffn_w_gate_up[l, 1], ffn_w_down[l, 1])

    return rmsnorm(x, final_norm)


def setup_inputs(seed=0):
    out = dict(first_inputs(seed))
    for name, value in second_inputs(seed + 1).items():
        if name != "x":
            out[name + "_2"] = value
    return out


def reference(
    x, norm_mix, norm_mlp, norm_final, ev_w_in, ev_rpb, ev_q_norm, ev_w_uq, ev_kv_norm,
    ev_w_ukv, ev_w_o, od_w_in, od_w_o, mlp_w1, mlp_w2, mem_2, ffn_norm_2, ffn_w_gate_up_2,
    ffn_w_down_2, mix_norm_2, mem_norm_2, mem_w_kv_2, a_w_in_2, a_conv_w_2, a_w_out_2,
    kv_norm_2, w_kvf_2, b_f_2, b_w_q_2, b_w_out_2, final_norm_2,
):
    x = first_block(
        x, norm_mix, norm_mlp, norm_final, ev_w_in, ev_rpb, ev_q_norm, ev_w_uq, ev_kv_norm,
        ev_w_ukv, ev_w_o, od_w_in, od_w_o, mlp_w1, mlp_w2,
    )
    return second_block(
        x, mem_2, ffn_norm_2, ffn_w_gate_up_2, ffn_w_down_2, mix_norm_2, mem_norm_2, mem_w_kv_2,
        a_w_in_2, a_conv_w_2, a_w_out_2, kv_norm_2, w_kvf_2, b_f_2, b_w_q_2, b_w_out_2,
        final_norm_2,
    )


_drawn_inputs = setup_inputs


def setup_inputs(seed=0):
    import zlib

    import numpy as np

    out = dict(_drawn_inputs(seed))
    spreads = {}
    factors = {'ev_q_norm': 3.533,
     'ffn_norm_2': 3.611,
     'mem_norm_2': 8.0,
     'kv_norm_2': 8.0,
     'final_norm_2': 2.714}
    for name, (base, spread) in spreads.items():
        noise = np.random.default_rng([zlib.crc32(name.encode()), seed]).standard_normal(out[name].shape)
        drawn = base * np.exp(spread * noise) if base else spread * noise
        out[name] = __import__('jax').numpy.asarray(drawn.astype(out[name].dtype))
    for name, factor in factors.items():
        out[name] = (out[name] * factor).astype(out[name].dtype)
    return out
```

```python
from contextlib import ExitStack

import numpy as np

import concourse.bass as bass
from concourse import mybir

F32 = mybir.dt.float32
F32R = mybir.dt.float32r
ALU = mybir.AluOpType
ACT = mybir.ActivationFunctionType
AXIS = mybir.AxisListType

P = 128
S = 256
TT = S // P
D = 1024
KD = D // P
CH = 2048
TCOLS = CH // KD
EPS = 1e-6
NEG = -1e30
NA_H, NA_W = 8, 512
DIL_G, DIL_H = 3, 16
FF1, FF2 = 4096, 2816
ROWS, GRID = 4, 64
SLOTS = 6

CONST = {}
_at = 0
for _name, _n in (("ident", P), ("dil", TT * DIL_G * S), ("causal", TT * S), ("window", GRID),
                  ("cosd", TT * 64), ("sind", TT * 64), ("cosm", TT * 32), ("sinm", TT * 32),
                  ("tri", TT * S)):
    CONST[_name] = (_at, _at + _n)
    _at += _n
NCONST = _at

GAINS = {}
_at = 0
for _name, _n in (("mix0", KD), ("mix1", KD), ("mlp0", KD), ("mlp1", KD), ("ffn00", KD),
                  ("ffn01", KD), ("ffn10", KD), ("ffn11", KD), ("bmix0", KD), ("bmix1", KD),
                  ("mem", KD), ("kv", KD), ("q_norm", 2), ("ckv_norm", 1), ("conv", 3 * KD),
                  ("b_f", 8)):
    GAINS[_name] = _at
    _at += _n
NGAIN = _at


class Count:

    def __init__(self, sem):
        self.sem, self.n, self.dyn = sem, 0, 0

    def inc(self, ins):
        self.n += 1
        ins.then_inc(self.sem, 1)

    def value(self):
        return self.dyn + self.n


def repeat(engine, n, body, counts=(), straight=False):
    if straight or n < 2:
        for i in range(n):
            body(i)
        return
    with engine.Fori(0, n) as i:
        start = [c.n for c, _ in counts]
        for c, per in counts:
            c.dyn = i * per
        body(i)
        for (c, per), was in zip(counts, start):
            assert c.n - was == per, (c.n, was, per)
            c.dyn, c.n = 0, was + per * n


class Plan:

    def __init__(self):
        self.stages, self.g, self.u, self.down = [], 0, 0, 0

    def add(self, kind, name, chunks=0, uses=0, **more):
        st = dict(kind=kind, name=name, g=self.g, u=self.u, n=chunks, down=self.down, **more)
        self.g += chunks
        self.u += uses
        self.down += kind == "down"
        self.stages.append(st)
        return st


def make_plan(w):
    p = Plan()

    def norm(gain, src="x"):
        p.add("norm", "norm_" + gain, gain=GAINS[gain], src=src)

    def up(name, weight, col, chunks, **more):
        p.add("up", name, chunks, chunks, w=weight, col=col, **more)

    def natural(name, weight, col, blocks, ncols=512, **more):
        p.add("natural", name, 2 * blocks, blocks, w=weight, col=col, blocks=blocks,
              ncols=ncols, **more)

    def down(name, weight, rows, scale=1.0, ncols=D, ks=2, after="x", src="h", **more):
        p.add("down", name, rows // (ks * P), 0, w=weight, scale=scale, ncols=ncols, ks=ks,
              after=after, src=src, **more)

    norm("mix0")
    up("na_qk", w["ev_w_in"], 0, 4, post="copy", dest="na_qk")
    natural("na_v", w["ev_w_in"], 1024, 1, dest="na_v")
    natural("latent", w["ev_w_in"], 1536, 1, ncols=416, dest="latent")
    p.add("mla_in", "mla_in")
    down("uq", w["ev_w_uq"], 256, ncols=768, after="q", src="c")
    down("ukv", w["ev_w_ukv"], 128, ks=1, after="kv", src="c")
    p.add("mla_qk", "mla_qk")
    p.add("attend", "even", what=[("na", h) for h in range(8)] + [("mla", h) for h in range(8)])
    down("ev_o", w["ev_w_o"], 1024)
    norm("mlp0")
    up("mlp_up", w["mlp_w1"][0], 0, FF1 // TCOLS, post="relu2", dest="h")
    down("mlp_down", w["mlp_w2"][0], FF1)
    norm("mix1")
    p.add("dilated_in", "dilated_in", DIL_G * 12, DIL_G * 6, w=w["od_w_in"])
    p.add("attend", "dilated", what=[("dil", h) for h in range(DIL_H)])
    down("od_o", w["od_w_o"], 1024)
    norm("mlp1")
    up("mlp_up", w["mlp_w1"][1], 0, FF1 // TCOLS, post="relu2", dest="h")
    down("mlp_down", w["mlp_w2"][1], FF1)
    p.add("final", "norm_final", out=False)
    norm("mem", src="mem")
    for l in range(2):
        up("mem_k", w["mem_w_kv"][l], 0, 2, post="copy", dest=f"mem_k{l}")
        natural("mem_v", w["mem_w_kv"][l], 512, 1, dest=f"mem_v{l}")
    for l in range(2):
        if l == 1:
            norm("kv")
            up("fox_k", w["w_kvf"], 0, 4, post="copy", dest="fox_k")
            natural("fox_v", w["w_kvf"], 1024, 2, dest="fox_v")
            p.add("forget", "forget", 1, 1, w=w["w_kvf"], col=2048)
        norm(f"ffn{l}0")
        p.add("glu", "glu", 2 * FF2 // TCOLS, 2 * FF2 // TCOLS, w=w["ffn_gu"][l][0])
        down("ffn_down", w["ffn_down"][l][0], FF2, scale=0.5)
        norm(f"bmix{l}")
        if l == 0:
            p.add("conv", "conv", 12, 12, w=w["a_w_in"])
            up("mem_q", w["a_w_in"], 3072, 2, post="copy", dest="mem_q")
            p.add("attend", "memory0", what=[("mem0", h) for h in range(4)])
            down("a_out", w["a_w_out"], 1536)
        else:
            up("fox_q", w["b_w_q"], 0, 4, post="copy", dest="fox_q")
            up("mem_q", w["b_w_q"], 1024, 2, post="copy", dest="mem_q")
            p.add("attend", "fox",
                  what=[("fox", h) for h in range(8)] + [("mem1", h) for h in range(4)])
            down("b_out", w["b_w_out"], 1536)
        norm(f"ffn{l}1")
        p.add("glu", "glu", 2 * FF2 // TCOLS, 2 * FF2 // TCOLS, w=w["ffn_gu"][l][1])
        down("ffn_down", w["ffn_down"][l][1], FF2, scale=0.5)
    p.add("final", "final_norm", out=True)
    return p


def build_program(nc, a, out):
    blocked = lambda m: m.rearrange("(k p) n -> p k n", p=P)
    w = {
        "ev_w_in": blocked(a["ev_w_in"][0]), "ev_w_uq": blocked(a["ev_w_uq"][0]),
        "ev_w_ukv": blocked(a["ev_w_ukv"][0]), "ev_w_o": blocked(a["ev_w_o"][0]),
        "od_w_in": blocked(a["od_w_in"][0]), "od_w_o": blocked(a["od_w_o"][0]),
        "mlp_w1": [blocked(a["mlp_w1"][l]) for l in range(2)],
        "mlp_w2": [blocked(a["mlp_w2"][l]) for l in range(2)],
        "ffn_gu": [[blocked(a["ffn_w_gate_up_2"][l, i]) for i in range(2)] for l in range(2)],
        "ffn_down": [[blocked(a["ffn_w_down_2"][l, i]) for i in range(2)] for l in range(2)],
        "mem_w_kv": [blocked(a["mem_w_kv_2"][l]) for l in range(2)],
        "a_w_in": blocked(a["a_w_in_2"][0]), "a_w_out": blocked(a["a_w_out_2"][0]),
        "w_kvf": blocked(a["w_kvf_2"]), "b_w_q": blocked(a["b_w_q_2"][0]),
        "b_w_out": blocked(a["b_w_out_2"][0]),
    }
    plan = make_plan(w)
    stages, G_TOTAL = plan.stages, plan.g

    ctx = ExitStack()
    with ctx:
        def sb(name, shape, dt=F32):
            return ctx.enter_context(nc.sbuf_tensor(name, shape, dt))

        def sem(name):
            return ctx.enter_context(nc.semaphore(name))

        W_raw = sb("W_raw", [P, 2, CH])
        W_hi = sb("W_hi", [P, 2, CH], F32R)
        W_lo = sb("W_lo", [P, 2, CH], F32R)
        XN = sb("XN", [P, KD, 2, S], F32R)
        SX = sb("SX", [P, 2, 2, 2 * S], F32R)
        X = sb("X", [P, TT, D])
        K = sb("K", [P, NCONST])
        G = sb("G", [P, NGAIN])
        GF = sb("GF", [P, D])
        T = sb("T", [P, 2048])
        T0 = T[:, 0:1024].rearrange("p (u n) -> p u n", u=2)
        T1, T2 = T[:, 1024:1536], T[:, 1536:2048]
        T3 = sb("T3", [P, 512])
        ST = sb("ST", [P, 64])
        U = sb("U", [P, 25088])
        PS = ctx.enter_context(nc.psum_tensor("PS", [P, 8, 512], F32))

        const = lambda name: K[:, CONST[name][0]:CONST[name][1]]
        ident = const("ident")

        def region(at, n):
            return U[:, at:at + n]

        H0 = 0
        XS = region(0, 2 * D).rearrange("p (t n) -> p t n", t=TT)
        R = dict(na_qk=2048, na_v=4096, mla_qn=5120, mla_kn=6656, latent=8192, lat_s=9024,
                 c=9792, mla_v=10560, mla_qT=11584, mla_kT=13632, na_bias=15680,
                 sm=18752, pt=21824)
        DIL0, DIL_SIZE = 2048, 6144
        RD = dict(sm=DIL0 + DIL_G * DIL_SIZE, pt=DIL0 + DIL_G * DIL_SIZE + 3072)
        rope_m1 = region(RD["sm"], 1024)
        rope_m2 = region(RD["sm"] + 1024, 1024)
        rope_out = region(RD["sm"] + 2048, 2048).rearrange("p (b n) -> p b n", b=2)
        RB = dict(mem=18944, mem_k0=7680, mem_k1=8704, mem_v0=9728, mem_v1=10752, fox_k=11776,
                  fox_v=13824, fox_q=15872, mem_q=17920, ck=18944, sm=20992, pt=24064)
        MEM = region(RB["mem"], 2 * D).rearrange("p (t n) -> p t n", t=TT)
        conv_b = region(RB["fox_v"], 1024).rearrange("p (c n) -> p c n", c=2)
        conv_cu = region(RB["fox_v"] + 1024, 2 * (S + 2)).rearrange("p (f t) -> p f t", f=2)
        conv_acc = region(RB["fox_v"] + 1664, 512).rearrange("p (f t) -> p f t", f=2)
        conv_tap = region(RB["fox_v"] + 2176, 512).rearrange("p (f t) -> p f t", f=2)
        dest_at = dict(R, **{k: RB[k] for k in RB if k not in ("sm", "pt")}, h=H0)
        v_layout = lambda at, blk: region(at + blk * 1024, 1024)

        first_in = sem("first_in")
        consts_in = sem("consts_in")
        gain_in = sem("gain_in")
        x_in, mem_in = sem("x_in"), sem("mem_in")
        raw_full = [sem("raw_full0"), sem("raw_full1")]
        w_hi = sem("w_hi")
        w_lo = sem("w_lo")
        chunk_done = sem("chunk_done")
        tile_done = sem("tile_done")
        acc_read = sem("acc_read")
        cross_out = sem("cross_out")
        h_done = sem("h_done")
        st_hi, st_lo = sem("st_hi"), sem("st_lo")
        x_new = sem("x_new")
        n_sq = sem("n_sq")
        n_rstd = sem("n_rstd")
        n_scaled = sem("n_scaled")
        n_tr = sem("n_tr")
        n_hi = sem("n_hi")
        n_lo = sem("n_lo")
        silu_out = sem("silu_out")
        rope_in, rope_sum = sem("rope_in"), sem("rope_sum")
        rope_tr, rope_kept = sem("rope_tr"), sem("rope_kept")
        mla_a, mla_p, mla_t, mla_r = sem("mla_a"), sem("mla_p"), sem("mla_t"), sem("mla_r")
        f_v, f_a, f_t = sem("f_v"), sem("f_a"), sem("f_t")
        s_score, s_soft, s_exp, s_norm = sem("s_score"), sem("s_soft"), sem("s_exp"), sem("s_norm")
        s_read = sem("s_read")
        s_pt, s_pte, s_pv = sem("s_pt"), sem("s_pte"), sem("s_pv")
        conv_cu_done = sem("conv_cu_done")
        conv_done = sem("conv_done")
        bias_in, bias_ready = sem("bias_in"), sem("bias_ready")
        dve_chain, act_chain, pool_chain = sem("dve_chain"), sem("act_chain"), sem("pool_chain")
        out_done = sem("out_done")

        def head(what, h):
            if what == "na":
                pb = 64 * (h % 2)
                q = region(R["na_qk"] + (h // 2) * S, S)[pb:pb + 64, :]
                k = region(R["na_qk"] + (4 + h // 2) * S, S)[pb:pb + 64, :]
                v = lambda g, kt: region(R["na_v"] + kt * 512 + h * 64, 64)
                y = region(H0 + (h // 2) * S, S)[pb:pb + 64, :]
                return dict(G=1, q=[q], k=[k], v=v, y=y, pb=pb, scale=64 ** -0.5, bias="na", R=R, h=h)
            if what == "mla":
                pb = 64 * (h % 2)
                q = region(R["mla_qT"] + h * S, S)[0:96, :]
                k = region(R["mla_kT"] + h * S, S)[0:96, :]
                v = lambda g, kt: region(R["mla_v"] + kt * 512 + h * 64, 64)
                y = region(H0 + (4 + h // 2) * S, S)[pb:pb + 64, :]
                return dict(G=1, q=[q], k=[k], v=v, y=y, pb=pb, scale=96 ** -0.5, bias=None, R=R, h=h)
            if what == "dil":
                pb, blk, pair = 64 * (h % 2), h // 8, h // 2
                q = [region(DIL0 + g * DIL_SIZE + pair * S, S)[pb:pb + 64, :] for g in range(3)]
                k = [region(DIL0 + g * DIL_SIZE + 2048 + pair * S, S)[pb:pb + 64, :] for g in range(3)]
                v = lambda g, kt: region(DIL0 + g * DIL_SIZE + 4096 + blk * 1024 + kt * 512
                                         + (h % 8) * 64, 64)
                y = region(H0 + pair * S, S)[pb:pb + 64, :]
                return dict(G=3, q=q, k=k, v=v, y=y, pb=pb, scale=64 ** -0.5, bias="dil", R=RD, h=h)
            if what == "fox":
                q = region(RB["fox_q"] + h * S, S)
                k = region(RB["fox_k"] + h * S, S)
                v = lambda g, kt: region(RB["fox_v"] + (h // 4) * 1024 + kt * 512 + (h % 4) * P, P)
                y = region(H0 + h * S, S)
                return dict(G=1, q=[q], k=[k], v=v, y=y, pb=0, scale=P ** -0.5, bias="fox", R=RB, h=h)
            l = int(what[3])
            q = region(RB["mem_q"] + h * S, S)
            k = region(RB[f"mem_k{l}"] + h * S, S)
            v = lambda g, kt: region(RB[f"mem_v{l}"] + kt * 512 + h * P, P)
            y = region(H0 + (8 + h) * S, S)
            return dict(G=1, q=[q], k=[k], v=v, y=y, pb=0, scale=P ** -0.5, bias=None, R=RB, h=h)

        heads, n_groups = [], 0
        h_count = 0
        n_norm = n_final = 0
        for st in stages:
            st["h0"] = h_count
            if st["kind"] == "attend":
                st["a0"] = len(heads)
                for what, h in st["what"]:
                    e = head(what, h)
                    e["group0"] = n_groups
                    n_groups += e["G"]
                    heads.append(e)
                h_count += len(st["what"])
            elif st["kind"] == "up" and st["dest"] == "h":
                h_count += st["n"]
            elif st["kind"] == "glu":
                h_count += st["n"] // 2
            elif st["kind"] == "mla_in":
                h_count += 3
            elif st["kind"] == "norm":
                st["i"] = n_norm
                n_norm += 1
            elif st["kind"] == "final":
                st["i"] = n_norm
                st["f"] = n_final
                n_norm += 1
                n_final += 1
        x_count = 0
        for st in stages:
            st["x0"] = x_count
            if st["kind"] in ("down", "final"):
                x_count += 2
        last_score, last_pt = {}, {}
        n_read = 0
        for n, e in enumerate(heads):
            e["score_banks"] = (0, 1, 2) if e["G"] == 3 else (n % 3,)
            e["score_prev"] = [last_score[b] for b in e["score_banks"] if b in last_score]
            for b in e["score_banks"]:
                last_score[b] = n
            e["pt_banks"] = [3 + g for g in range(3)] if e["G"] == 3 else [3 + n % 2]
            e["pt_prev"] = []
            for g, b in enumerate(e["pt_banks"]):
                e["pt_prev"].append(last_pt.get(b))
                last_pt[b] = e["group0"] + g + 1
            e["scores"] = (PS[:, 0:3, :].rearrange("p b n -> p (b n)") if e["G"] == 3
                           else PS[:, n % 3, :])
            width = e["G"] * S * TT
            e["probs"] = (region(e["R"]["sm"] + (n % 3) * width, width) if n % 3 < 2
                          else T[:, 0:width])
            e["read"] = n_read
            n_read += bool(e["bias"])
            e["ptile"] = [region(e["R"]["pt"] + g * 512 if e["G"] == 3
                                 else e["R"]["pt"] + (n % 2) * 512, 512) for g in range(e["G"])]
            e["mx"] = ST[:, 8 + 8 * (n % 3):10 + 8 * (n % 3)]
            e["z"] = ST[:, 10 + 8 * (n % 3):12 + 8 * (n % 3)]
            e["rz"] = ST[:, 12 + 8 * (n % 3):14 + 8 * (n % 3)]


        k_norm = n_glu = n_staged = n_cross = 0
        for n, st in enumerate(stages):
            if st["kind"] == "norm":
                st["k"] = k_norm
                k_norm += 1
            st["cross0"] = n_cross
            if st["kind"] in ("up", "glu", "conv"):
                n_cross += st["n"]
            if st["kind"] == "glu":
                st["silu0"] = n_glu
                n_glu += st["n"] // 2
            if st["kind"] == "down":
                st["staged0"] = n_staged
                n_staged += st["n"]
                before = stages[n - 1]
                st["each"] = before["kind"] == "glu" or before.get("dest") == "h"
        i_norm = lambda st: st["i"]
        cross0 = lambda st: st["cross0"]
        silu0 = lambda st: st["silu0"]
        u_of = lambda st: st["u"]
        staged0 = lambda st: st["staged0"]
        n_made = lambda st: st["n"]

        def e_out_done(n):
            for st in stages:
                if st["kind"] == "attend" and st["a0"] <= n < st["a0"] + len(st["what"]):
                    return st["h0"] + n - st["a0"] + 1

        def raw_count(g, slot):
            if isinstance(g, int):
                return 16 * (g // 2 + 1)
            return g * 8 + (16 if slot == 0 else 8)

        def down_src(st, j):
            if st["src"] == "c":
                at = R["c"] + (0 if st["name"] == "uq" else 2 * S)
                return region(at, st["ks"] * S)
            return U[:, bass.ds(H0 + j * 2 * S, 2 * S)]

        def operands_ready(eng, st):
            eng.wait_ge(acc_read, st["u"])
            if st["name"] == "even":
                eng.wait_ge(mla_a, 2)
                eng.wait_ge(mla_p, 3)
            if st["name"] == "dilated":
                eng.wait_ge(rope_kept, 4 * DIL_G)
            if st["name"] == "fox":
                eng.wait_ge(dve_chain, 1)

        halves = lambda slot, h: slice(h * (CH // 2), (h + 1) * (CH // 2))
        block = ctx.enter_context(nc.Block())

        @block.sync
        def _(sp):
            sp.dma_start(X[:], a["x"][0].rearrange("(t p) n -> p t n", p=P)).then_inc(x_in, 16)

            def load(g, slot, src, ks, n):
                if not isinstance(g, int) or g >= 2:
                    sp.wait_ge(w_lo, 2 * (g - 1))
                dst = W_raw[:, slot, 0:ks * n].rearrange("p (k n) -> p k n", k=ks)
                sp.dma_start(dst, src).then_inc(raw_full[slot], 16)

            for st in stages:
                g0, n, kind = st["g"], st["n"], st["kind"]
                w_ = st.get("w")
                slots = (g0 % 2, (g0 + 1) % 2)
                if kind == "up":
                    def body(i):
                        for s in range(2):
                            load(g0 + 2 * i + s, slots[s],
                                 w_[:, :, bass.ds(st["col"] + (2 * i + s) * TCOLS, TCOLS)], KD, TCOLS)
                    repeat(sp, n // 2, body, straight=g0 == 0)
                elif kind == "glu":
                    def body(i):
                        for s in range(2):
                            load(g0 + 2 * i + s, slots[s],
                                 w_[:, :, bass.ds(s * FF2 + i * TCOLS, TCOLS)], KD, TCOLS)
                    repeat(sp, n // 2, body)
                elif kind == "natural":
                    for b in range(st["blocks"]):
                        for c in range(2):
                            col = st["col"] + b * 512
                            load(g0 + 2 * b + c, slots[c],
                                 w_[:, 4 * c:4 * c + 4, col:col + st["ncols"]], 4, st["ncols"])
                elif kind == "dilated_in":
                    def body(i):
                        for c in range(2):
                            load(g0 + 2 * i + c, slots[c],
                                 w_[:, 4 * c:4 * c + 4, bass.ds(i * 512, 512)], 4, 512)
                    repeat(sp, n // 2, body)
                elif kind == "conv":
                    for c in range(4):
                        for part in range(3):
                            col = part * D + c * TCOLS
                            load(g0 + 3 * c + part, (g0 + 3 * c + part) % 2,
                                 w_[:, :, col:col + TCOLS], KD, TCOLS)
                elif kind == "forget":
                    load(g0, slots[0], w_[:, :, st["col"]:st["col"] + 8], KD, 8)
                elif kind == "down":
                    ks = st["ks"]

                    def body(i):
                        for s in range(2):
                            load(g0 + 2 * i + s, slots[s],
                                 w_[:, bass.ds((2 * i + s) * ks, ks), :], ks, st["ncols"])
                    repeat(sp, n // 2, body)
                    if n % 2:
                        load(g0 + n - 1, (g0 + n - 1) % 2, w_[:, (n - 1) * ks:n * ks, :], ks,
                             st["ncols"])
            sp.wait_ge(x_new, x_count)
            sp.dma_start(out[0].rearrange("(t p) n -> p t n", p=P), X[:]).then_inc(out_done, 16)
            sp.wait_ge(out_done, 16)

        @block.tensor
        def _(pe):
            mm, tr = nc.tensor.matmul, nc.tensor.transpose

            def chunk_ready(g):
                pe.wait_ge(w_lo, 2 * g + 2)

            def acc_free(u):
                if not isinstance(u, int) or u >= 2:
                    pe.wait_ge(acc_read, u - 1)

            def wT(tile, slot, k, fb):
                return tile[:, slot, k * TCOLS + fb * P:k * TCOLS + (fb + 1) * P]

            def up_chunk(g, u, slot, pair):
                chunk_ready(g)
                acc_free(u)
                for fb in range(2):
                    bank = PS[:, 2 * pair + fb, :]
                    for k in range(KD):
                        if fb == 0 and slot == slots[0] and k % 2 == 0:
                            pe.wait_ge(n_lo, xn_ready + k // 2 + 1)
                        both = XN[:, k, :, :].rearrange("p a t -> p (a t)")
                        if k == 0:
                            mm(bank, wT(W_hi, slot, k, fb), both, start=True, stop=False)
                            mm(bank[:, S:], wT(W_lo, slot, k, fb), XN[:, k, 0, :],
                               start=False, stop=False)
                        else:
                            mm(bank[:, S:], wT(W_lo, slot, k, fb), XN[:, k, 0, :],
                               start=False, stop=False)
                            last = mm(bank, wT(W_hi, slot, k, fb), both, start=False,
                                      stop=k == KD - 1)
                last.then_inc(chunk_done, 1)

            def three(bank, xh, xl, wh, wl, start, stop):
                mm(bank, xh, wh, start=start, stop=False)
                mm(bank, xh, wl, start=False, stop=False)
                return mm(bank, xl, wh, start=False, stop=stop)

            def natural_chunk(g, slot, pair, c, ncols):
                chunk_ready(g)
                for t in range(TT):
                    for ks in range(4):
                        k, n = 4 * c + ks, slice(ks * ncols, (ks + 1) * ncols)
                        if t == 0 and k % 2 == 0:
                            pe.wait_ge(n_lo, xn_ready + k // 2 + 1)
                        last = three(PS[:, 2 * pair + t, 0:ncols],
                                     XN[:, k, 0, t * P:(t + 1) * P], XN[:, k, 1, t * P:(t + 1) * P],
                                     W_hi[:, slot, n], W_lo[:, slot, n], k == 0, k == KD - 1)
                last.then_inc(chunk_done, 1)

            def down_chunk(st, g, staged, slot, first, final):
                chunk_ready(g)
                pe.wait_ge(st_lo, staged)
                ncols, ks_n = st["ncols"], st["ks"]
                for t in range(TT):
                    for ks in range(ks_n):
                        x = slice(ks * S + t * P, ks * S + (t + 1) * P)
                        for b in range(2):
                            lo, hi = b * 512, min(ncols, b * 512 + 512)
                            n = slice(ks * ncols + lo, ks * ncols + hi)
                            last = three(PS[:, 4 + 2 * t + b, 0:hi - lo],
                                         SX[:, slot, 0, x], SX[:, slot, 1, x],
                                         W_hi[:, slot, n], W_lo[:, slot, n],
                                         first and ks == 0, final and ks == ks_n - 1)
                    if final and t == 0:
                        last.then_inc(tile_done, 1)
                last.then_inc(chunk_done, 1)

            staged = 0
            pe.wait_ge(first_in, 32)
            for st in stages:
                g0, u0, n, kind = st["g"], st["u"], st["n"], st["kind"]
                slots, pairs = (g0 % 2, (g0 + 1) % 2), (u0 % 2, (u0 + 1) % 2)
                if kind == "forget":
                    pe.wait_ge(consts_in, 16)
                if kind == "norm":
                    i = st["i"]
                    pe.wait_ge(n_scaled, 2 * i_norm(st) + 2)
                    for b in range(4):
                        for k in (2 * b, 2 * b + 1):
                            for t in range(TT):
                                at = (k % 2) * S + t * P
                                last = tr(PS[:, 4 + b, at:at + P], XS[:, t, k * P:(k + 1) * P], ident)
                        last.then_inc(n_tr, 1)
                    xn_ready = 4 * st["k"]
                elif kind in ("up", "glu"):
                    def body(i):
                        for s in range(2):
                            up_chunk(g0 + 2 * i + s, u0 + 2 * i + s, slots[s], pairs[s])
                    repeat(pe, n // 2, body, straight=g0 == 0)
                elif kind == "conv":
                    for c in range(n):
                        up_chunk(g0 + c, u0 + c, (g0 + c) % 2, (u0 + c) % 2)
                elif kind == "natural":
                    for b in range(st["blocks"]):
                        acc_free(u0 + b)
                        for c in range(2):
                            natural_chunk(g0 + 2 * b + c, slots[c], (u0 + b) % 2, c, st["ncols"])
                elif kind == "dilated_in":
                    def turn(i, b, q):
                        pe.wait_ge(rope_sum, 4 * i + b + 1)
                        if q >= 2:
                            pe.wait_ge(rope_kept, 4 * i + b - 1)
                        elif not isinstance(i, int):
                            pass
                        for pr in range(4):
                            for t in range(TT):
                                last = tr(PS[:, 4 + 2 * (b % 2) + pr // 2,
                                             (pr % 2) * S + t * P:(pr % 2) * S + (t + 1) * P],
                                          rope_out[:, b % 2, t * 512 + pr * P:t * 512 + (pr + 1) * P],
                                          ident)
                        last.then_inc(rope_tr, 1)

                    def body(i):
                        for b in range(6):
                            acc_free(u0 + 6 * i + b)
                            for c in range(2):
                                natural_chunk(g0 + 12 * i + 2 * b + c, slots[c], (u0 + b) % 2, c, 512)
                            if 1 <= b <= 4:
                                turn(i, b - 1, b - 1)
                    repeat(pe, DIL_G, body)
                elif kind == "forget":
                    chunk_ready(g0)
                    acc_free(u0)
                    for t in range(TT):
                        for k in range(KD):
                            f = slice(k * 8, k * 8 + 8)
                            last = three(PS[:, 2 * pairs[0] + t, 0:8], XN[:, k, 0, t * P:(t + 1) * P],
                                         XN[:, k, 1, t * P:(t + 1) * P], W_hi[:, slots[0], f],
                                         W_lo[:, slots[0], f], k == 0, k == KD - 1)
                    last.then_inc(chunk_done, 1)
                    pe.wait_ge(f_v, 2)
                    tri, ls = const("tri"), T1[:, 80:96]
                    for q in range(TT):
                        for t in range(TT):
                            mm(PS[:, 0, q * 8:q * 8 + 8], tri[:, t * S + q * P:t * S + (q + 1) * P],
                               ls[:, t * 8:t * 8 + 8], start=t == 0, stop=t == TT - 1)
                    for h in range(8):
                        for t in range(TT):
                            last = mm(PS[:, 4 + h // 2, (h % 2) * S:(h % 2 + 1) * S],
                                      ls[:, t * 8 + h:t * 8 + h + 1].to_broadcast([P, P]),
                                      tri[:, t * S:(t + 1) * S], start=t == 0, stop=t == TT - 1)
                    last.then_inc(f_t, 1)
                elif kind == "down":
                    for j in (0,) if n > 1 else ():
                        down_chunk(st, g0, staged + 1, g0 % 2, True, False)
                    if n == 1:
                        if st["name"] == "ukv":
                            pe.wait_ge(x_new, st["x0"])
                        down_chunk(st, g0, staged + 1, g0 % 2, True, True)
                    mid = max(n - 2, 0)

                    def body(i):
                        for s in range(2):
                            down_chunk(st, g0 + 1 + 2 * i + s, staged + 2 + 2 * i + s,
                                       (g0 + 1 + s) % 2, False, False)
                    repeat(pe, mid // 2, body)
                    for j in range(1 + mid // 2 * 2, n):
                        down_chunk(st, g0 + j, staged + j + 1, (g0 + j) % 2, False, j == n - 1)
                    staged += n
                elif kind == "mla_in":
                    pe.wait_ge(acc_read, u0)
                    pe.wait_ge(mla_p, 1)
                    lat = region(R["lat_s"], 768)
                    for b in range(3):
                        for t in range(TT):
                            last = tr(PS[:, b // 2, (b % 2) * S + t * P:(b % 2) * S + (t + 1) * P],
                                      lat[:, t * 384 + b * P:t * 384 + (b + 1) * P], ident)
                    last.then_inc(mla_t, 1)
                elif kind == "mla_qk":
                    pe.wait_ge(mla_p, 2)
                    for src, bank in ((R["mla_qn"], 4), (R["mla_kn"], 0)):
                        for h in range(8):
                            for t in range(TT):
                                at = (h % 2) * S + t * P
                                last = tr(PS[0:96, bank + h // 2, at:at + P],
                                          region(src + t * 768 + h * 96, 96), ident)
                        last.then_inc(mla_t, 1)
                elif kind == "attend":
                    a0, m = st["a0"], len(st["what"])

                    def scores(n):
                        e = heads[n]
                        if n == a0:
                            operands_ready(pe, st)
                        for prev in e["score_prev"]:
                            if heads[prev]["bias"]:
                                pe.wait_ge(s_read, heads[prev]["read"] + 1)
                            else:
                                pe.wait_ge(s_exp, 2 * prev + 2)
                        for t in range(TT):
                            for g in range(e["G"]):
                                at = (t * e["G"] + g) * S
                                last = mm(e["scores"][:, at:at + S], e["q"][g][:, t * P:(t + 1) * P],
                                          e["k"][g], start=True, stop=True)
                        last.then_inc(s_score, 1)

                    def transposes(n):
                        e = heads[n]
                        pe.wait_ge(s_norm, n + 1)
                        for g in range(e["G"]):
                            if e["pt_prev"][g]:
                                pe.wait_ge(s_pte, e["pt_prev"][g])
                            for kt in range(TT):
                                for t in range(TT):
                                    at = (t * e["G"] + g) * S + kt * P
                                    last = tr(PS[:, e["pt_banks"][g],
                                                 kt * S + t * P:kt * S + (t + 1) * P],
                                              e["probs"][:, at:at + P], ident)
                            last.then_inc(s_pt, 1)

                    def values(n):
                        e = heads[n]
                        if n >= 2:
                            pe.wait_ge(h_done, e_out_done(n - 2))
                        d = 64 if e["pb"] or e["bias"] in ("na", "dil") or e["scale"] == 96 ** -0.5 else P
                        o = PS[e["pb"]:e["pb"] + d, 6 + n % 2, 0:S]
                        for g in range(e["G"]):
                            pe.wait_ge(s_pte, e["group0"] + g + 1)
                            for kt in range(TT):
                                last = mm(o, e["v"](g, kt), e["ptile"][g][:, kt * S:(kt + 1) * S],
                                          start=g == 0 and kt == 0,
                                          stop=g == e["G"] - 1 and kt == TT - 1)
                        last.then_inc(s_pv, 1)

                    for n_ in range(3):
                        scores(a0 + n_)
                    for n_ in range(a0, a0 + m):
                        transposes(n_)
                        if n_ + 3 < a0 + m:
                            scores(n_ + 3)
                        values(n_)

        @block.scalar
        def _(act):
            A = nc.scalar.activation

            def split_hi(g, slot):
                if not isinstance(g, int) or g >= 2:
                    act.wait_ge(chunk_done, g - 1)
                act.wait_ge(raw_full[slot], raw_count(g, slot))
                for h in range(2):
                    A(W_hi[:, slot, halves(slot, h)], W_raw[:, slot, halves(slot, h)],
                      ACT.Copy).then_inc(w_hi, 1)

            def ahead(g, slot):
                if not isinstance(g, int) or g + 1 < G_TOTAL:
                    split_hi(g + 1, 1 - slot)

            def cross(g, u, pair):
                act.wait_ge(chunk_done, g + 1)
                if not isinstance(u, int) or u >= 2:
                    act.wait_ge(acc_read, u - 1)
                A(T0[:, pair, :].rearrange("p (f t) -> p f t", f=2),
                  PS[:, 2 * pair:2 * pair + 2, S:2 * S], ACT.Copy).then_inc(cross_out, 1)

            def stage_hi(st, j, g, slot):
                if st["src"] == "c":
                    act.wait_ge(h_done, st["h0"])
                elif st["each"]:
                    act.wait_ge(h_done, st["h0"] - n_made(st) + j + 1)
                else:
                    act.wait_ge(h_done, st["h0"])
                    if st["name"] == "a_out":
                        act.wait_ge(conv_done, 4)
                act.wait_ge(chunk_done, g - 1)
                A(SX[:, slot, 0, 0:st["ks"] * S], down_src(st, j), ACT.Copy).then_inc(st_hi, 1)

            act.dma_start(K[:, 0:P], a["const"][:, 0:P]).then_inc(first_in, 16)
            act.dma_start(G[:], a["gains"]).then_inc(first_in, 16)
            split_hi(0, 0)
            act.wait_ge(first_in, 32)
            for st in stages:
                g0, u0, n, kind = st["g"], st["u"], st["n"], st["kind"]
                slots, pairs = (g0 % 2, (g0 + 1) % 2), (u0 % 2, (u0 + 1) % 2)
                if kind in ("norm", "final"):
                    i = i_norm(st)
                    src = MEM if st.get("src") == "mem" else X
                    if st.get("src") == "mem":
                        act.wait_ge(mem_in, 16)
                        act.wait_ge(x_new, st["x0"])
                    elif st["x0"] == 0:
                        act.wait_ge(x_in, 16)
                    for t in range(TT):
                        if st.get("src") != "mem" and st["x0"]:
                            act.wait_ge(x_new, st["x0"] - 1 + t)
                        if i:
                            act.wait_ge(n_scaled, 2 * i)
                        A(XS[:, t, :], src[:, t, :], ACT.Square,
                          accum_out=ST[:, t:t + 1]).then_inc(n_sq, 1)
                    if kind == "norm":
                        for b in range(4):
                            act.wait_ge(n_tr, 4 * st["k"] + b + 1)
                            if b == 0:
                                act.wait_ge(chunk_done, g0) if g0 else None
                            for k in (2 * b, 2 * b + 1):
                                last = A(XN[:, k, 0, :], PS[:, 4 + b, (k % 2) * S:(k % 2 + 1) * S],
                                         ACT.Copy, scale=G[:, st["gain"] + k:st["gain"] + k + 1])
                            last.then_inc(n_hi, 1)
                elif kind in ("up", "conv", "natural"):
                    def body(i):
                        for s in range(2):
                            ahead(g0 + 2 * i + s, slots[s])
                            if kind != "natural":
                                cross(g0 + 2 * i + s, u0 + 2 * i + s, pairs[s])
                    repeat(act, n // 2, body, straight=g0 == 0)
                elif kind == "glu":
                    def body(i):
                        for s in range(2):
                            ahead(g0 + 2 * i + s, slots[s])
                            if s == 1:
                                act.wait_ge(acc_read, u_of(st) + 2 * i + 1)
                                act.wait_ge(h_done, st["h0"] + i)
                                A(T3[:], T1, ACT.Silu).then_inc(silu_out, 1)
                            cross(g0 + 2 * i + s, u0 + 2 * i + s, pairs[s])
                    A(ST[:, 60:61], G[:, 0:1], ACT.Silu)
                    repeat(act, n // 2, body)
                elif kind == "dilated_in":
                    def keep(i, b):
                        act.wait_ge(rope_tr, 4 * i + b + 1)
                        at = i * DIL_SIZE + (DIL0 + (b // 2) * 2048 + (b % 2) * 1024)
                        A(U[:, bass.ds(at, 1024)],
                          PS[:, 4 + 2 * (b % 2):6 + 2 * (b % 2), :].rearrange("p b n -> p (b n)"),
                          ACT.Copy).then_inc(rope_kept, 1)

                    def body(i):
                        for b in range(6):
                            for c in range(2):
                                ahead(g0 + 12 * i + 2 * b + c, slots[c])
                            if b >= 2:
                                keep(i, b - 2)
                    repeat(act, DIL_G, body)
                elif kind == "down":
                    def body(i):
                        for s in range(2):
                            stage_hi(st, 2 * i + s, g0 + 2 * i + s, slots[s])
                            ahead(g0 + 2 * i + s, slots[s])
                    repeat(act, n // 2, body)
                    if n % 2:
                        stage_hi(st, n - 1, g0 + n - 1, (g0 + n - 1) % 2)
                        ahead(g0 + n - 1, (g0 + n - 1) % 2)
                elif kind == "forget":
                    ahead(g0, slots[0])
                    act.wait_ge(f_v, 1)
                    A(T1[:, 32:48], T1[:, 16:32], ACT.Exp, scale=-1.0).then_inc(f_a, 1)
                    act.wait_ge(f_a, 1)
                    A(T1[:, 48:64], T1[:, 32:48], ACT.Ln, bias=1.0).then_inc(f_a, 1)
                elif kind == "mla_in":
                    act.wait_ge(acc_read, u_of(st))
                    lat = region(R["latent"], 832)
                    for t in range(TT):
                        A(T1[:, t * 256:(t + 1) * 256], lat[:, t * 416:t * 416 + 256], ACT.Square,
                          accum_out=ST[:, 4 + t:5 + t])
                        last = A(T2[:, t * 256:t * 256 + P], lat[:, t * 416 + 256:t * 416 + 384],
                                 ACT.Square, accum_out=ST[:, 6 + t:7 + t])
                    last.then_inc(mla_a, 1)
                elif kind == "mla_qk":
                    act.wait_ge(mla_t, 2)
                    A(region(R["mla_qT"], 2048)[0:96, :],
                      PS[0:96, 4:8, :].rearrange("p b n -> p (b n)"), ACT.Copy).then_inc(mla_a, 1)
                elif kind == "attend":
                    a0, m = st["a0"], len(st["what"])

                    def exps(n):
                        e = heads[n]
                        act.wait_ge(s_soft, n + 1)
                        w_ = e["G"] * S
                        for t in range(TT):
                            src = e["probs"] if e["bias"] else e["scores"]
                            A(e["probs"][:, t * w_:(t + 1) * w_], src[:, t * w_:(t + 1) * w_], ACT.Exp,
                              bias=e["mx"][:, t:t + 1], scale=1.0 if e["bias"] else e["scale"],
                              accum_out=e["z"][:, t:t + 1]).then_inc(s_exp, 1)

                    def keep_pt(n):
                        e = heads[n]
                        for g in range(e["G"]):
                            act.wait_ge(s_pt, e["group0"] + g + 1)
                            if n:
                                act.wait_ge(s_pv, n - 1 if e["G"] == 1 and n > 1 else n)
                            A(e["ptile"][g], PS[:, e["pt_banks"][g], :], ACT.Copy).then_inc(s_pte, 1)

                    exps(a0)
                    exps(a0 + 1)
                    for n_ in range(a0, a0 + m):
                        keep_pt(n_)
                        if n_ + 2 < a0 + m:
                            exps(n_ + 2)

        @block.vector
        def _(dve):
            V = nc.vector
            chain = Count(dve_chain)

            def link(ins):
                chain.inc(ins)
                dve.wait_ge(dve_chain, chain.value())

            def split_lo(g, slot):
                for h in range(2):
                    dve.wait_ge(w_hi, 2 * g + h + 1)
                    V.tensor_tensor(W_lo[:, slot, halves(slot, h)], W_raw[:, slot, halves(slot, h)],
                                    W_hi[:, slot, halves(slot, h)], ALU.subtract).then_inc(w_lo, 1)

            def ahead(g, slot):
                if not isinstance(g, int) or g + 1 < G_TOTAL:
                    split_lo(g + 1, 1 - slot)

            def add_halves(st, dst, u, pair):
                dve.wait_ge(cross_out, u - u_of(st) + cross0(st) + 1)
                return V.tensor_tensor(dst.rearrange("p (f t) -> p f t", f=2),
                                       PS[:, 2 * pair:2 * pair + 2, 0:S],
                                       T0[:, pair, :].rearrange("p (f t) -> p f t", f=2), ALU.add)

            split_lo(0, 0)
            dve.wait_ge(first_in, 32)
            silu_n = 0
            for st in stages:
                g0, u0, n, kind = st["g"], st["u"], st["n"], st["kind"]
                slots, pairs = (g0 % 2, (g0 + 1) % 2), (u0 % 2, (u0 + 1) % 2)
                if kind in ("norm", "final"):
                    i = i_norm(st)
                    src = MEM if st.get("src") == "mem" else X
                    if kind == "final":
                        dve.wait_ge(gain_in, 16 * (st["f"] + 1))
                    for t in range(TT):
                        dve.wait_ge(n_rstd, 2 * i + t + 1)
                        if kind == "final":
                            V.tensor_scalar(XS[:, t, :], X[:, t, :], ST[:, t:t + 1], None,
                                            ALU.mult).then_inc(n_scaled, 1)
                            dve.wait_ge(n_scaled, 2 * i + t + 1)
                            V.tensor_tensor(X[:, t, :], XS[:, t, :], GF[:], ALU.mult).then_inc(x_new, 1)
                        else:
                            V.tensor_scalar(XS[:, t, :], src[:, t, :], ST[:, t:t + 1], None,
                                            ALU.mult).then_inc(n_scaled, 1)
                    if kind == "norm":
                        for b in range(4):
                            dve.wait_ge(n_hi, 4 * st["k"] + b + 1)
                            for k in (2 * b, 2 * b + 1):
                                last = V.scalar_tensor_tensor(
                                    XN[:, k, 1, :], PS[:, 4 + b, (k % 2) * S:(k % 2 + 1) * S],
                                    G[:, st["gain"] + k:st["gain"] + k + 1], XN[:, k, 0, :],
                                    ALU.mult, ALU.subtract)
                            last.then_inc(n_lo, 1)
                elif kind == "up":
                    at = dest_at[st["dest"]]

                    def body(i):
                        for s in range(2):
                            g, c = g0 + 2 * i + s, 2 * i + s
                            ahead(g, slots[s])
                            dve.wait_ge(chunk_done, g + 1)
                            dst = U[:, bass.ds(at + c * 512, 512)]
                            if st["post"] == "copy":
                                add_halves(st, dst, u0 + c, pairs[s]).then_inc(acc_read, 1)
                            else:
                                dve.wait_ge(h_done, st["h0"] + c)
                                add_halves(st, T1, u0 + c, pairs[s]).then_inc(acc_read, 1)
                                dve.wait_ge(acc_read, u0 + c + 1)
                                V.scalar_tensor_tensor(dst, T1, 0.0, T1, ALU.max,
                                                       ALU.mult).then_inc(h_done, 1)
                    repeat(dve, n // 2, body, straight=g0 == 0)
                elif kind == "glu":
                    def body(i):
                        ahead(g0 + 2 * i, slots[0])
                        dve.wait_ge(chunk_done, g0 + 2 * i + 1)
                        dve.wait_ge(h_done, st["h0"] + i)
                        add_halves(st, T1, u0 + 2 * i, pairs[0]).then_inc(acc_read, 1)
                        ahead(g0 + 2 * i + 1, slots[1])
                        dve.wait_ge(chunk_done, g0 + 2 * i + 2)
                        add_halves(st, T2, u0 + 2 * i + 1, pairs[1]).then_inc(acc_read, 1)
                        dve.wait_ge(acc_read, u0 + 2 * i + 2)
                        dve.wait_ge(silu_out, silu0(st) + i + 1)
                        V.tensor_tensor(U[:, bass.ds(H0 + i * 512, 512)], T3[:], T2,
                                        ALU.mult).then_inc(h_done, 1)
                    repeat(dve, n // 2, body)
                elif kind == "natural":
                    ncols = st["ncols"]
                    for b in range(st["blocks"]):
                        for c in range(2):
                            ahead(g0 + 2 * b + c, slots[c])
                        dve.wait_ge(chunk_done, g0 + 2 * b + 2)
                        p = (u0 + b) % 2
                        at = dest_at[st["dest"]] + b * 1024
                        V.tensor_copy(region(at, 2 * ncols).rearrange("p (t n) -> p t n", t=2),
                                      PS[:, 2 * p:2 * p + 2, 0:ncols]).then_inc(acc_read, 1)
                elif kind == "dilated_in":
                    cosd, sind = const("cosd"), const("sind")

                    def wide(table, t, lo, hi):
                        return table[:, t * 64 + lo:t * 64 + hi].unsqueeze(1).to_broadcast([P, 8, hi - lo])

                    def body(i):
                        for b in range(6):
                            for c in range(2):
                                ahead(g0 + 12 * i + 2 * b + c, slots[c])
                            dve.wait_ge(chunk_done, g0 + 12 * i + 2 * b + 2)
                            p = (u0 + b) % 2
                            if b >= 4:
                                at = i * DIL_SIZE + (DIL0 + 4096 + (b - 4) * 1024)
                                V.tensor_copy(U[:, bass.ds(at, 1024)],
                                              PS[:, 2 * p:2 * p + 2, :].rearrange("p b n -> p (b n)")
                                              ).then_inc(acc_read, 1)
                                continue
                            if b:
                                dve.wait_ge(rope_sum, 4 * i + b)
                            for t in range(TT):
                                x = PS[:, 2 * p + t, :].rearrange("p (h d) -> p h d", h=8)
                                m1 = rope_m1[:, t * 512:(t + 1) * 512].rearrange("p (h d) -> p h d", h=8)
                                m2 = rope_m2[:, t * 512:(t + 1) * 512].rearrange("p (h d) -> p h d", h=8)
                                V.tensor_tensor(m1, x, wide(cosd, t, 0, 64), ALU.mult)
                                V.tensor_tensor(m2[:, :, 0:32], x[:, :, 32:64],
                                                wide(sind, t, 0, 32), ALU.mult)
                                last = V.tensor_tensor(m2[:, :, 32:64], x[:, :, 0:32],
                                                       wide(sind, t, 32, 64), ALU.mult)
                            last.then_inc(acc_read, 1)
                    repeat(dve, DIL_G, body)
                elif kind == "conv":
                    for c in range(4):
                        for part in range(3):
                            j = 3 * c + part
                            ahead(g0 + j, (g0 + j) % 2)
                            if part == 0 and c >= 2:
                                dve.wait_ge(conv_done, c - 1)
                            if part and c:
                                dve.wait_ge(conv_cu_done, c)
                            dst = (conv_b[:, c % 2, :], T1, T2)[part]
                            add_halves(st, dst, u0 + j, (u0 + j) % 2).then_inc(acc_read, 1)
                elif kind == "down":
                    def body(i):
                        for s in range(2):
                            ahead(g0 + 2 * i + s, slots[s])
                    repeat(dve, n // 2, body)
                    if n % 2:
                        ahead(g0 + n - 1, (g0 + n - 1) % 2)
                    for t in range(TT):
                        if t == 0:
                            dve.wait_ge(tile_done, st["down"] + 1)
                        else:
                            dve.wait_ge(chunk_done, g0 + n)
                        y = PS[:, 4 + 2 * t:6 + 2 * t, :].rearrange("p b n -> p (b n)")
                        if st["after"] == "x":
                            V.scalar_tensor_tensor(X[:, t, :], y, st["scale"], X[:, t, :],
                                                   ALU.mult, ALU.add).then_inc(x_new, 1)
                        elif st["after"] == "q":
                            V.tensor_copy(region(R["mla_qn"] + t * 768, 768),
                                          y[:, 0:768]).then_inc(x_new, 1)
                        else:
                            yh = y.rearrange("p (h d) -> p h d", h=8)
                            kn = region(R["mla_kn"] + t * 768, 768).rearrange("p (h d) -> p h d", h=8)
                            V.tensor_copy(kn[:, :, 0:64], yh[:, :, 0:64])
                            V.tensor_copy(region(R["mla_v"] + t * 512, 512)
                                          .rearrange("p (h d) -> p h d", h=8),
                                          yh[:, :, 64:128]).then_inc(x_new, 1)
                    if st["after"] == "q":
                        dve.wait_ge(x_new, st["x0"] + 2)
                        for t in range(TT):
                            q = region(R["mla_qn"] + t * 768, 768).rearrange("p (h d) -> p h d", h=8)
                            rope32(q[:, :, 64:96], q[:, :, 64:96], t, 8)
                    if st["after"] == "kv":
                        for t in range(TT):
                            kn = region(R["mla_kn"] + t * 768, 768).rearrange("p (h d) -> p h d", h=8)
                            last = V.tensor_copy(kn[:, :, 64:96], T3[:, t * 32:(t + 1) * 32]
                                                 .unsqueeze(1).to_broadcast([P, 8, 32]))
                        last.then_inc(mla_p, 1)
                elif kind == "mla_in":
                    def rope32(dst, x, t, h):
                        cos, sin = const("cosm"), const("sinm")
                        m1 = T1[:, 0:h * 32].rearrange("p (h d) -> p h d", h=h)
                        m2 = T2[:, 0:h * 32].rearrange("p (h d) -> p h d", h=h)
                        tab = lambda c, lo, hi: (c[:, t * 32 + lo:t * 32 + hi].unsqueeze(1)
                                                 .to_broadcast([P, h, hi - lo]))
                        V.tensor_tensor(m1, x, tab(cos, 0, 32), ALU.mult)
                        V.tensor_tensor(m2[:, :, 0:16], x[:, :, 16:32], tab(sin, 0, 16), ALU.mult)
                        link(V.tensor_tensor(m2[:, :, 16:32], x[:, :, 0:16], tab(sin, 16, 32), ALU.mult))
                        link(V.tensor_tensor(dst, m1, m2, ALU.add))

                    lat = region(R["latent"], 832)
                    lat_s = region(R["lat_s"], 768)
                    dve.wait_ge(consts_in, 16)
                    dve.wait_ge(mla_r, 2)
                    for t in range(TT):
                        rope32(T3[:, t * 32:(t + 1) * 32].unsqueeze(1),
                               lat[:, t * 416 + 384:t * 416 + 416].unsqueeze(1), t, 1)
                    for t in range(TT):
                        V.tensor_scalar(lat_s[:, t * 384:t * 384 + 256], lat[:, t * 416:t * 416 + 256],
                                        ST[:, 4 + t:5 + t], None, ALU.mult)
                        last = V.tensor_scalar(lat_s[:, t * 384 + 256:t * 384 + 384],
                                               lat[:, t * 416 + 256:t * 416 + 384],
                                               ST[:, 6 + t:7 + t], None, ALU.mult)
                    last.then_inc(mla_p, 1)
                    dve.wait_ge(mla_t, 1)
                    for b in range(3):
                        col = GAINS["q_norm"] + b if b < 2 else GAINS["ckv_norm"]
                        V.tensor_scalar(region(R["c"] + b * S, S), PS[:, b // 2, (b % 2) * S:(b % 2 + 1) * S],
                                        G[:, col:col + 1], None, ALU.mult).then_inc(h_done, 1)
                elif kind == "mla_qk":
                    dve.wait_ge(mla_t, 3)
                    V.tensor_copy(region(R["mla_kT"], 2048)[0:96, :],
                                  PS[0:96, 0:4, :].rearrange("p b n -> p (b n)")).then_inc(mla_p, 1)
                elif kind == "forget":
                    ahead(g0, slots[0])
                    dve.wait_ge(chunk_done, g0 + 1)
                    p = pairs[0]
                    for t in range(TT):
                        last = V.tensor_tensor(T1[:, t * 8:t * 8 + 8], PS[:, 2 * p + t, 0:8],
                                               G[:, GAINS["b_f"]:GAINS["b_f"] + 8], ALU.add)
                    last.then_inc(acc_read, 1)
                    dve.wait_ge(acc_read, u0 + 1)
                    link(V.tensor_scalar(T1[:, 16:32], T1[:, 0:16], -1.0, None, ALU.mult))
                    V.tensor_tensor(T1[:, 16:32], T1[:, 0:16], T1[:, 16:32], ALU.max).then_inc(f_v, 1)
                    link(V.tensor_scalar(T1[:, 64:80], T1[:, 0:16], 0.0, None, ALU.min))
                    dve.wait_ge(f_a, 2)
                    V.tensor_tensor(T1[:, 80:96], T1[:, 64:80], T1[:, 48:64],
                                    ALU.subtract).then_inc(f_v, 1)
                    dve.wait_ge(f_t, 1)
                    link(V.tensor_copy(ST[:, 32:48], PS[:, 0, 0:16]))
                    link(V.tensor_copy(region(RB["ck"], 2048), PS[:, 4:8, :].rearrange("p b n -> p (b n)")))
                elif kind == "attend":
                    a0, m = st["a0"], len(st["what"])

                    def soft(n):
                        e = heads[n]
                        dve.wait_ge(s_score, n + 1)
                        if n >= 3:
                            back = heads[n - 3]
                            dve.wait_ge(s_pt, back["group0"] + back["G"])
                        w_ = e["G"] * S
                        sc = e["scores"].rearrange("p (t n) -> p t n", t=2)
                        pr = e["probs"].rearrange("p (t n) -> p t n", t=2)
                        if e["bias"] is None:
                            link(V.tensor_reduce(e["mx"], sc, AXIS.X, ALU.max, negate=True))
                            V.tensor_scalar(e["mx"], e["mx"], e["scale"], None,
                                            ALU.mult).then_inc(s_soft, 1)
                            return
                        if e["bias"] == "dil":
                            V.scalar_tensor_tensor(e["probs"], e["scores"], e["scale"],
                                                   const("dil"), ALU.mult, ALU.add
                                                   ).then_inc(s_read, 1)
                        elif e["bias"] == "na":
                            if n == a0:
                                dve.wait_ge(bias_ready, 1)
                            for t in range(TT):
                                at = R["na_bias"] + e["h"] * SLOTS * GRID + (2 - 2 * t) * GRID
                                last = V.scalar_tensor_tensor(pr[:, t, :], sc[:, t, :], e["scale"],
                                                              region(at, S), ALU.mult, ALU.add)
                            last.then_inc(s_read, 1)
                        else:
                            ck = region(RB["ck"] + e["h"] * S, S)
                            for t in range(TT):
                                last = V.scalar_tensor_tensor(pr[:, t, :], sc[:, t, :], e["scale"], ck,
                                                              ALU.mult, ALU.subtract)
                            last.then_inc(s_read, 1)
                            dve.wait_ge(s_read, e["read"] + 1)
                            for t in range(TT):
                                col = 32 + t * 8 + e["h"]
                                last = V.scalar_tensor_tensor(
                                    pr[:, t, :], pr[:, t, :], ST[:, col:col + 1],
                                    const("causal")[:, t * S:(t + 1) * S], ALU.add, ALU.add)
                            link(last)
                        dve.wait_ge(s_read, e["read"] + 1)
                        V.tensor_reduce(e["mx"], pr, AXIS.X, ALU.max, negate=True).then_inc(s_soft, 1)

                    def normalise(n):
                        e = heads[n]
                        w_ = e["G"] * S
                        dve.wait_ge(s_exp, 2 * n + 2)
                        link(V.reciprocal(e["rz"], e["z"]))
                        for t in range(TT):
                            pr = e["probs"][:, t * w_:(t + 1) * w_]
                            last = V.tensor_scalar(pr, pr, e["rz"][:, t:t + 1], None, ALU.mult)
                        last.then_inc(s_norm, 1)

                    def output(n):
                        e = heads[n]
                        dve.wait_ge(s_pv, n + 1)
                        d = e["y"].shape[0]
                        V.tensor_copy(e["y"], PS[e["pb"]:e["pb"] + d, 6 + n % 2, 0:S]).then_inc(h_done, 1)

                    soft(a0)
                    soft(a0 + 1)
                    normalise(a0)
                    soft(a0 + 2)
                    for n_ in range(a0, a0 + m):
                        if n_ + 1 < a0 + m:
                            normalise(n_ + 1)
                        if n_ > a0:
                            output(n_ - 1)
                        if n_ + 3 < a0 + m:
                            soft(n_ + 3)
                    output(a0 + m - 1)

        @block.gpsimd
        def _(pool):
            chain = Count(pool_chain)
            chain.inc(nc.gpsimd.memset(ST[:, 62:64], -0.5))
            gains = (a["norm_final"], a["final_norm_2"])
            wide = lambda v: v.rearrange("(o n) -> o n", o=1).to_broadcast([P, D])

            def rstd(cols, width, done):
                chain.inc(nc.gpsimd.tensor_scalar(cols, cols, 1.0 / width, EPS, ALU.mult, ALU.add))
                pool.wait_ge(pool_chain, chain.value())
                nc.gpsimd.tensor_tensor(cols, cols, ST[:, 62:62 + cols.shape[1]], ALU.pow).then_inc(done, 1)

            for st in stages:
                g0, n, kind = st["g"], st["n"], st["kind"]
                if kind in ("norm", "final"):
                    for t in range(TT):
                        pool.wait_ge(n_sq, 2 * i_norm(st) + t + 1)
                        rstd(ST[:, t:t + 1], D, n_rstd)
                    if st["i"] == 0:
                        pool.dma_start(K[:, P:], a["const"][:, P:]).then_inc(consts_in, 16)
                        bias = region(R["na_bias"], NA_H * SLOTS * GRID)
                        pool.dma_start(bias, a["na_bias"]).then_inc(bias_in, 16)
                        pool.dma_start(GF[:], wide(gains[0])).then_inc(gain_in, 16)
                        pool.wait_ge(bias_in, 16)
                        pool.wait_ge(consts_in, 16)
                        rows = NA_H * SLOTS
                        view = bias.rearrange("p (r n) -> p r n", r=rows)
                        window = const("window").unsqueeze(1).to_broadcast([P, rows, GRID])
                        nc.gpsimd.tensor_tensor(view, view, window, ALU.add).then_inc(bias_ready, 1)
                if kind == "mla_in":
                    pool.wait_ge(mla_a, 1)
                    rstd(ST[:, 4:6], 256, mla_r)
                    rstd(ST[:, 6:8], 128, mla_r)
                if kind == "down":
                    def body(i, js=(0, 1)):
                        for s in js:
                            j, slot = 2 * i + s, (g0 + s) % 2
                            pool.wait_ge(st_hi, staged0(st) + j + 1)
                            nc.gpsimd.tensor_tensor(SX[:, slot, 1, 0:st["ks"] * S], down_src(st, j),
                                                    SX[:, slot, 0, 0:st["ks"] * S],
                                                    ALU.subtract).then_inc(st_lo, 1)
                    repeat(pool, n // 2, body)
                    if n % 2:
                        body(n // 2, (0,))
                    if st["name"] == "od_o":
                        pool.wait_ge(x_new, st["x0"] + 2)
                        pool.dma_start(MEM, a["mem_2"][0].rearrange("(t p) n -> p t n", p=P)
                                       ).then_inc(mem_in, 16)
                elif kind == "conv":
                    Pg = nc.gpsimd
                    T2v = [t.rearrange("p (f t) -> p f t", f=2) for t in (T1, T2)]

                    def step(ins):
                        chain.inc(ins)
                        pool.wait_ge(pool_chain, chain.value())

                    step(Pg.memset(conv_cu[:, :, 0:2], 0.0))
                    for c in range(4):
                        pool.wait_ge(acc_read, st["u"] + 3 * c + 3)
                        Pg.tensor_tensor(conv_cu[:, :, 2:S + 2], T2v[0], T2v[1],
                                         ALU.mult).then_inc(conv_cu_done, 1)
                        pool.wait_ge(conv_cu_done, c + 1)
                        for tap in (2, 1, 0):
                            dst = conv_acc if tap == 2 else conv_tap
                            for f in range(2):
                                col = GAINS["conv"] + tap * KD + 2 * c + f
                                last = Pg.tensor_scalar(dst[:, f, :], conv_cu[:, f, tap:tap + S],
                                                        G[:, col:col + 1], None, ALU.mult)
                            step(last)
                            if tap != 2:
                                step(Pg.tensor_tensor(conv_acc, conv_acc, conv_tap, ALU.add))
                        Pg.tensor_tensor(region(H0 + c * 512, 512),
                                         conv_acc.rearrange("p f t -> p (f t)"),
                                         conv_b[:, c % 2, :], ALU.mult).then_inc(conv_done, 1)
                        pool.wait_ge(conv_done, c + 1)
                elif kind == "dilated_in":
                    def body(i):
                        for b in range(4):
                            pool.wait_ge(acc_read, u_of(st) + 6 * i + b + 1)
                            if b >= 2:
                                pool.wait_ge(rope_tr, 4 * i + b - 1)
                            nc.gpsimd.tensor_tensor(rope_out[:, b % 2, :], rope_m1, rope_m2,
                                                    ALU.add).then_inc(rope_sum, 1)
                    repeat(pool, DIL_G, body)
                elif kind == "final" and not st["out"]:
                    pool.wait_ge(x_new, st["x0"] + 2)
                    pool.dma_start(GF[:], wide(gains[1])).then_inc(gain_in, 16)


def _constants():
    p, k = np.arange(P), np.arange(S)
    tokens = np.arange(S).reshape(TT, P)
    out = np.zeros((P, NCONST), np.float32)

    def put(name, value):
        lo, hi = CONST[name]
        out[:, lo:hi] = np.asarray(value, np.float32).reshape(P, hi - lo)

    put("ident", np.eye(P))
    q = tokens.T[:, :, None]
    far = k[None, None, :] - q
    put("dil", np.stack([np.where(ok, 0.0, NEG) for ok in
                         (np.abs(far) <= 64, far % 4 == 0, far % 16 == 0)], axis=2))
    put("causal", np.where(far <= 0, 0.0, NEG))
    c = p % GRID
    start = np.clip(c - 8, 0, GRID - 16)[:, None]
    col = np.arange(GRID)[None, :]
    put("window", np.where((col >= start) & (col < start + 16), 0.0, NEG))
    for name, dim in (("d", 64), ("m", 32)):
        inv = np.float32(1.0) / np.float32(10000.0) ** (np.arange(0, dim, 2, dtype=np.float32)
                                                        / np.float32(dim))
        ang = np.arange(S, dtype=np.float32)[:, None] * inv[None, :].astype(np.float32)
        cos, sin = np.cos(ang).astype(np.float32), np.sin(ang).astype(np.float32)
        cos = np.concatenate([cos, cos], 1).reshape(TT, P, dim).transpose(1, 0, 2)
        sin = np.concatenate([-sin, sin], 1).reshape(TT, P, dim).transpose(1, 0, 2)
        put("cos" + name, cos)
        put("sin" + name, sin)
    put("tri", (tokens.T[:, :, None] <= k[None, None, :]))
    return out


_WEIGHTS = ["x", "norm_final", "ev_w_in", "ev_w_uq", "ev_w_ukv", "ev_w_o", "od_w_in", "od_w_o",
            "mlp_w1", "mlp_w2", "mem_2", "ffn_w_gate_up_2", "ffn_w_down_2", "mem_w_kv_2",
            "a_w_in_2", "a_w_out_2", "w_kvf_2", "b_w_q_2", "b_w_out_2", "final_norm_2"]


def kernel(**inputs):
    import concourse.bacc as bacc
    from concourse.bass_utils import run_bass_kernel_spmd

    x = {k: np.asarray(v) for k, v in inputs.items()}
    cols = lambda v: v.reshape(-1, P).T
    gains = np.concatenate(
        [cols(x["norm_mix"][0]), cols(x["norm_mix"][1]), cols(x["norm_mlp"][0]),
         cols(x["norm_mlp"][1])]
        + [cols(x["ffn_norm_2"][l, i]) for l in range(2) for i in range(2)]
        + [cols(x["mix_norm_2"][0]), cols(x["mix_norm_2"][1]), cols(x["mem_norm_2"]),
           cols(x["kv_norm_2"]), cols(x["ev_q_norm"][0]), cols(x["ev_kv_norm"][0])]
        + [cols(x["a_conv_w_2"][0, j]) for j in range(3)]
        + [np.broadcast_to(x["b_f_2"], (P, 8))], axis=1)
    rel = np.clip(np.arange(GRID)[None, :] - np.arange(GRID)[:, None] + 15, 0, 30)
    rpb = x["ev_rpb"][0]
    na = [np.take(rpb[:, first:first + SLOTS], rel, axis=2).transpose(2, 0, 1, 3)
          for first in (5, 4)]
    arrays = {k: np.ascontiguousarray(x[k]) for k in _WEIGHTS}
    arrays["gains"] = np.ascontiguousarray(gains)
    arrays["na_bias"] = np.ascontiguousarray(np.concatenate(na, axis=0).reshape(P, -1))
    arrays["const"] = _constants()

    nc = bacc.Bacc("TRN2", target_bir_lowering=False, num_devices=1)
    handles = {k: nc.dram_tensor(f"in_{k}", v.shape, mybir.dt.from_np(v.dtype),
                                 kind="ExternalInput").ap() for k, v in arrays.items()}
    out = nc.dram_tensor("out_x", (1, S, D), F32, kind="ExternalOutput").ap()
    build_program(nc, handles, out)
    r = run_bass_kernel_spmd(nc, [{f"in_{k}": v for k, v in arrays.items()}], core_ids=[0])
    return r.results[0]["out_x"]
```

```python
from contextlib import ExitStack

import numpy as np

import concourse.bass as bass
from concourse import mybir

F32 = mybir.dt.float32
F32R = mybir.dt.float32r
ALU = mybir.AluOpType
ACT = mybir.ActivationFunctionType
AXIS = mybir.AxisListType

P = 128
S = 256
TT = S // P
D = 1024
KD = D // P
CH = 2048
TCOLS = CH // KD
EPS = 1e-6
NEG = -1e30
NA_H, NA_W = 8, 512
DIL_G, DIL_H = 3, 16
RES = 4
FF1, FF2 = 4096, 2816
ROWS, GRID = 4, 64
SLOTS = 6

CONST = {}
_at = 0
for _name, _n in (("ident", P), ("cosm", TT * 32), ("sinm", TT * 32), ("window", GRID),
                  ("dil", TT * 2 * S), ("causal", TT * S), ("cosd", TT * 64),
                  ("sind", TT * 64), ("tri", TT * S)):
    CONST[_name] = (_at, _at + _n)
    _at += _n
NCONST = _at
FIRST = CONST["window"][1]

GAINS = {}
_at = 0
for _name, _n in (("mix0", KD), ("mix1", KD), ("mlp0", KD), ("mlp1", KD), ("ffn00", KD),
                  ("ffn01", KD), ("ffn10", KD), ("ffn11", KD), ("bmix0", KD), ("bmix1", KD),
                  ("mem", KD), ("kv", KD), ("q_norm", 2), ("ckv_norm", 1), ("conv", 3 * KD),
                  ("b_f", 8)):
    GAINS[_name] = _at
    _at += _n
NGAIN = _at


class Count:

    def __init__(self, sem):
        self.sem, self.n, self.dyn = sem, 0, 0

    def inc(self, ins):
        self.n += 1
        ins.then_inc(self.sem, 1)

    def value(self):
        return self.dyn + self.n


def repeat(engine, n, body, counts=(), straight=False):
    if straight or n < 2:
        for i in range(n):
            body(i)
        return
    with engine.Fori(0, n) as i:
        start = [c.n for c, _ in counts]
        for c, per in counts:
            c.dyn = i * per
        body(i)
        for (c, per), was in zip(counts, start):
            assert c.n - was == per, (c.n, was, per)
            c.dyn, c.n = 0, was + per * n


class Plan:

    def __init__(self):
        self.stages, self.g, self.u, self.down = [], 0, 0, 0

    def add(self, kind, name, chunks=0, uses=0, **more):
        st = dict(kind=kind, name=name, g=self.g, u=self.u, n=chunks, down=self.down, **more)
        self.g += chunks
        self.u += uses
        self.down += kind == "down"
        self.stages.append(st)
        return st


def make_plan(w):
    p = Plan()

    def norm(gain, fill=None, again=False, by_residue=False):
        fill = fill and dict(zip(("what", "l", "c"), fill))
        p.add("norm", "norm_" + gain, *((1, 1) if fill else ()), gain=GAINS[gain], again=again,
              by_residue=by_residue,
              fill=fill, w=fill and w["mem_w_kv"][fill["l"]])

    def up(name, weight, col, chunks, **more):
        p.add("up", name, chunks, chunks, w=weight, col=col, **more)

    def natural(name, weight, col, blocks, ncols=512, **more):
        p.add("natural", name, 2 * blocks, blocks, w=weight, col=col, blocks=blocks,
              ncols=ncols, **more)

    def down(name, weight, rows, scale=1.0, ncols=D, ks=2, after="x", src="h", **more):
        p.add("down", name, rows // (ks * P), 0, w=weight, scale=scale, ncols=ncols, ks=ks,
              after=after, src=src, **more)

    norm("mix0")
    natural("latent", w["ev_w_in"], 1536, 1, ncols=416, dest="latent")
    p.add("mem_scale", "mem_scale")
    p.add("mla_in", "mla_in")
    up("na_qk", w["ev_w_in"], 0, 1, post="copy", dest="na_qk", latents=True)
    up("na_qk", w["ev_w_in"], 256, 1, post="copy", dest="na_qk", at=512)
    p.add("mla_turn", "mla_turn")
    p.add("mem_turn", "mem_turn", 0, 2, gain=GAINS["mem"])
    up("na_qk", w["ev_w_in"], 512, 1, post="copy", dest="na_qk", at=1024)
    down("ukv", w["ev_w_ukv"], 128, ks=1, after="kv", src="c")
    up("na_qk", w["ev_w_in"], 768, 1, post="copy", dest="na_qk", at=1536)
    p.add("mla_k", "mla_k", 0, 2)
    down("uq", w["ev_w_uq"], 256, ncols=768, after="q", src="c")
    natural("na_v", w["ev_w_in"], 1024, 1, dest="na_v")
    p.add("attend", "even", what=[("na", h) for h in range(8)] + [("mla", h) for h in range(8)])
    down("ev_o", w["ev_w_o"], 1024)
    norm("mlp0")
    up("mlp_up", w["mlp_w1"][0], 0, FF1 // TCOLS, post="relu2", dest="h")
    down("mlp_down", w["mlp_w2"][0], FF1)
    norm("mix1", by_residue=True)
    p.add("dilated_in", "dilated_in", DIL_G * 12, DIL_G * 6, w=w["od_w_in"])
    p.add("attend", "dilated", what=[("dil", h) for h in range(DIL_H)])
    down("od_o", w["od_w_o"], 1024)
    norm("mlp1", ("k", 0, 0))
    up("mlp_up", w["mlp_w1"][1], 0, FF1 // TCOLS, post="relu2", dest="h")
    down("mlp_down", w["mlp_w2"][1], FF1)
    p.add("final", "norm_final", 1, 1, out=False, fill=dict(what="v", l=0, c=0),
          w=w["mem_w_kv"][0])
    for l in range(2):
        if l == 1:
            norm("kv", ("k", 1, 1))
            up("fox_k", w["w_kvf"], 0, 4, post="copy", dest="fox_k")
            natural("fox_v", w["w_kvf"], 1024, 2, dest="fox_v")
            p.add("forget", "forget", 1, 1, w=w["w_kvf"], col=2048)
        norm(f"ffn{l}0", ("k", 0, 1) if l == 0 else ("v", 1, 0), again=l == 1)
        if l == 1:
            p.add("sums", "sums", 0, 1)
        p.add("glu", "glu", 2 * FF2 // TCOLS, 2 * FF2 // TCOLS, w=w["ffn_gu"][l][0])
        down("ffn_down", w["ffn_down"][l][0], FF2, scale=0.5)
        norm(f"bmix{l}", ("v", l, 1))
        if l == 0:
            p.add("conv", "conv", 12, 12, w=w["a_w_in"])
            up("mem_q", w["a_w_in"], 3072, 2, post="copy", dest="mem_q0")
            p.add("attend", "memory0", what=[("mem0", h) for h in range(4)])
            down("a_out", w["a_w_out"], 1536)
        else:
            up("fox_q", w["b_w_q"], 0, 4, post="copy", dest="fox_q")
            up("mem_q", w["b_w_q"], 1024, 2, post="copy", dest="mem_q1")
            p.add("attend", "fox",
                  what=[e for h in range(4) for e in (("fox", 2 * h), ("fox", 2 * h + 1), ("mem1", h))])
            down("b_out", w["b_w_out"], 1536)
        norm(f"ffn{l}1", ("k", 1, 0) if l == 0 else None)
        p.add("glu", "glu", 2 * FF2 // TCOLS, 2 * FF2 // TCOLS, w=w["ffn_gu"][l][1])
        down("ffn_down", w["ffn_down"][l][1], FF2, scale=0.5)
    p.add("final", "final_norm", out=True, fill=None)
    return p


def build_program(nc, a, out):
    blocked = lambda m: m.rearrange("(k p) n -> p k n", p=P)
    w = {
        "ev_w_in": blocked(a["ev_w_in"][0]), "ev_w_uq": blocked(a["ev_w_uq"][0]),
        "ev_w_ukv": blocked(a["ev_w_ukv"][0]), "ev_w_o": blocked(a["ev_w_o"][0]),
        "od_w_in": blocked(a["od_w_in"][0]), "od_w_o": blocked(a["od_w_o"][0]),
        "mlp_w1": [blocked(a["mlp_w1"][l]) for l in range(2)],
        "mlp_w2": [blocked(a["mlp_w2"][l]) for l in range(2)],
        "ffn_gu": [[blocked(a["ffn_w_gate_up_2"][l, i]) for i in range(2)] for l in range(2)],
        "ffn_down": [[blocked(a["ffn_w_down_2"][l, i]) for i in range(2)] for l in range(2)],
        "mem_w_kv": [blocked(a["mem_w_kv_2"][l]) for l in range(2)],
        "a_w_in": blocked(a["a_w_in_2"][0]), "a_w_out": blocked(a["a_w_out_2"][0]),
        "w_kvf": blocked(a["w_kvf_2"]), "b_w_q": blocked(a["b_w_q_2"][0]),
        "b_w_out": blocked(a["b_w_out_2"][0]),
    }
    plan = make_plan(w)
    stages, G_TOTAL = plan.stages, plan.g

    ctx = ExitStack()
    with ctx:
        def sb(name, shape, dt=F32):
            return ctx.enter_context(nc.sbuf_tensor(name, shape, dt))

        def sem(name):
            return ctx.enter_context(nc.semaphore(name))

        W_raw = sb("W_raw", [P, 2, CH])
        W_hi = sb("W_hi", [P, 2, CH], F32R)
        W_lo = sb("W_lo", [P, 2, CH], F32R)
        XM = sb("XM", [P, KD, 2, S], F32R)
        XN = sb("XN", [P, KD, 2, S], F32R)
        SX = sb("SX", [P, 2, 2, 2 * S], F32R)
        X = sb("X", [P, TT, D])
        K = sb("K", [P, NCONST])
        G = sb("G", [P, NGAIN])
        T = sb("T", [P, 2048])
        T0 = T[:, 0:1024].rearrange("p (u n) -> p u n", u=2)
        T1, T2 = T[:, 1024:1536], T[:, 1536:2048]
        ST = sb("ST", [P, 64])
        U = sb("U", [P, 23040])
        PS = ctx.enter_context(nc.psum_tensor("PS", [P, 8, 512], F32))

        const = lambda name: K[:, CONST[name][0]:CONST[name][1]]
        ident = const("ident")

        def region(at, n):
            return U[:, at:at + n]

        H0 = 0
        XS = region(0, 2 * D).rearrange("p (t n) -> p t n", t=TT)
        R = dict(na_qk=2048, na_v=4096, mla_qn=5120, mla_kn=6656, latent=8192, lat_s=9024,
                 c=9792, mla_v=10560, mla_qT=11584, mla_kT=13632, na_bias=15680,
                 sm=18752, pt=19776, mem=20800, kpe=22848)
        MEM = region(R["mem"], 2 * D).rearrange("p (t n) -> p t n", t=TT)
        KPE = region(R["kpe"], TT * 32)
        DIL0, DIL_SIZE = H0, 6144
        RD = dict(sm=DIL0 + DIL_G * DIL_SIZE, pt=DIL0 + DIL_G * DIL_SIZE + 2048)
        rope_m1 = region(RD["sm"], 1024)
        rope_m2 = region(RD["sm"] + 1024, 1024)
        rope_out = region(RD["sm"] + 2048, 2048).rearrange("p (b n) -> p b n", b=2)
        RB = dict(mem_k0=8192, mem_k1=9216, mem_v0=10240, mem_v1=11264, fox_k=12288,
                  fox_v=14336, fox_q=16384, ck=18432, sm=20992, pt=22016)
        RB["mem_q0"], RB["mem_q1"] = RB["fox_q"], RB["mem_k0"]
        T3 = region(RB["sm"], 512)
        GF = region(RB["pt"], D)
        conv_b = region(RB["fox_k"], 1024).rearrange("p (c n) -> p c n", c=2)
        conv_cu = region(RB["fox_k"] + 1024, 2 * (S + 2)).rearrange("p (f t) -> p f t", f=2)
        conv_acc = region(RB["fox_k"] + 1664, 512).rearrange("p (f t) -> p f t", f=2)
        conv_tap = region(RB["fox_k"] + 2176, 512).rearrange("p (f t) -> p f t", f=2)
        dest_at = dict(R, **{k: RB[k] for k in RB if k not in ("sm", "pt")}, h=H0)
        v_layout = lambda at, blk: region(at + blk * 1024, 1024)

        first_in = sem("first_in")
        consts_in = sem("consts_in")
        gain_in = sem("gain_in")
        x_in = [sem("x_in0"), sem("x_in1")]
        mem_in = sem("mem_in")
        warm = sem("warm")
        raw_tail = sem("raw_tail")
        raw_full = [sem("raw_full0"), sem("raw_full1")]
        w_hi = sem("w_hi")
        w_lo = sem("w_lo")
        chunk_done = sem("chunk_done")
        tile_done = sem("tile_done")
        acc_read = sem("acc_read")
        cross_out = sem("cross_out")
        h_done = sem("h_done")
        st_hi, st_lo = sem("st_hi"), sem("st_lo")
        x_new = sem("x_new")
        n_sq = sem("n_sq")
        n_rstd = sem("n_rstd")
        n_scaled = sem("n_scaled")
        n_tr = sem("n_tr")
        n_hi = sem("n_hi")
        n_lo = sem("n_lo")
        silu_out = sem("silu_out")
        rope_in, rope_sum = sem("rope_in"), sem("rope_sum")
        rope_tr, rope_kept = sem("rope_tr"), sem("rope_kept")
        mla_a, mla_p, mla_t, mla_r = sem("mla_a"), sem("mla_p"), sem("mla_t"), sem("mla_r")
        f_v, f_a, f_t = sem("f_v"), sem("f_a"), sem("f_t")
        s_score, s_soft, s_exp, s_norm = sem("s_score"), sem("s_soft"), sem("s_exp"), sem("s_norm")
        s_read = sem("s_read")
        s_pt, s_pte, s_pv = sem("s_pt"), sem("s_pte"), sem("s_pv")
        conv_cu_done = sem("conv_cu_done")
        conv_done = sem("conv_done")
        bias_in, bias_ready = sem("bias_in"), sem("bias_ready")
        dve_chain, act_chain, pool_chain = sem("dve_chain"), sem("act_chain"), sem("pool_chain")
        out_done = sem("out_done")

        def head(what, h):
            if what == "na":
                pb = 64 * (h % 2)
                q = region(R["na_qk"] + (h // 2) * S, S)[pb:pb + 64, :]
                k = region(R["na_qk"] + (4 + h // 2) * S, S)[pb:pb + 64, :]
                v = lambda g, kt: region(R["na_v"] + kt * 512 + h * 64, 64)
                y = region(H0 + (h // 2) * S, S)[pb:pb + 64, :]
                return dict(G=1, q=[q], k=[k], v=v, y=y, pb=pb, scale=64 ** -0.5, bias="na", R=R, h=h)
            if what == "mla":
                pb = 64 * (h % 2)
                q = region(R["mla_qT"] + h * S, S)[0:96, :]
                k = region(R["mla_kT"] + h * S, S)[0:96, :]
                v = lambda g, kt: region(R["mla_v"] + kt * 512 + h * 64, 64)
                y = region(H0 + (4 + h // 2) * S, S)[pb:pb + 64, :]
                return dict(G=1, q=[q], k=[k], v=v, y=y, pb=pb, scale=96 ** -0.5, bias=None, R=R, h=h)
            if what == "dil":
                pb, blk, pair = 64 * (h % 2), h // 8, h // 2
                q = [region(DIL0 + g * DIL_SIZE + pair * S, S)[pb:pb + 64, :] for g in range(3)]
                k = [region(DIL0 + g * DIL_SIZE + 2048 + pair * S, S)[pb:pb + 64, :] for g in range(3)]
                v = lambda g, kt: region(DIL0 + g * DIL_SIZE + 4096 + blk * 1024 + kt * 512
                                         + (h % 8) * 64, 64)
                y = region(H0 + pair * S, S)[pb:pb + 64, :]
                return dict(G=3, q=q, k=k, v=v, y=y, pb=pb, scale=64 ** -0.5, bias="dil", R=RD, h=h)
            if what == "fox":
                q = region(RB["fox_q"] + h * S, S)
                k = region(RB["fox_k"] + h * S, S)
                v = lambda g, kt: region(RB["fox_v"] + (h // 4) * 1024 + kt * 512 + (h % 4) * P, P)
                y = region(H0 + h * S, S)
                return dict(G=1, q=[q], k=[k], v=v, y=y, pb=0, scale=P ** -0.5, bias="fox", R=RB, h=h)
            l = int(what[3])
            q = region(RB[f"mem_q{l}"] + h * S, S)
            k = region(RB[f"mem_k{l}"] + h * S, S)
            v = lambda g, kt: region(RB[f"mem_v{l}"] + kt * 512 + h * P, P)
            y = region(H0 + (8 + h) * S, S)
            return dict(G=1, q=[q], k=[k], v=v, y=y, pb=0, scale=P ** -0.5, bias=None, R=RB, h=h)

        heads, n_groups = [], 0
        h_count = 0
        n_norm = n_final = 0
        for st in stages:
            st["h0"] = h_count
            if st["kind"] == "attend":
                st["a0"] = len(heads)
                for what, h in st["what"]:
                    e = head(what, h)
                    e["group0"] = n_groups
                    e["parts"] = 2 if e["G"] == 3 else 1
                    e["w"] = 2 * S if e["G"] == 3 else S
                    n_groups += e["parts"]
                    heads.append(e)
                h_count += len(st["what"])
            elif st["kind"] == "up" and st["dest"] == "h":
                h_count += st["n"]
            elif st["kind"] == "glu":
                h_count += st["n"] // 2
            elif st["kind"] == "mla_turn":
                h_count += 3
            elif st["kind"] in ("norm", "mem_scale"):
                st["i"] = n_norm - st.get("again", False)
                n_norm += not st.get("again")
            elif st["kind"] == "final":
                st["i"] = n_norm
                st["f"] = n_final
                n_norm += 1
                n_final += 1
        x_count = 0
        for st in stages:
            st["x0"] = x_count
            if st["kind"] in ("down", "final"):
                x_count += 2
        last_score, last_pt = {}, {}
        n_read = 0
        for n, e in enumerate(heads):
            e["score_banks"] = (n % 2 * 2, n % 2 * 2 + 1) if e["G"] == 3 else (n % 3,)
            e["score_prev"] = [last_score[b] for b in e["score_banks"] if b in last_score]
            for b in e["score_banks"]:
                last_score[b] = n
            e["pt_banks"] = [4, 5] if e["G"] == 3 else [3 + n % 2]
            e["pt_prev"] = []
            for g, b in enumerate(e["pt_banks"]):
                e["pt_prev"].append(last_pt.get(b))
                last_pt[b] = e["group0"] + g + 1
            b = e["score_banks"]
            e["scores"] = PS[:, b[0]:b[-1] + 1, :].rearrange("p b n -> p (b n)")
            width = e["w"] * TT
            e["probs"] = (region(e["R"]["sm"] + (n % 3) * width, width) if n % 3 < 2
                          else T[:, 0:width])
            e["read"] = n_read
            n_read += bool(e["bias"])
            e["ptile"] = [region(e["R"]["pt"] + ((n % 2) * e["parts"] + g) * 512, 512)
                          for g in range(e["parts"])]
            e["mx"] = ST[:, 8 + 8 * (n % 3):10 + 8 * (n % 3)]
            e["z"] = ST[:, 10 + 8 * (n % 3):12 + 8 * (n % 3)]
            e["rz"] = ST[:, 12 + 8 * (n % 3):14 + 8 * (n % 3)]


        k_norm = k_turn = n_glu = n_staged = n_cross = 0
        for n, st in enumerate(stages):
            if st["kind"] in ("norm", "mem_turn"):
                st["turn"] = k_turn
                k_turn += 1
            if st["kind"] == "norm":
                st["k"] = k_norm
                k_norm += 1
            if st["kind"] == "mem_turn":
                xm_ready = st["u"] + 2
            st["cross0"] = n_cross
            if st["kind"] in ("up", "glu", "conv") or (st.get("fill") or {}).get("what") == "k":
                n_cross += st["n"]
            if st["kind"] == "glu":
                st["silu0"] = n_glu
                n_glu += st["n"] // 2
            if st["kind"] == "down":
                st["staged0"] = n_staged
                n_staged += st["n"]
                before = stages[n - 1]
                before["next_down"] = st
                st["each"] = before["kind"] == "glu" or before.get("dest") == "h"
        i_norm = lambda st: st["i"]
        cross0 = lambda st: st["cross0"]
        silu0 = lambda st: st["silu0"]
        u_of = lambda st: st["u"]
        staged0 = lambda st: st["staged0"]
        before_heads = lambda st: len(stages[stages.index(st) - 1]["what"])
        n_made = lambda st: st["n"]

        def e_out_done(n):
            for st in stages:
                if st["kind"] == "attend" and st["a0"] <= n < st["a0"] + len(st["what"]):
                    return st["h0"] + n - st["a0"] + 1

        def raw_count(g, slot):
            if isinstance(g, int):
                return 16 * (g // 2 + 1)
            return g * 8 + (16 if slot == 0 else 8)

        def down_src(st, j):
            if st["src"] == "c":
                at = R["c"] + (0 if st["name"] == "uq" else 2 * S)
                return region(at, st["ks"] * S)
            return U[:, bass.ds(H0 + j * 2 * S, 2 * S)]

        def operands_ready(pe, st, n):
            if n == 0:
                pe.wait_ge(acc_read, st["u"])
                if st["name"] == "dilated":
                    pe.wait_ge(rope_kept, 4 * DIL_G)
            if st["what"][n] == ("mla", 0):
                pe.wait_ge(mla_a, 2)

        tokens_in = lambda st, x: x.rearrange("p (j r) -> p r j", r=RES) if st.get("by_residue") else x
        tokens_out = lambda st, x: x.rearrange("p (r j) -> p r j", r=RES) if st.get("by_residue") else x

        halves = lambda slot, h: slice(h * (CH // 2), (h + 1) * (CH // 2))
        block = ctx.enter_context(nc.Block())

        @block.sync
        def _(sp):
            for t in range(TT):
                sp.dma_start(X[:, t, :], a["x"][0, t * P:(t + 1) * P, :]).then_inc(x_in[t], 16)

            def load(g, slot, src, ks, n):
                if not isinstance(g, int) or g >= 2:
                    sp.wait_ge(w_lo, 2 * (g - 1))
                dst = W_raw[:, slot, 0:ks * n].rearrange("p (k n) -> p k n", k=ks)
                sp.dma_start(dst, src).then_inc(raw_full[slot], 16)

            for st in stages:
                g0, n, kind = st["g"], st["n"], st["kind"]
                w_ = st.get("w")
                slots = (g0 % 2, (g0 + 1) % 2)
                if kind == "up":
                    def body(i, ss=(0, 1)):
                        for s in ss:
                            load(g0 + 2 * i + s, slots[s],
                                 w_[:, :, bass.ds(st["col"] + (2 * i + s) * TCOLS, TCOLS)], KD, TCOLS)
                    repeat(sp, n // 2, body)
                    if n % 2:
                        body(n // 2, (0,))
                elif kind in ("norm", "final") and st["fill"]:
                    f = st["fill"]
                    col = (512 if f["what"] == "v" else 0) + f["c"] * TCOLS
                    load(g0, slots[0], w_[:, :, col:col + TCOLS], KD, TCOLS)
                elif kind == "glu":
                    def body(i):
                        for s in range(2):
                            load(g0 + 2 * i + s, slots[s],
                                 w_[:, :, bass.ds(s * FF2 + i * TCOLS, TCOLS)], KD, TCOLS)
                    repeat(sp, n // 2, body)
                elif kind == "natural":
                    for b in range(st["blocks"]):
                        for c in range(2):
                            col = st["col"] + b * 512
                            load(g0 + 2 * b + c, slots[c],
                                 w_[:, 4 * c:4 * c + 4, col:col + st["ncols"]], 4, st["ncols"])
                elif kind == "dilated_in":
                    def body(i):
                        for c in range(2):
                            load(g0 + 2 * i + c, slots[c],
                                 w_[:, 4 * c:4 * c + 4, bass.ds(i * 512, 512)], 4, 512)
                    repeat(sp, n // 2, body)
                elif kind == "conv":
                    for c in range(4):
                        for part in range(3):
                            col = part * D + c * TCOLS
                            load(g0 + 3 * c + part, (g0 + 3 * c + part) % 2,
                                 w_[:, :, col:col + TCOLS], KD, TCOLS)
                elif kind == "forget":
                    load(g0, slots[0], w_[:, :, st["col"]:st["col"] + 8], KD, 8)
                elif kind == "down":
                    ks = st["ks"]

                    def body(i):
                        for s in range(2):
                            load(g0 + 2 * i + s, slots[s],
                                 w_[:, bass.ds((2 * i + s) * ks, ks), :], ks, st["ncols"])
                    repeat(sp, n // 2, body)
                    if n % 2:
                        load(g0 + n - 1, (g0 + n - 1) % 2, w_[:, (n - 1) * ks:n * ks, :], ks,
                             st["ncols"])
            sp.wait_ge(x_new, x_count)
            sp.dma_start(out[0].rearrange("(t p) n -> p t n", p=P), X[:]).then_inc(out_done, 16)
            sp.wait_ge(out_done, 16)

        @block.tensor
        def _(pe):
            mm, tr = nc.tensor.matmul, nc.tensor.transpose

            def chunk_ready(g):
                pe.wait_ge(w_lo, 2 * g + 2)

            def acc_free(u):
                if not isinstance(u, int) or u >= 2:
                    pe.wait_ge(acc_read, u - 1)

            def wT(tile, slot, k, fb):
                return tile[:, slot, k * TCOLS + fb * P:k * TCOLS + (fb + 1) * P]

            def up_chunk(g, u, slot, pair, xn=XN, first=True):
                chunk_ready(g)
                acc_free(u)
                if xn is XM:
                    pe.wait_ge(acc_read, xm_ready)
                for fb in range(2):
                    bank = PS[:, 2 * pair + fb, :]
                    for k in range(KD):
                        if fb == 0 and first and xn is XN and k % 2 == 0:
                            pe.wait_ge(n_lo, xn_ready + k // 2 + 1)
                        both = xn[:, k, :, :].rearrange("p a t -> p (a t)")
                        if k == 0:
                            mm(bank, wT(W_hi, slot, k, fb), both, start=True, stop=False)
                            mm(bank[:, S:], wT(W_lo, slot, k, fb), xn[:, k, 0, :],
                               start=False, stop=False)
                        else:
                            mm(bank[:, S:], wT(W_lo, slot, k, fb), xn[:, k, 0, :],
                               start=False, stop=False)
                            last = mm(bank, wT(W_hi, slot, k, fb), both, start=False,
                                      stop=k == KD - 1)
                last.then_inc(chunk_done, 1)

            def three(bank, xh, xl, wh, wl, start, stop):
                mm(bank, xh, wh, start=start, stop=False)
                mm(bank, xh, wl, start=False, stop=False)
                return mm(bank, xl, wh, start=False, stop=stop)

            def natural_chunk(g, slot, pair, c, ncols):
                chunk_ready(g)
                for t in range(TT):
                    for ks in range(4):
                        k, n = 4 * c + ks, slice(ks * ncols, (ks + 1) * ncols)
                        if t == 0 and k % 2 == 0:
                            pe.wait_ge(n_lo, xn_ready + k // 2 + 1)
                        last = three(PS[:, 2 * pair + t, 0:ncols],
                                     XN[:, k, 0, t * P:(t + 1) * P], XN[:, k, 1, t * P:(t + 1) * P],
                                     W_hi[:, slot, n], W_lo[:, slot, n], k == 0, k == KD - 1)
                last.then_inc(chunk_done, 1)

            def fill_chunk(st):
                g, u = st["g"], st["u"]
                if st["fill"]["what"] == "k":
                    up_chunk(g, u, g % 2, u % 2, XM)
                    return
                chunk_ready(g)
                acc_free(u)
                pe.wait_ge(acc_read, xm_ready)
                for t in range(TT):
                    for k in range(KD):
                        n = slice(k * TCOLS, (k + 1) * TCOLS)
                        last = three(PS[:, 2 * (u % 2) + t, 0:TCOLS],
                                     XM[:, k, 0, t * P:(t + 1) * P], XM[:, k, 1, t * P:(t + 1) * P],
                                     W_hi[:, g % 2, n], W_lo[:, g % 2, n], k == 0, k == KD - 1)
                last.then_inc(chunk_done, 1)

            def down_chunk(st, g, staged, slot, first, final):
                chunk_ready(g)
                pe.wait_ge(st_lo, staged)
                ncols, ks_n = st["ncols"], st["ks"]
                for t in range(TT):
                    if first and t == 1 and st["src"] == "h" and not st["each"]:
                        pe.wait_ge(h_done, st["h0"])
                    for ks in range(ks_n):
                        x = slice(ks * S + t * P, ks * S + (t + 1) * P)
                        for b in range(2):
                            lo, hi = b * 512, min(ncols, b * 512 + 512)
                            n = slice(ks * ncols + lo, ks * ncols + hi)
                            last = three(PS[:, 4 + 2 * t + b, 0:hi - lo],
                                         SX[:, slot, 0, x], SX[:, slot, 1, x],
                                         W_hi[:, slot, n], W_lo[:, slot, n],
                                         first and ks == 0, final and ks == ks_n - 1)
                    if final and t == 0:
                        last.then_inc(tile_done, 1)
                last.then_inc(chunk_done, 1)

            def turn_xs(bank, blocks):
                for b in blocks:
                    for k in (2 * b, 2 * b + 1):
                        for t in range(TT):
                            at = (k % 2) * S + t * P
                            last = tr(PS[:, bank + b, at:at + P], XS[:, t, k * P:(k + 1) * P], ident)
                    last.then_inc(n_tr, 1)

            def turn_heads(src, bank, hs):
                for h in hs:
                    for t in range(TT):
                        at = (h % 2) * S + t * P
                        last = tr(PS[0:96, bank + h // 2, at:at + P],
                                  region(src + t * 768 + h * 96, 96), ident)
                last.then_inc(mla_t, 1)

            pe.wait_ge(warm, 1)
            for _ in range(8):
                mm(PS[:, 0, :], T[:, 0:P], T[:, 0:512], start=True, stop=True)
            staged = 0
            pe.wait_ge(first_in, 32)
            for st in stages:
                g0, u0, n, kind = st["g"], st["u"], st["n"], st["kind"]
                slots, pairs = (g0 % 2, (g0 + 1) % 2), (u0 % 2, (u0 + 1) % 2)
                if kind == "sums":
                    pe.wait_ge(consts_in, 16)
                if kind == "norm":
                    i = st["i"]
                    if st["fill"] and not st["again"]:
                        fill_chunk(st)
                    pe.wait_ge(n_scaled, 2 * i_norm(st) + 2)
                    turn_xs(4, range(4))
                    if st["fill"] and st["again"]:
                        fill_chunk(st)
                    xn_ready = 4 * st["k"]
                elif kind == "final" and st["fill"]:
                    fill_chunk(st)
                elif kind == "mem_turn":
                    pe.wait_ge(n_scaled, 4)
                    for b in range(2):
                        acc_free(u0 + b)
                        turn_xs(2 * pairs[b] - 2 * b, (2 * b, 2 * b + 1))
                elif kind in ("up", "glu"):
                    def body(i, ss=(0, 1)):
                        for s in ss:
                            up_chunk(g0 + 2 * i + s, u0 + 2 * i + s, slots[s], pairs[s], first=s == 0)
                    repeat(pe, n // 2, body)
                    if n % 2:
                        body(n // 2, (0,))
                elif kind == "conv":
                    for c in range(n):
                        up_chunk(g0 + c, u0 + c, (g0 + c) % 2, (u0 + c) % 2, first=c == 0)
                elif kind == "natural":
                    for b in range(st["blocks"]):
                        acc_free(u0 + b)
                        for c in range(2):
                            natural_chunk(g0 + 2 * b + c, slots[c], (u0 + b) % 2, c, st["ncols"])
                elif kind == "dilated_in":
                    def turn(i, b, q):
                        pe.wait_ge(rope_sum, 4 * i + b + 1)
                        if q >= 2:
                            pe.wait_ge(rope_kept, 4 * i + b - 1)
                        elif not isinstance(i, int):
                            pass
                        for pr in range(4):
                            for t in range(TT):
                                last = tr(PS[:, 4 + 2 * (b % 2) + pr // 2,
                                             (pr % 2) * S + t * P:(pr % 2) * S + (t + 1) * P],
                                          rope_out[:, b % 2, t * 512 + pr * P:t * 512 + (pr + 1) * P],
                                          ident)
                        last.then_inc(rope_tr, 1)

                    def body(i):
                        for b in range(6):
                            acc_free(u0 + 6 * i + b)
                            for c in range(2):
                                natural_chunk(g0 + 12 * i + 2 * b + c, slots[c], (u0 + b) % 2, c, 512)
                            if 1 <= b <= 4:
                                turn(i, b - 1, b - 1)
                    repeat(pe, DIL_G, body)
                elif kind == "forget":
                    chunk_ready(g0)
                    acc_free(u0)
                    for t in range(TT):
                        for k in range(KD):
                            f = slice(k * 8, k * 8 + 8)
                            last = three(PS[:, 2 * pairs[0] + t, 0:8], XN[:, k, 0, t * P:(t + 1) * P],
                                         XN[:, k, 1, t * P:(t + 1) * P], W_hi[:, slots[0], f],
                                         W_lo[:, slots[0], f], k == 0, k == KD - 1)
                    last.then_inc(chunk_done, 1)
                elif kind == "sums":
                    pe.wait_ge(f_v, 2)
                    acc_free(u0)
                    pe.wait_ge(n_lo, xn_ready + 4)
                    tri, ls = const("tri"), T1[:, 80:96]
                    for q in range(TT):
                        for t in range(TT):
                            mm(PS[:, 2 * pairs[0], q * 8:q * 8 + 8],
                               tri[:, t * S + q * P:t * S + (q + 1) * P],
                               ls[:, t * 8:t * 8 + 8], start=t == 0, stop=t == TT - 1)
                    for h in range(8):
                        for t in range(TT):
                            last = mm(PS[:, 4 + h // 2, (h % 2) * S:(h % 2 + 1) * S],
                                      ls[:, t * 8 + h:t * 8 + h + 1].to_broadcast([P, P]),
                                      tri[:, t * S:(t + 1) * S], start=t == 0, stop=t == TT - 1)
                    last.then_inc(f_t, 1)
                elif kind == "down":
                    for j in (0,) if n > 1 else ():
                        down_chunk(st, g0, staged + 1, g0 % 2, True, False)
                    if n == 1:
                        if st["name"] == "uq":
                            pe.wait_ge(x_new, st["x0"])
                        down_chunk(st, g0, staged + 1, g0 % 2, True, True)
                    mid = max(n - 2, 0)

                    def body(i):
                        for s in range(2):
                            down_chunk(st, g0 + 1 + 2 * i + s, staged + 2 + 2 * i + s,
                                       (g0 + 1 + s) % 2, False, False)
                    repeat(pe, mid // 2, body)
                    for j in range(1 + mid // 2 * 2, n):
                        down_chunk(st, g0 + j, staged + j + 1, (g0 + j) % 2, False, j == n - 1)
                    staged += n
                elif kind == "mla_turn":
                    pe.wait_ge(mla_p, 1)
                    lat = region(R["lat_s"], 768)
                    for b in range(3):
                        for t in range(TT):
                            last = tr(PS[:, 4 + b // 2, (b % 2) * S + t * P:(b % 2) * S + (t + 1) * P],
                                      lat[:, t * 384 + b * P:t * 384 + (b + 1) * P], ident)
                    last.then_inc(mla_t, 1)
                elif kind == "mla_k":
                    pe.wait_ge(mla_p, 2)
                    for b in range(2):
                        acc_free(u0 + b)
                        turn_heads(R["mla_kn"], 2 * pairs[b] - 2 * b, range(4 * b, 4 * b + 4))
                elif kind == "attend":
                    a0, m = st["a0"], len(st["what"])

                    def scores(n):
                        e = heads[n]
                        operands_ready(pe, st, n - a0)
                        for prev in e["score_prev"]:
                            if heads[prev]["bias"]:
                                pe.wait_ge(s_read, heads[prev]["read"] + 1)
                            else:
                                pe.wait_ge(s_exp, 2 * prev + 2)
                        for t in range(TT):
                            for g in range(e["G"]):
                                at = t * e["w"] + (S + (g - 1) * P if g else 0)
                                keys = slice(t * P, (t + 1) * P) if g else slice(0, S)
                                last = mm(e["scores"][:, at:at + keys.stop - keys.start],
                                          e["q"][g][:, t * P:(t + 1) * P], e["k"][g][:, keys],
                                          start=True, stop=True)
                        last.then_inc(s_score, 1)

                    def transposes(n):
                        e = heads[n]
                        pe.wait_ge(s_norm, n + 1)
                        if st["name"] == "even" and n == a0 + 1:
                            pe.wait_ge(mla_a, 2)
                        for part in range(e["parts"]):
                            if e["pt_prev"][part]:
                                pe.wait_ge(s_pte, e["pt_prev"][part])
                            for i in range(2):
                                for t in range(TT):
                                    at = t * e["w"] + part * S + i * P
                                    last = tr(PS[:, e["pt_banks"][part],
                                                 i * S + t * P:i * S + (t + 1) * P],
                                              e["probs"][:, at:at + P], ident)
                            last.then_inc(s_pt, 1)

                    def values(n):
                        e = heads[n]
                        if st["name"] == "even" and n == a0:
                            pe.wait_ge(mla_a, 2)
                        if n >= 2:
                            pe.wait_ge(h_done, e_out_done(n - 2))
                        d = 64 if e["pb"] or e["bias"] in ("na", "dil") or e["scale"] == 96 ** -0.5 else P
                        o = PS[e["pb"]:e["pb"] + d, 6 + n % 2, 0:S]
                        pe.wait_ge(s_pte, e["group0"] + 1)
                        for kt in range(TT):
                            last = mm(o, e["v"](0, kt), e["ptile"][0][:, kt * S:(kt + 1) * S],
                                      start=kt == 0, stop=kt == TT - 1 and e["parts"] == 1)
                        if e["parts"] == 2:
                            pe.wait_ge(s_pte, e["group0"] + 2)
                            for g in (1, 2):
                                for t in range(TT):
                                    at = (g - 1) * S + t * P
                                    last = mm(o[:, t * P:(t + 1) * P], e["v"](g, t),
                                              e["ptile"][1][:, at:at + P], start=False,
                                              stop=g == 2 and t == TT - 1)
                        last.then_inc(s_pv, 1)

                    for n_ in range(3):
                        scores(a0 + n_)
                    if st["name"] == "even":
                        pe.wait_ge(mla_p, 3)
                        turn_heads(R["mla_qn"], 4, range(8))
                    for n_ in range(a0, a0 + m):
                        transposes(n_)
                        if n_ + 3 < a0 + m:
                            scores(n_ + 3)
                        values(n_)

        @block.scalar
        def _(act):
            A = nc.scalar.activation

            def split_hi(g, slot):
                if not isinstance(g, int) or g >= 2:
                    act.wait_ge(chunk_done, g - 1)
                act.wait_ge(raw_full[slot], raw_count(g, slot))
                for h in range(2):
                    A(W_hi[:, slot, halves(slot, h)], W_raw[:, slot, halves(slot, h)],
                      ACT.Copy).then_inc(w_hi, 1)

            def ahead(g, slot):
                if not isinstance(g, int) or g + 1 < G_TOTAL:
                    split_hi(g + 1, 1 - slot)

            def cross(g, u, pair):
                act.wait_ge(chunk_done, g + 1)
                if not isinstance(u, int) or u >= 2:
                    act.wait_ge(acc_read, u - 1)
                A(T0[:, pair, :].rearrange("p (f t) -> p f t", f=2),
                  PS[:, 2 * pair:2 * pair + 2, S:2 * S], ACT.Copy).then_inc(cross_out, 1)

            def square(st, t):
                if st["kind"] == "mem_scale":
                    act.wait_ge(mem_in, 16)
                elif st["x0"] == 0:
                    act.wait_ge(x_in[t], 16)
                else:
                    act.wait_ge(x_new, st["x0"] - 1 + t)
                if st["i"]:
                    act.wait_ge(n_scaled, 2 * st["i"])
                src = MEM if st["kind"] == "mem_scale" else X
                A(XS[:, t, :], src[:, t, :], ACT.Square,
                  accum_out=ST[:, t:t + 1]).then_inc(n_sq, 1)

            def round_xs(st, dst, bank, blocks):
                for b in blocks:
                    act.wait_ge(n_tr, 4 * st["turn"] + b + 1)
                    for k in (2 * b, 2 * b + 1):
                        last = A(tokens_out(st, dst[:, k, 0, :]),
                                 tokens_in(st, PS[:, bank + b, (k % 2) * S:(k % 2 + 1) * S]), ACT.Copy, scale=G[:, st["gain"] + k:st["gain"] + k + 1])
                    last.then_inc(n_hi, 1)

            def stage_early(st):
                for j in range(min(2, st["n"])):
                    stage_hi(st, j, st["g"] + j, (st["g"] + j) % 2, True)

            def stage_hi(st, j, g, slot, early=False):
                if st["src"] == "c":
                    act.wait_ge(h_done, st["h0"])
                elif st["each"]:
                    act.wait_ge(h_done, st["h0"] - n_made(st) + j + 1)
                elif early:
                    act.wait_ge(conv_done, 4) if st["name"] == "a_out" else act.wait_ge(
                        h_done, st["h0"] - before_heads(st) + 8)
                else:
                    act.wait_ge(h_done, st["h0"])
                if not early or st["src"] == "c":
                    act.wait_ge(chunk_done, g - 1)
                A(SX[:, slot, 0, 0:st["ks"] * S], down_src(st, j), ACT.Copy).then_inc(st_hi, 1)

            mem_scale = next(st for st in stages if st["kind"] == "mem_scale")
            act.dma_start(K[:, 0:FIRST], a["const"][:, 0:FIRST]).then_inc(first_in, 16)
            act.dma_start(G[:], a["gains"]).then_inc(first_in, 16)
            act.wait_ge(first_in, 32)
            for st in stages:
                g0, u0, n, kind = st["g"], st["u"], st["n"], st["kind"]
                slots, pairs = (g0 % 2, (g0 + 1) % 2), (u0 % 2, (u0 + 1) % 2)
                if kind in ("norm", "final"):
                    for t in () if st.get("again") else range(TT):
                        square(st, t)
                    if g0 == 0:
                        act.wait_ge(raw_tail, 1)
                        split_hi(0, 0)
                    if st.get("fill"):
                        ahead(g0, slots[0])
                    if kind == "norm":
                        act.wait_ge(chunk_done, g0) if g0 else None
                        round_xs(st, XN, 4, range(4))
                    if st.get("fill") and st["fill"]["what"] == "k":
                        cross(g0, u0, pairs[0])
                elif kind == "mem_turn":
                    for b in range(2):
                        round_xs(st, XM, 2 * pairs[b] - 2 * b, (2 * b, 2 * b + 1))
                elif kind in ("up", "conv", "natural"):
                    def body(i, ss=(0, 1)):
                        for s in ss:
                            ahead(g0 + 2 * i + s, slots[s])
                            if kind != "natural":
                                cross(g0 + 2 * i + s, u0 + 2 * i + s, pairs[s])
                            if st.get("dest") == "latent" and s == 0:
                                for t in range(TT):
                                    square(mem_scale, t)
                    early = st.get("next_down")
                    repeat(act, n // 2 - bool(early and n > 1), body, straight=g0 == 0)
                    if early:
                        stage_early(early)
                        if n > 1:
                            body(n // 2 - 1)
                    if n % 2:
                        body(n // 2, (0,))
                elif kind == "glu":
                    def body(i):
                        for s in range(2):
                            ahead(g0 + 2 * i + s, slots[s])
                            if s == 1:
                                act.wait_ge(acc_read, u_of(st) + 2 * i + 1)
                                act.wait_ge(h_done, st["h0"] + i)
                                A(T3, T1, ACT.Silu).then_inc(silu_out, 1)
                            cross(g0 + 2 * i + s, u0 + 2 * i + s, pairs[s])
                    A(ST[:, 60:61], G[:, 0:1], ACT.Silu)
                    repeat(act, n // 2 - 1, body)
                    stage_early(st["next_down"])
                    body(n // 2 - 1)
                elif kind == "dilated_in":
                    def keep(i, b):
                        act.wait_ge(rope_tr, 4 * i + b + 1)
                        at = i * DIL_SIZE + (DIL0 + (b // 2) * 2048 + (b % 2) * 1024)
                        A(U[:, bass.ds(at, 1024)],
                          PS[:, 4 + 2 * (b % 2):6 + 2 * (b % 2), :].rearrange("p b n -> p (b n)"),
                          ACT.Copy).then_inc(rope_kept, 1)

                    def body(i):
                        for b in range(6):
                            for c in range(2):
                                ahead(g0 + 12 * i + 2 * b + c, slots[c])
                            if b >= 2:
                                keep(i, b - 2)
                    repeat(act, DIL_G, body)
                elif kind == "down":
                    def body(i):
                        for s in range(2):
                            ahead(g0 + 2 * i + s, slots[s])
                            stage_hi(st, 2 * i + s + 2, g0 + 2 * i + s + 2, slots[s])
                    rounds = max(n - 2, 0) // 2
                    repeat(act, rounds, body)
                    for j in range(2 * rounds, n):
                        ahead(g0 + j, (g0 + j) % 2)
                        if j + 2 < n:
                            stage_hi(st, j + 2, g0 + j + 2, (g0 + j) % 2)
                elif kind == "forget":
                    ahead(g0, slots[0])
                    act.wait_ge(f_v, 1)
                    A(T1[:, 32:48], T1[:, 16:32], ACT.Exp, scale=-1.0).then_inc(f_a, 1)
                    act.wait_ge(f_a, 1)
                    A(T1[:, 48:64], T1[:, 32:48], ACT.Ln, bias=1.0).then_inc(f_a, 1)
                elif kind == "mla_in":
                    act.wait_ge(acc_read, u_of(st))
                    lat = region(R["latent"], 832)
                    for t in range(TT):
                        A(T1[:, t * 256:(t + 1) * 256], lat[:, t * 416:t * 416 + 256], ACT.Square,
                          accum_out=ST[:, 4 + t:5 + t])
                        last = A(T2[:, t * 256:t * 256 + P], lat[:, t * 416 + 256:t * 416 + 384],
                                 ACT.Square, accum_out=ST[:, 6 + t:7 + t])
                    last.then_inc(mla_a, 1)
                elif kind == "mla_k":
                    stage_early(st["next_down"])
                elif kind == "attend":
                    a0, m = st["a0"], len(st["what"])

                    def exps(n):
                        e = heads[n]
                        act.wait_ge(s_soft, n + 1)
                        w_ = e["w"]
                        for t in range(TT):
                            src = e["probs"] if e["bias"] else e["scores"]
                            A(e["probs"][:, t * w_:(t + 1) * w_], src[:, t * w_:(t + 1) * w_], ACT.Exp,
                              bias=e["mx"][:, t:t + 1], scale=1.0 if e["bias"] else e["scale"],
                              accum_out=e["z"][:, t:t + 1]).then_inc(s_exp, 1)

                    def keep_pt(n):
                        e = heads[n]
                        for g in range(e["parts"]):
                            act.wait_ge(s_pt, e["group0"] + g + 1)
                            if n > 1:
                                act.wait_ge(s_pv, n - 1)
                            A(e["ptile"][g], PS[:, e["pt_banks"][g], :], ACT.Copy).then_inc(s_pte, 1)

                    exps(a0)
                    if st["name"] == "even":
                        act.wait_ge(mla_t, 4)
                        A(region(R["mla_qT"], 2048)[0:96, :],
                          PS[0:96, 4:8, :].rearrange("p b n -> p (b n)"), ACT.Copy).then_inc(mla_a, 1)
                    exps(a0 + 1)
                    for n_ in range(a0, a0 + m):
                        keep_pt(n_)
                        if n_ + 2 < a0 + m:
                            exps(n_ + 2)
                        if n_ == a0 + m - 3:
                            stage_early(st["next_down"])

        @block.vector
        def _(dve):
            V = nc.vector
            chain = Count(dve_chain)
            V.memset(T[:, 0:512], 0.0).then_inc(warm, 1)

            def link(ins):
                chain.inc(ins)
                dve.wait_ge(dve_chain, chain.value())

            def split_lo(g, slot):
                for h in range(2):
                    dve.wait_ge(w_hi, 2 * g + h + 1)
                    V.tensor_tensor(W_lo[:, slot, halves(slot, h)], W_raw[:, slot, halves(slot, h)],
                                    W_hi[:, slot, halves(slot, h)], ALU.subtract).then_inc(w_lo, 1)

            def ahead(g, slot):
                if not isinstance(g, int) or g + 1 < G_TOTAL:
                    split_lo(g + 1, 1 - slot)

            def add_halves(st, dst, u, pair):
                dve.wait_ge(cross_out, u - u_of(st) + cross0(st) + 1)
                return V.tensor_tensor(dst.rearrange("p (f t) -> p f t", f=2),
                                       PS[:, 2 * pair:2 * pair + 2, 0:S],
                                       T0[:, pair, :].rearrange("p (f t) -> p f t", f=2), ALU.add)

            def rest_xs(st, dst, bank, b):
                dve.wait_ge(n_hi, 4 * st["turn"] + b + 1)
                for k in (2 * b, 2 * b + 1):
                    last = V.scalar_tensor_tensor(
                        tokens_out(st, dst[:, k, 1, :]),
                        tokens_in(st, PS[:, bank, (k % 2) * S:(k % 2 + 1) * S]),
                        G[:, st["gain"] + k:st["gain"] + k + 1], tokens_out(st, dst[:, k, 0, :]),
                        ALU.mult, ALU.subtract)
                return last

            def rope32(dst, x, t, h, complete=False):
                cos, sin = const("cosm"), const("sinm")
                m1 = T1[:, 0:h * 32].rearrange("p (h d) -> p h d", h=h)
                m2 = T2[:, 0:h * 32].rearrange("p (h d) -> p h d", h=h)
                tab = lambda c, lo, hi: (c[:, t * 32 + lo:t * 32 + hi].unsqueeze(1)
                                         .to_broadcast([P, h, hi - lo]))
                V.tensor_tensor(m1, x, tab(cos, 0, 32), ALU.mult)
                V.tensor_tensor(m2[:, :, 0:16], x[:, :, 16:32], tab(sin, 0, 16), ALU.mult)
                link(V.tensor_tensor(m2[:, :, 16:32], x[:, :, 0:16], tab(sin, 16, 32), ALU.mult))
                last = V.tensor_tensor(dst, m1, m2, ALU.add)
                last.then_inc(mla_p, 1) if complete else link(last)

            def scale_latents():
                lat = region(R["latent"], 832)
                lat_s = region(R["lat_s"], 768)
                dve.wait_ge(mla_r, 2)
                for t in range(TT):
                    rope32(KPE[:, t * 32:(t + 1) * 32].unsqueeze(1),
                           lat[:, t * 416 + 384:t * 416 + 416].unsqueeze(1), t, 1)
                for t in range(TT):
                    V.tensor_scalar(lat_s[:, t * 384:t * 384 + 256], lat[:, t * 416:t * 416 + 256],
                                    ST[:, 4 + t:5 + t], None, ALU.mult)
                    last = V.tensor_scalar(lat_s[:, t * 384 + 256:t * 384 + 384],
                                           lat[:, t * 416 + 256:t * 416 + 384],
                                           ST[:, 6 + t:7 + t], None, ALU.mult)
                last.then_inc(mla_p, 1)

            dve.wait_ge(first_in, 32)
            silu_n = 0
            for st in stages:
                g0, u0, n, kind = st["g"], st["u"], st["n"], st["kind"]
                slots, pairs = (g0 % 2, (g0 + 1) % 2), (u0 % 2, (u0 + 1) % 2)
                if kind in ("norm", "final", "mem_scale"):
                    i, again = i_norm(st), st.get("again")
                    src = MEM if kind == "mem_scale" else X
                    if kind == "final":
                        dve.wait_ge(gain_in, 16 * (st["f"] + 1))
                    for t in () if again else range(TT):
                        dve.wait_ge(n_rstd, 2 * i + t + 1)
                        V.tensor_scalar(XS[:, t, :], src[:, t, :], ST[:, t:t + 1], None,
                                        ALU.mult).then_inc(n_scaled, 1)
                        if kind == "final":
                            dve.wait_ge(n_scaled, 2 * i + t + 1)
                            V.tensor_tensor(X[:, t, :], XS[:, t, :], GF, ALU.mult).then_inc(x_new, 1)
                    if i == 0:
                        split_lo(0, 0)
                    if st.get("fill"):
                        ahead(g0, slots[0])
                    if kind == "norm":
                        for b in range(4):
                            rest_xs(st, XN, 4 + b, b).then_inc(n_lo, 1)
                    if st.get("fill"):
                        f = st["fill"]
                        at = RB[f"mem_{f['what']}{f['l']}"]
                        if f["what"] == "k":
                            add_halves(st, region(at + f["c"] * 512, 512), u0, pairs[0]
                                       ).then_inc(acc_read, 1)
                        else:
                            dve.wait_ge(chunk_done, g0 + 1)
                            dst = region(at, 1024).rearrange("p (t n) -> p t n", t=2)
                            V.tensor_copy(dst[:, :, f["c"] * TCOLS:(f["c"] + 1) * TCOLS],
                                          PS[:, 2 * pairs[0]:2 * pairs[0] + 2, 0:TCOLS]
                                          ).then_inc(acc_read, 1)
                elif kind == "mem_turn":
                    for b in range(4):
                        last = rest_xs(st, XM, 2 * pairs[b // 2] + b % 2, b)
                        if b % 2:
                            last.then_inc(acc_read, 1)
                elif kind == "up":
                    at = dest_at[st["dest"]] + st.get("at", 0)

                    def body(i, ss=(0, 1)):
                        for s in ss:
                            g, c = g0 + 2 * i + s, 2 * i + s
                            ahead(g, slots[s])
                            if st.get("latents"):
                                scale_latents()
                            dve.wait_ge(chunk_done, g + 1)
                            dst = U[:, bass.ds(at + c * 512, 512)]
                            if st["post"] == "copy":
                                add_halves(st, dst, u0 + c, pairs[s]).then_inc(acc_read, 1)
                            else:
                                dve.wait_ge(h_done, st["h0"] + c)
                                add_halves(st, T1, u0 + c, pairs[s]).then_inc(acc_read, 1)
                                dve.wait_ge(acc_read, u0 + c + 1)
                                V.scalar_tensor_tensor(dst, T1, 0.0, T1, ALU.max,
                                                       ALU.mult).then_inc(h_done, 1)
                    repeat(dve, n // 2, body)
                    if n % 2:
                        body(n // 2, (0,))
                elif kind == "glu":
                    def body(i):
                        ahead(g0 + 2 * i, slots[0])
                        dve.wait_ge(chunk_done, g0 + 2 * i + 1)
                        dve.wait_ge(h_done, st["h0"] + i)
                        add_halves(st, T1, u0 + 2 * i, pairs[0]).then_inc(acc_read, 1)
                        ahead(g0 + 2 * i + 1, slots[1])
                        dve.wait_ge(chunk_done, g0 + 2 * i + 2)
                        add_halves(st, T2, u0 + 2 * i + 1, pairs[1]).then_inc(acc_read, 1)
                        dve.wait_ge(acc_read, u0 + 2 * i + 2)
                        dve.wait_ge(silu_out, silu0(st) + i + 1)
                        V.tensor_tensor(U[:, bass.ds(H0 + i * 512, 512)], T3, T2,
                                        ALU.mult).then_inc(h_done, 1)
                    repeat(dve, n // 2, body)
                elif kind == "natural":
                    ncols = st["ncols"]
                    for b in range(st["blocks"]):
                        for c in range(2):
                            ahead(g0 + 2 * b + c, slots[c])
                        dve.wait_ge(chunk_done, g0 + 2 * b + 2)
                        p = (u0 + b) % 2
                        at = dest_at[st["dest"]] + b * 1024
                        V.tensor_copy(region(at, 2 * ncols).rearrange("p (t n) -> p t n", t=2),
                                      PS[:, 2 * p:2 * p + 2, 0:ncols]).then_inc(acc_read, 1)
                elif kind == "dilated_in":
                    dve.wait_ge(consts_in, 16)
                    cosd, sind = const("cosd"), const("sind")

                    def wide(table, t, lo, hi):
                        return table[:, t * 64 + lo:t * 64 + hi].unsqueeze(1).to_broadcast([P, 8, hi - lo])

                    def body(i):
                        for b in range(6):
                            for c in range(2):
                                ahead(g0 + 12 * i + 2 * b + c, slots[c])
                            dve.wait_ge(chunk_done, g0 + 12 * i + 2 * b + 2)
                            p = (u0 + b) % 2
                            if b >= 4:
                                at = i * DIL_SIZE + (DIL0 + 4096 + (b - 4) * 1024)
                                V.tensor_copy(U[:, bass.ds(at, 1024)],
                                              PS[:, 2 * p:2 * p + 2, :].rearrange("p b n -> p (b n)")
                                              ).then_inc(acc_read, 1)
                                continue
                            if b:
                                dve.wait_ge(rope_sum, 4 * i + b)
                            for t in range(TT):
                                x = PS[:, 2 * p + t, :].rearrange("p (h d) -> p h d", h=8)
                                m1 = rope_m1[:, t * 512:(t + 1) * 512].rearrange("p (h d) -> p h d", h=8)
                                m2 = rope_m2[:, t * 512:(t + 1) * 512].rearrange("p (h d) -> p h d", h=8)
                                V.tensor_tensor(m1, x, wide(cosd, t, 0, 64), ALU.mult)
                                V.tensor_tensor(m2[:, :, 0:32], x[:, :, 32:64],
                                                wide(sind, t, 0, 32), ALU.mult)
                                last = V.tensor_tensor(m2[:, :, 32:64], x[:, :, 0:32],
                                                       wide(sind, t, 32, 64), ALU.mult)
                            last.then_inc(acc_read, 1)
                    repeat(dve, DIL_G, body)
                elif kind == "conv":
                    for c in range(4):
                        for part in range(3):
                            j = 3 * c + part
                            ahead(g0 + j, (g0 + j) % 2)
                            if part == 0 and c >= 2:
                                dve.wait_ge(conv_done, c - 1)
                            if part and c:
                                dve.wait_ge(conv_cu_done, c)
                            dst = (conv_b[:, c % 2, :], T1, T2)[part]
                            add_halves(st, dst, u0 + j, (u0 + j) % 2).then_inc(acc_read, 1)
                elif kind == "down":
                    def body(i):
                        for s in range(2):
                            ahead(g0 + 2 * i + s, slots[s])
                    repeat(dve, n // 2, body)
                    if n % 2:
                        ahead(g0 + n - 1, (g0 + n - 1) % 2)
                    for t in range(TT):
                        if t == 0:
                            dve.wait_ge(tile_done, st["down"] + 1)
                        else:
                            dve.wait_ge(chunk_done, g0 + n)
                        y = PS[:, 4 + 2 * t:6 + 2 * t, :].rearrange("p b n -> p (b n)")
                        if st["after"] == "x":
                            V.scalar_tensor_tensor(X[:, t, :], y, st["scale"], X[:, t, :],
                                                   ALU.mult, ALU.add).then_inc(x_new, 1)
                        elif st["after"] == "q":
                            V.tensor_copy(region(R["mla_qn"] + t * 768, 768),
                                          y[:, 0:768]).then_inc(x_new, 1)
                        else:
                            yh = y.rearrange("p (h d) -> p h d", h=8)
                            kn = region(R["mla_kn"] + t * 768, 768).rearrange("p (h d) -> p h d", h=8)
                            V.tensor_copy(kn[:, :, 0:64], yh[:, :, 0:64])
                            V.tensor_copy(region(R["mla_v"] + t * 512, 512)
                                          .rearrange("p (h d) -> p h d", h=8),
                                          yh[:, :, 64:128]).then_inc(x_new, 1)
                    if st["after"] == "q":
                        dve.wait_ge(x_new, st["x0"] + 2)
                        for t in range(TT):
                            q = region(R["mla_qn"] + t * 768, 768).rearrange("p (h d) -> p h d", h=8)
                            rope32(q[:, :, 64:96], q[:, :, 64:96], t, 8, t == TT - 1)
                    if st["after"] == "kv":
                        for t in range(TT):
                            kn = region(R["mla_kn"] + t * 768, 768).rearrange("p (h d) -> p h d", h=8)
                            last = V.tensor_copy(kn[:, :, 64:96], KPE[:, t * 32:(t + 1) * 32]
                                                 .unsqueeze(1).to_broadcast([P, 8, 32]))
                        last.then_inc(mla_p, 1)
                elif kind == "mla_turn":
                    dve.wait_ge(mla_t, 1)
                    for b in range(3):
                        col = GAINS["q_norm"] + b if b < 2 else GAINS["ckv_norm"]
                        V.tensor_scalar(region(R["c"] + b * S, S), PS[:, 4 + b // 2, (b % 2) * S:(b % 2 + 1) * S],
                                        G[:, col:col + 1], None, ALU.mult).then_inc(h_done, 1)
                elif kind == "mla_k":
                    for b in range(2):
                        dve.wait_ge(mla_t, 2 + b)
                        V.tensor_copy(region(R["mla_kT"] + b * 1024, 1024)[0:96, :],
                                      PS[0:96, 2 * pairs[b]:2 * pairs[b] + 2, :]
                                      .rearrange("p b n -> p (b n)")).then_inc(acc_read, 1)
                elif kind == "forget":
                    ahead(g0, slots[0])
                    dve.wait_ge(chunk_done, g0 + 1)
                    p = pairs[0]
                    for t in range(TT):
                        last = V.tensor_tensor(T1[:, t * 8:t * 8 + 8], PS[:, 2 * p + t, 0:8],
                                               G[:, GAINS["b_f"]:GAINS["b_f"] + 8], ALU.add)
                    last.then_inc(acc_read, 1)
                    dve.wait_ge(acc_read, u0 + 1)
                    link(V.tensor_scalar(T1[:, 16:32], T1[:, 0:16], -1.0, None, ALU.mult))
                    V.tensor_tensor(T1[:, 16:32], T1[:, 0:16], T1[:, 16:32], ALU.max).then_inc(f_v, 1)
                    link(V.tensor_scalar(T1[:, 64:80], T1[:, 0:16], 0.0, None, ALU.min))
                elif kind == "sums":
                    dve.wait_ge(f_a, 2)
                    V.tensor_tensor(T1[:, 80:96], T1[:, 64:80], T1[:, 48:64],
                                    ALU.subtract).then_inc(f_v, 1)
                    dve.wait_ge(f_t, 1)
                    V.tensor_copy(ST[:, 32:48], PS[:, 2 * pairs[0], 0:16]).then_inc(acc_read, 1)
                    link(V.tensor_copy(region(RB["ck"], 2048),
                                       PS[:, 4:8, :].rearrange("p b n -> p (b n)")))
                elif kind == "attend":
                    a0, m = st["a0"], len(st["what"])

                    def soft(n):
                        e = heads[n]
                        dve.wait_ge(s_score, n + 1)
                        if n >= 3:
                            back = heads[n - 3]
                            dve.wait_ge(s_pt, back["group0"] + back["parts"])
                        w_ = e["w"]
                        sc = e["scores"].rearrange("p (t n) -> p t n", t=2)
                        pr = e["probs"].rearrange("p (t n) -> p t n", t=2)
                        if e["bias"] is None:
                            link(V.tensor_reduce(e["mx"], sc, AXIS.X, ALU.max, negate=True))
                            V.tensor_scalar(e["mx"], e["mx"], e["scale"], None,
                                            ALU.mult).then_inc(s_soft, 1)
                            return
                        if e["bias"] == "dil":
                            V.scalar_tensor_tensor(e["probs"], e["scores"], e["scale"],
                                                   const("dil"), ALU.mult, ALU.add
                                                   ).then_inc(s_read, 1)
                        elif e["bias"] == "na":
                            if n == a0:
                                dve.wait_ge(bias_ready, 1)
                            for t in range(TT):
                                at = R["na_bias"] + e["h"] * SLOTS * GRID + (2 - 2 * t) * GRID
                                last = V.scalar_tensor_tensor(pr[:, t, :], sc[:, t, :], e["scale"],
                                                              region(at, S), ALU.mult, ALU.add)
                            last.then_inc(s_read, 1)
                        else:
                            ck = region(RB["ck"] + e["h"] * S, S)
                            for t in range(TT):
                                last = V.scalar_tensor_tensor(pr[:, t, :], sc[:, t, :], e["scale"], ck,
                                                              ALU.mult, ALU.subtract)
                            last.then_inc(s_read, 1)
                            dve.wait_ge(s_read, e["read"] + 1)
                            for t in range(TT):
                                col = 32 + t * 8 + e["h"]
                                last = V.scalar_tensor_tensor(
                                    pr[:, t, :], pr[:, t, :], ST[:, col:col + 1],
                                    const("causal")[:, t * S:(t + 1) * S], ALU.add, ALU.add)
                            link(last)
                        dve.wait_ge(s_read, e["read"] + 1)
                        V.tensor_reduce(e["mx"], pr, AXIS.X, ALU.max, negate=True).then_inc(s_soft, 1)

                    def normalise(n):
                        e = heads[n]
                        w_ = e["w"]
                        dve.wait_ge(s_exp, 2 * n + 2)
                        link(V.reciprocal(e["rz"], e["z"]))
                        for t in range(TT):
                            pr = e["probs"][:, t * w_:(t + 1) * w_]
                            last = V.tensor_scalar(pr, pr, e["rz"][:, t:t + 1], None, ALU.mult)
                        last.then_inc(s_norm, 1)

                    def output(n):
                        e = heads[n]
                        dve.wait_ge(s_pv, n + 1)
                        d = e["y"].shape[0]
                        y, o = e["y"], PS[e["pb"]:e["pb"] + d, 6 + n % 2, 0:S]
                        if e["bias"] == "dil":
                            y = y.rearrange("p (j r) -> p r j", r=RES)
                            o = o.rearrange("p (r j) -> p r j", r=RES)
                        V.tensor_copy(y, o).then_inc(h_done, 1)

                    soft(a0)
                    soft(a0 + 1)
                    normalise(a0)
                    soft(a0 + 2)
                    for n_ in range(a0, a0 + m):
                        if n_ + 1 < a0 + m:
                            normalise(n_ + 1)
                        if n_ > a0:
                            output(n_ - 1)
                        if n_ + 3 < a0 + m:
                            soft(n_ + 3)
                    output(a0 + m - 1)

        @block.gpsimd
        def _(pool):
            chain = Count(pool_chain)
            nc.gpsimd.memset(W_raw[:, :, 4 * 416:], 0.0).then_inc(raw_tail, 1)
            chain.inc(nc.gpsimd.memset(ST[:, 62:64], -0.5))
            gains = (a["norm_final"], a["final_norm_2"])
            wide = lambda v: v.rearrange("(o n) -> o n", o=1).to_broadcast([P, D])

            def rstd(cols, width, done):
                chain.inc(nc.gpsimd.tensor_scalar(cols, cols, 1.0 / width, EPS, ALU.mult, ALU.add))
                pool.wait_ge(pool_chain, chain.value())
                nc.gpsimd.tensor_tensor(cols, cols, ST[:, 62:62 + cols.shape[1]], ALU.pow).then_inc(done, 1)

            pool.wait_ge(x_in[1], 16)
            pool.dma_start(MEM, a["mem_2"][0].rearrange("(t p) n -> p t n", p=P)).then_inc(mem_in, 16)
            for st in stages:
                g0, n, kind = st["g"], st["n"], st["kind"]
                if kind in ("norm", "final", "mem_scale") and not st.get("again"):
                    for t in range(TT):
                        pool.wait_ge(n_sq, 2 * i_norm(st) + t + 1)
                        rstd(ST[:, t:t + 1], D, n_rstd)
                if kind == "mla_in":
                    pool.wait_ge(mla_a, 1)
                    rstd(ST[:, 4:6], 256, mla_r)
                    rstd(ST[:, 6:8], 128, mla_r)
                if st["name"] == "na_v":
                    bias = region(R["na_bias"], NA_H * SLOTS * GRID)
                    pool.dma_start(bias, a["na_bias"]).then_inc(bias_in, 16)
                    pool.dma_start(K[:, FIRST:], a["const"][:, FIRST:]).then_inc(consts_in, 16)
                    pool.wait_ge(first_in, 32)
                    pool.wait_ge(bias_in, 16)
                    rows = NA_H * SLOTS
                    view = bias.rearrange("p (r n) -> p r n", r=rows)
                    window = const("window").unsqueeze(1).to_broadcast([P, rows, GRID])
                    nc.gpsimd.tensor_tensor(view, view, window, ALU.add).then_inc(bias_ready, 1)
                if kind == "down":
                    def body(i, js=(0, 1)):
                        for s in js:
                            j, slot = 2 * i + s, (g0 + s) % 2
                            pool.wait_ge(st_hi, staged0(st) + j + 1)
                            nc.gpsimd.tensor_tensor(SX[:, slot, 1, 0:st["ks"] * S], down_src(st, j),
                                                    SX[:, slot, 0, 0:st["ks"] * S],
                                                    ALU.subtract).then_inc(st_lo, 1)
                    repeat(pool, n // 2, body)
                    if n % 2:
                        body(n // 2, (0,))
                    if st["name"] in ("od_o", "b_out"):
                        pool.wait_ge(x_new, st["x0"] + 2)
                        pool.dma_start(GF, wide(gains[st["name"] == "b_out"])).then_inc(gain_in, 16)
                elif kind == "conv":
                    Pg = nc.gpsimd
                    T2v = [t.rearrange("p (f t) -> p f t", f=2) for t in (T1, T2)]

                    def step(ins):
                        chain.inc(ins)
                        pool.wait_ge(pool_chain, chain.value())

                    step(Pg.memset(conv_cu[:, :, 0:2], 0.0))
                    for c in range(4):
                        pool.wait_ge(acc_read, st["u"] + 3 * c + 3)
                        Pg.tensor_tensor(conv_cu[:, :, 2:S + 2], T2v[0], T2v[1],
                                         ALU.mult).then_inc(conv_cu_done, 1)
                        pool.wait_ge(conv_cu_done, c + 1)
                        for tap in (2, 1, 0):
                            dst = conv_acc if tap == 2 else conv_tap
                            for f in range(2):
                                col = GAINS["conv"] + tap * KD + 2 * c + f
                                last = Pg.tensor_scalar(dst[:, f, :], conv_cu[:, f, tap:tap + S],
                                                        G[:, col:col + 1], None, ALU.mult)
                            step(last)
                            if tap != 2:
                                step(Pg.tensor_tensor(conv_acc, conv_acc, conv_tap, ALU.add))
                        Pg.tensor_tensor(region(H0 + c * 512, 512),
                                         conv_acc.rearrange("p f t -> p (f t)"),
                                         conv_b[:, c % 2, :], ALU.mult).then_inc(conv_done, 1)
                        pool.wait_ge(conv_done, c + 1)
                elif kind == "dilated_in":
                    def body(i):
                        for b in range(4):
                            pool.wait_ge(acc_read, u_of(st) + 6 * i + b + 1)
                            if b >= 2:
                                pool.wait_ge(rope_tr, 4 * i + b - 1)
                            nc.gpsimd.tensor_tensor(rope_out[:, b % 2, :], rope_m1, rope_m2,
                                                    ALU.add).then_inc(rope_sum, 1)
                    repeat(pool, DIL_G, body)


def _constants():
    p, k = np.arange(P), np.arange(S)
    tokens = np.arange(S).reshape(TT, P)
    out = np.zeros((P, NCONST), np.float32)

    def put(name, value):
        lo, hi = CONST[name]
        out[:, lo:hi] = np.asarray(value, np.float32).reshape(P, hi - lo)

    put("ident", np.eye(P))
    q = tokens.T[:, :, None]
    far = k[None, None, :] - q
    order = np.arange(S).reshape(-1, RES).T.reshape(-1)
    tiles = order.reshape(TT, P)
    far_all = order[None, None, :] - tiles.T[:, :, None]
    far_own = tiles[None, :, :] - tiles.T[:, :, None]
    put("dil", np.concatenate([np.where(ok, 0.0, NEG) for ok in
                               (np.abs(far_all) <= 64, far_own % 4 == 0, far_own % 16 == 0)], axis=2))
    put("causal", np.where(far <= 0, 0.0, NEG))
    c = p % GRID
    start = np.clip(c - 8, 0, GRID - 16)[:, None]
    col = np.arange(GRID)[None, :]
    put("window", np.where((col >= start) & (col < start + 16), 0.0, NEG))
    for name, dim in (("d", 64), ("m", 32)):
        inv = np.float32(1.0) / np.float32(10000.0) ** (np.arange(0, dim, 2, dtype=np.float32)
                                                        / np.float32(dim))
        pos = (order if name == "d" else np.arange(S)).astype(np.float32)
        ang = pos[:, None] * inv[None, :].astype(np.float32)
        cos, sin = np.cos(ang).astype(np.float32), np.sin(ang).astype(np.float32)
        cos = np.concatenate([cos, cos], 1).reshape(TT, P, dim).transpose(1, 0, 2)
        sin = np.concatenate([-sin, sin], 1).reshape(TT, P, dim).transpose(1, 0, 2)
        put("cos" + name, cos)
        put("sin" + name, sin)
    put("tri", (tokens.T[:, :, None] <= k[None, None, :]))
    return out


_WEIGHTS = ["x", "norm_final", "ev_w_in", "ev_w_uq", "ev_w_ukv", "ev_w_o", "od_w_in", "od_w_o",
            "mlp_w1", "mlp_w2", "mem_2", "ffn_w_gate_up_2", "ffn_w_down_2", "mem_w_kv_2",
            "a_w_in_2", "a_w_out_2", "w_kvf_2", "b_w_q_2", "b_w_out_2", "final_norm_2"]


def kernel(**inputs):
    import concourse.bacc as bacc
    from concourse.bass_utils import run_bass_kernel_spmd

    x = {k: np.asarray(v) for k, v in inputs.items()}
    cols = lambda v: v.reshape(-1, P).T
    gains = np.concatenate(
        [cols(x["norm_mix"][0]), cols(x["norm_mix"][1]), cols(x["norm_mlp"][0]),
         cols(x["norm_mlp"][1])]
        + [cols(x["ffn_norm_2"][l, i]) for l in range(2) for i in range(2)]
        + [cols(x["mix_norm_2"][0]), cols(x["mix_norm_2"][1]), cols(x["mem_norm_2"]),
           cols(x["kv_norm_2"]), cols(x["ev_q_norm"][0]), cols(x["ev_kv_norm"][0])]
        + [cols(x["a_conv_w_2"][0, j]) for j in range(3)]
        + [np.broadcast_to(x["b_f_2"], (P, 8))], axis=1)
    rel = np.clip(np.arange(GRID)[None, :] - np.arange(GRID)[:, None] + 15, 0, 30)
    rpb = x["ev_rpb"][0]
    na = [np.take(rpb[:, first:first + SLOTS], rel, axis=2).transpose(2, 0, 1, 3)
          for first in (5, 4)]
    arrays = {k: np.ascontiguousarray(x[k]) for k in _WEIGHTS}
    arrays["gains"] = np.ascontiguousarray(gains)
    arrays["na_bias"] = np.ascontiguousarray(np.concatenate(na, axis=0).reshape(P, -1))
    arrays["const"] = _constants()

    nc = bacc.Bacc("TRN2", target_bir_lowering=False, num_devices=1)
    handles = {k: nc.dram_tensor(f"in_{k}", v.shape, mybir.dt.from_np(v.dtype),
                                 kind="ExternalInput").ap() for k, v in arrays.items()}
    out = nc.dram_tensor("out_x", (1, S, D), F32, kind="ExternalOutput").ap()
    build_program(nc, handles, out)
    r = run_bass_kernel_spmd(nc, [{f"in_{k}": v for k, v in arrays.items()}], core_ids=[0])
    return r.results[0]["out_x"]
```

```python
from contextlib import ExitStack

import numpy as np

import concourse.bass as bass
from concourse import mybir

F32 = mybir.dt.float32
F32R = mybir.dt.float32r
ALU = mybir.AluOpType
ACT = mybir.ActivationFunctionType
AXIS = mybir.AxisListType

P = 128
S = 256
TT = S // P
D = 1024
KD = D // P
CH = 2048
TCOLS = CH // KD
EPS = 1e-6
NEG = -1e30
NA_H = 8
DIL_G, DIL_H = 3, 16
RES = 4
FF1, FF2 = 4096, 2816
GRID = 64
SLOTS = 6

CONST = {}
_at = 0
for _name, _n in (("ident", P), ("cosm", TT * 32), ("sinm", TT * 32), ("window", GRID),
                  ("dil", TT * 2 * S), ("causal", TT * S), ("cosd", TT * 64),
                  ("sind", TT * 64), ("tri", TT * S)):
    CONST[_name] = (_at, _at + _n)
    _at += _n
NCONST = _at
FIRST = CONST["window"][1]

GAINS = {}
_at = 0
for _name, _n in (("mix0", KD), ("mix1", KD), ("mlp0", KD), ("mlp1", KD), ("ffn00", KD),
                  ("ffn01", KD), ("ffn10", KD), ("ffn11", KD), ("bmix0", KD), ("bmix1", KD),
                  ("mem", KD), ("kv", KD), ("q_norm", 2), ("ckv_norm", 1), ("conv", 3 * KD),
                  ("b_f", 8)):
    GAINS[_name] = _at
    _at += _n
NGAIN = _at


class Count:

    def __init__(self, sem):
        self.sem, self.n, self.dyn = sem, 0, 0

    def inc(self, ins):
        self.n += 1
        ins.then_inc(self.sem, 1)

    def value(self):
        return self.dyn + self.n


def repeat(engine, n, body, counts=(), straight=False):
    if straight or n < 2:
        for i in range(n):
            body(i)
        return
    with engine.Fori(0, n) as i:
        start = [c.n for c, _ in counts]
        for c, per in counts:
            c.dyn = i * per
        body(i)
        for (c, per), was in zip(counts, start):
            assert c.n - was == per, (c.n, was, per)
            c.dyn, c.n = 0, was + per * n


class Plan:

    def __init__(self):
        self.stages, self.g, self.u, self.down = [], 0, 0, 0

    def add(self, kind, name, chunks=0, uses=0, **more):
        st = dict(kind=kind, name=name, g=self.g, u=self.u, n=chunks, down=self.down, **more)
        self.g += chunks
        self.u += uses
        self.down += kind == "down"
        self.stages.append(st)
        return st


def make_plan(w):
    p = Plan()

    def norm(gain, fill=None, again=False, by_residue=False):
        fill = fill and dict(zip(("what", "l", "c"), fill))
        p.add("norm", "norm_" + gain, *((1, 1) if fill else ()), gain=GAINS[gain], again=again,
              by_residue=by_residue,
              fill=fill, w=fill and w["mem_w_kv"][fill["l"]])

    def up(name, weight, col, chunks, **more):
        p.add("up", name, chunks, chunks, w=weight, col=col, **more)

    def natural(name, weight, col, blocks, ncols=512, **more):
        p.add("natural", name, 2 * blocks, blocks, w=weight, col=col, blocks=blocks,
              ncols=ncols, **more)

    def down(name, weight, rows, scale=1.0, ncols=D, ks=2, after="x", src="h", **more):
        p.add("down", name, rows // (ks * P), 0, w=weight, scale=scale, ncols=ncols, ks=ks,
              after=after, src=src, **more)

    norm("mix0")
    natural("latent", w["ev_w_in"], 1536, 1, ncols=416, dest="latent")
    p.add("mem_scale", "mem_scale")
    p.add("mla_in", "mla_in")
    up("na_qk", w["ev_w_in"], 0, 1, post="copy", dest="na_qk", latents=True)
    up("na_qk", w["ev_w_in"], 256, 1, post="copy", dest="na_qk", at=512)
    p.add("mla_turn", "mla_turn")
    p.add("mem_turn", "mem_turn", gain=GAINS["mem"])
    up("na_qk", w["ev_w_in"], 512, 1, post="copy", dest="na_qk", at=1024, memory=True)
    down("ukv", w["ev_w_ukv"], 128, ks=1, after="kv", src="c")
    up("na_qk", w["ev_w_in"], 768, 1, post="copy", dest="na_qk", at=1536)
    p.add("mla_k", "mla_k", 0, 2)
    down("uq", w["ev_w_uq"], 256, ncols=768, after="q", src="c")
    natural("na_v", w["ev_w_in"], 1024, 1, dest="na_v")
    p.add("attend", "even", what=[("na", h) for h in range(8)] + [("mla", h) for h in range(8)])
    down("ev_o", w["ev_w_o"], 1024)
    norm("mlp0")
    up("mlp_up", w["mlp_w1"][0], 0, FF1 // TCOLS, post="relu2", dest="h")
    down("mlp_down", w["mlp_w2"][0], FF1)
    norm("mix1", by_residue=True)
    p.add("dilated_in", "dilated_in", DIL_G * 12, DIL_G * 6, w=w["od_w_in"])
    p.add("attend", "dilated", what=[("dil", h) for h in range(DIL_H)])
    down("od_o", w["od_w_o"], 1024)
    norm("mlp1", ("k", 0, 0))
    up("mlp_up", w["mlp_w1"][1], 0, FF1 // TCOLS, post="relu2", dest="h")
    down("mlp_down", w["mlp_w2"][1], FF1)
    p.add("final", "norm_final", 1, 1, out=False, fill=dict(what="v", l=0, c=0),
          w=w["mem_w_kv"][0])
    for l in range(2):
        if l == 1:
            norm("kv", ("k", 1, 1))
            up("fox_k", w["w_kvf"], 0, 4, post="copy", dest="fox_k")
            natural("fox_v", w["w_kvf"], 1024, 2, dest="fox_v")
            p.add("forget", "forget", 1, 1, w=w["w_kvf"], col=2048)
        norm(f"ffn{l}0", ("k", 0, 1) if l == 0 else ("v", 1, 0), again=l == 1)
        if l == 1:
            p.add("sums", "sums", 0, 1)
        p.add("glu", "glu", 2 * FF2 // TCOLS, 2 * FF2 // TCOLS, w=w["ffn_gu"][l][0])
        down("ffn_down", w["ffn_down"][l][0], FF2, scale=0.5)
        norm(f"bmix{l}", ("v", l, 1))
        if l == 0:
            p.add("conv", "conv", 12, 12, w=w["a_w_in"])
            up("mem_q", w["a_w_in"], 3072, 2, post="copy", dest="mem_q0")
            p.add("attend", "memory0", what=[("mem0", h) for h in range(4)])
            down("a_out", w["a_w_out"], 1536)
        else:
            up("fox_q", w["b_w_q"], 0, 4, post="copy", dest="fox_q")
            up("mem_q", w["b_w_q"], 1024, 2, post="copy", dest="mem_q1")
            p.add("attend", "fox",
                  what=[e for h in range(4) for e in (("fox", 2 * h), ("fox", 2 * h + 1), ("mem1", h))])
            down("b_out", w["b_w_out"], 1536)
        norm(f"ffn{l}1", ("k", 1, 0) if l == 0 else None)
        p.add("glu", "glu", 2 * FF2 // TCOLS, 2 * FF2 // TCOLS, w=w["ffn_gu"][l][1])
        down("ffn_down", w["ffn_down"][l][1], FF2, scale=0.5)
    p.add("final", "final_norm", out=True, fill=None)
    return p


def build_program(nc, a, out):
    blocked = lambda m: m.rearrange("(k p) n -> p k n", p=P)
    w = {
        "ev_w_in": blocked(a["ev_w_in"][0]), "ev_w_uq": blocked(a["ev_w_uq"][0]),
        "ev_w_ukv": blocked(a["ev_w_ukv"][0]), "ev_w_o": blocked(a["ev_w_o"][0]),
        "od_w_in": blocked(a["od_w_in"][0]), "od_w_o": blocked(a["od_w_o"][0]),
        "mlp_w1": [blocked(a["mlp_w1"][l]) for l in range(2)],
        "mlp_w2": [blocked(a["mlp_w2"][l]) for l in range(2)],
        "ffn_gu": [[blocked(a["ffn_w_gate_up_2"][l, i]) for i in range(2)] for l in range(2)],
        "ffn_down": [[blocked(a["ffn_w_down_2"][l, i]) for i in range(2)] for l in range(2)],
        "mem_w_kv": [blocked(a["mem_w_kv_2"][l]) for l in range(2)],
        "a_w_in": blocked(a["a_w_in_2"][0]), "a_w_out": blocked(a["a_w_out_2"][0]),
        "w_kvf": blocked(a["w_kvf_2"]), "b_w_q": blocked(a["b_w_q_2"][0]),
        "b_w_out": blocked(a["b_w_out_2"][0]),
    }
    plan = make_plan(w)
    stages, G_TOTAL = plan.stages, plan.g

    ctx = ExitStack()
    with ctx:
        def sb(name, shape, dt=F32):
            return ctx.enter_context(nc.sbuf_tensor(name, shape, dt))

        def sem(name):
            return ctx.enter_context(nc.semaphore(name))

        W_raw = sb("W_raw", [P, 2, CH])
        W_hi = sb("W_hi", [P, 2, CH], F32R)
        W_lo = sb("W_lo", [P, 2, CH], F32R)
        XM = sb("XM", [P, KD, 2, S], F32R)
        XN = sb("XN", [P, KD, 2, S], F32R)
        SX = sb("SX", [P, 2, 2, 2 * S], F32R)
        X = sb("X", [P, TT, D])
        K = sb("K", [P, NCONST])
        G = sb("G", [P, NGAIN])
        T = sb("T", [P, 2048])
        T0 = T[:, 0:1024].rearrange("p (u n) -> p u n", u=2)
        T1, T2 = T[:, 1024:1536], T[:, 1536:2048]
        ST = sb("ST", [P, 64])
        U = sb("U", [P, 23040])
        PS = ctx.enter_context(nc.psum_tensor("PS", [P, 8, 512], F32))

        const = lambda name: K[:, CONST[name][0]:CONST[name][1]]
        ident = const("ident")

        def region(at, n):
            return U[:, at:at + n]

        H0 = 0
        XS = region(0, 2 * D).rearrange("p (t n) -> p t n", t=TT)
        R = dict(na_qk=2048, na_v=4096, mla_qn=5120, mla_kn=6656, latent=8192, lat_s=9024,
                 c=9792, mla_v=10560, mla_qT=11584, mla_kT=13632, na_bias=15680,
                 sm=18752, pt=19776, mem=20800, kpe=22848)
        MEM = region(R["mem"], 2 * D).rearrange("p (t n) -> p t n", t=TT)
        KPE = region(R["kpe"], TT * 32)
        DIL0, DIL_SIZE = H0, 6144
        RD = dict(sm=DIL0 + DIL_G * DIL_SIZE, pt=DIL0 + DIL_G * DIL_SIZE + 2048)
        rope_m1 = region(RD["sm"], 1024)
        rope_m2 = region(RD["sm"] + 1024, 1024)
        rope_out = region(RD["sm"] + 2048, 2048).rearrange("p (b n) -> p b n", b=2)
        RB = dict(mem_k0=8192, mem_k1=9216, mem_v0=10240, mem_v1=11264, fox_k=12288,
                  fox_v=14336, fox_q=16384, ck=18432, sm=20992, pt=22016)
        RB["mem_q0"], RB["mem_q1"] = RB["fox_q"], RB["mem_k0"]
        T3 = region(RB["sm"], 512)
        GF = region(RB["pt"], D)
        conv_b = region(RB["fox_k"], 1024).rearrange("p (c n) -> p c n", c=2)
        conv_cu = region(RB["fox_k"] + 1024, 2 * (S + 2)).rearrange("p (f t) -> p f t", f=2)
        conv_acc = region(RB["fox_k"] + 1664, 512).rearrange("p (f t) -> p f t", f=2)
        conv_tap = region(RB["fox_k"] + 2176, 512).rearrange("p (f t) -> p f t", f=2)
        dest_at = dict(R, **{k: RB[k] for k in RB if k not in ("sm", "pt")}, h=H0)

        first_in = sem("first_in")
        consts_in = sem("consts_in")
        gain_in = sem("gain_in")
        x_in = [sem("x_in0"), sem("x_in1")]
        mem_in = sem("mem_in")
        warm = sem("warm")
        raw_tail = sem("raw_tail")
        raw_full = [sem("raw_full0"), sem("raw_full1")]
        w_hi = sem("w_hi")
        w_lo = sem("w_lo")
        chunk_done = sem("chunk_done")
        tile_done = sem("tile_done")
        acc_read = sem("acc_read")
        cross_out = sem("cross_out")
        h_done = sem("h_done")
        st_hi, st_lo = sem("st_hi"), sem("st_lo")
        x_new = sem("x_new")
        n_sq = sem("n_sq")
        n_rstd = sem("n_rstd")
        n_scaled = sem("n_scaled")
        n_tr = sem("n_tr")
        n_hi = sem("n_hi")
        n_lo = sem("n_lo")
        silu_out = sem("silu_out")
        rope_sum = sem("rope_sum")
        rope_tr = sem("rope_tr")
        rope_kept = sem("rope_kept")
        mla_a = sem("mla_a")
        mla_r = sem("mla_r")
        mla_p = sem("mla_p")
        mla_t = sem("mla_t")
        xm_done = sem("xm_done")
        f_v, f_a = sem("f_v"), sem("f_a")
        f_t = sem("f_t")
        s_score = sem("s_score")
        s_read = sem("s_read")
        s_soft = sem("s_soft")
        s_exp = sem("s_exp")
        s_norm = sem("s_norm")
        s_pt = sem("s_pt")
        s_pte = sem("s_pte")
        s_pv = sem("s_pv")
        conv_cu_done = sem("conv_cu_done")
        conv_done = sem("conv_done")
        bias_in = sem("bias_in")
        bias_ready = sem("bias_ready")
        dve_chain, pool_chain = sem("dve_chain"), sem("pool_chain")
        out_done = sem("out_done")

        def head(what, h):
            if what == "na":
                pb = 64 * (h % 2)
                q = region(R["na_qk"] + (h // 2) * S, S)[pb:pb + 64, :]
                k = region(R["na_qk"] + (4 + h // 2) * S, S)[pb:pb + 64, :]
                v = lambda g, kt: region(R["na_v"] + kt * 512 + h * 64, 64)
                y = region(H0 + (h // 2) * S, S)[pb:pb + 64, :]
                return dict(G=1, q=[q], k=[k], v=v, y=y, pb=pb, scale=64 ** -0.5, bias="na", R=R, h=h)
            if what == "mla":
                pb = 64 * (h % 2)
                q = region(R["mla_qT"] + h * S, S)[0:96, :]
                k = region(R["mla_kT"] + h * S, S)[0:96, :]
                v = lambda g, kt: region(R["mla_v"] + kt * 512 + h * 64, 64)
                y = region(H0 + (4 + h // 2) * S, S)[pb:pb + 64, :]
                return dict(G=1, q=[q], k=[k], v=v, y=y, pb=pb, scale=96 ** -0.5, bias=None, R=R, h=h)
            if what == "dil":
                pb, blk, pair = 64 * (h % 2), h // 8, h // 2
                q = [region(DIL0 + g * DIL_SIZE + pair * S, S)[pb:pb + 64, :] for g in range(3)]
                k = [region(DIL0 + g * DIL_SIZE + 2048 + pair * S, S)[pb:pb + 64, :] for g in range(3)]
                v = lambda g, kt: region(DIL0 + g * DIL_SIZE + 4096 + blk * 1024 + kt * 512
                                         + (h % 8) * 64, 64)
                y = region(H0 + pair * S, S)[pb:pb + 64, :]
                return dict(G=3, q=q, k=k, v=v, y=y, pb=pb, scale=64 ** -0.5, bias="dil", R=RD, h=h)
            if what == "fox":
                q = region(RB["fox_q"] + h * S, S)
                k = region(RB["fox_k"] + h * S, S)
                v = lambda g, kt: region(RB["fox_v"] + (h // 4) * 1024 + kt * 512 + (h % 4) * P, P)
                y = region(H0 + h * S, S)
                return dict(G=1, q=[q], k=[k], v=v, y=y, pb=0, scale=P ** -0.5, bias="fox", R=RB, h=h)
            l = int(what[3])
            q = region(RB[f"mem_q{l}"] + h * S, S)
            k = region(RB[f"mem_k{l}"] + h * S, S)
            v = lambda g, kt: region(RB[f"mem_v{l}"] + kt * 512 + h * P, P)
            y = region(H0 + (8 + h) * S, S)
            return dict(G=1, q=[q], k=[k], v=v, y=y, pb=0, scale=P ** -0.5, bias=None, R=RB, h=h)

        heads, n_groups = [], 0
        h_count = 0
        n_norm = n_final = 0
        for st in stages:
            st["h0"] = h_count
            if st["kind"] == "attend":
                st["a0"] = len(heads)
                for what, h in st["what"]:
                    e = head(what, h)
                    e["group0"] = n_groups
                    e["parts"] = 2 if e["G"] == 3 else 1
                    e["w"] = 2 * S if e["G"] == 3 else S
                    e["cols"] = ([slice(0, P), slice(P, P + S)] if what == "fox" else
                                 [slice(t * e["w"], (t + 1) * e["w"]) for t in range(TT)])
                    n_groups += e["parts"]
                    heads.append(e)
                h_count += len(st["what"])
            elif st["kind"] == "up" and st["dest"] == "h":
                h_count += st["n"]
            elif st["kind"] == "glu":
                h_count += st["n"] // 2
            elif st["kind"] == "mla_turn":
                h_count += 3
            elif st["kind"] in ("norm", "mem_scale"):
                st["i"] = n_norm - st.get("again", False)
                n_norm += not st.get("again")
            elif st["kind"] == "final":
                st["i"] = n_norm
                st["f"] = n_final
                n_norm += 1
                n_final += 1
        x_count = 0
        for st in stages:
            st["x0"] = x_count
            if st["kind"] in ("down", "final"):
                x_count += 4
        last_score, last_pt = {}, {}
        n_read = 0
        for n, e in enumerate(heads):
            e["score_banks"] = (4 + n % 2 * 2, 5 + n % 2 * 2) if e["G"] == 3 else (4 + n % 3,)
            e["score_prev"] = [last_score[b] for b in e["score_banks"] if b in last_score]
            for b in e["score_banks"]:
                last_score[b] = n
            e["pt_banks"] = [0, 1] if e["G"] == 3 else [n % 2]
            e["pt_prev"] = []
            for g, b in enumerate(e["pt_banks"]):
                e["pt_prev"].append(last_pt.get(b))
                last_pt[b] = e["group0"] + g + 1
            b = e["score_banks"]
            e["scores"] = PS[:, b[0]:b[-1] + 1, :].rearrange("p b n -> p (b n)")
            width = e["w"] * TT
            e["probs"] = (region(e["R"]["sm"] + (n % 3) * width, width) if n % 3 < 2
                          else T[:, 0:width] if e["G"] == 3 else T1)
            e["read"] = n_read
            n_read += bool(e["bias"])
            e["ptile"] = [region(e["R"]["pt"] + ((n % 2) * e["parts"] + g) * 512, 512)
                          for g in range(e["parts"])]
            e["mx"] = ST[:, 8 + 8 * (n % 3):10 + 8 * (n % 3)]
            e["z"] = ST[:, 10 + 8 * (n % 3):12 + 8 * (n % 3)]
            e["rz"] = ST[:, 12 + 8 * (n % 3):14 + 8 * (n % 3)]


        k_norm = k_turn = n_glu = n_staged = n_cross = 0
        for n, st in enumerate(stages):
            if st["kind"] in ("norm", "mem_turn"):
                st["turn"] = k_turn
                k_turn += 1
            if st["kind"] == "norm":
                st["k"] = k_norm
                k_norm += 1
            st["cross0"] = n_cross
            if st["kind"] in ("up", "glu", "conv") or (st.get("fill") or {}).get("what") == "k":
                n_cross += st["n"]
            if st["kind"] == "glu":
                st["silu0"] = n_glu
                n_glu += st["n"] // 2
            if st["kind"] == "down":
                st["staged0"] = n_staged
                n_staged += st["n"]
                before = stages[n - 1]
                before["next_down"] = st
                st["each"] = before["kind"] == "glu" or before.get("dest") == "h"
            if st["kind"] == "attend":
                stages[n - 1]["next_attend"] = st
        before_heads = lambda st: len(stages[stages.index(st) - 1]["what"])

        def e_out_done(n):
            for st in stages:
                if st["kind"] == "attend" and st["a0"] <= n < st["a0"] + len(st["what"]):
                    return st["h0"] + n - st["a0"] + 1

        def raw_count(g, slot):
            if isinstance(g, int):
                return 16 * (g // 2 + 1)
            return g * 8 + (16 if slot == 0 else 8)

        def down_src(st, j):
            if st["src"] == "c":
                at = R["c"] + (0 if st["name"] == "uq" else 2 * S)
                return region(at, st["ks"] * S)
            return U[:, bass.ds(H0 + j * 2 * S, 2 * S)]

        opened = lambda st: 3 if st["name"] in ("even", "fox") else 2

        tokens_in = lambda st, x: x.rearrange("p (j r) -> p r j", r=RES) if st.get("by_residue") else x
        tokens_out = lambda st, x: x.rearrange("p (r j) -> p r j", r=RES) if st.get("by_residue") else x

        halves = lambda h: slice(h * (CH // 2), (h + 1) * (CH // 2))
        block = ctx.enter_context(nc.Block())

        @block.sync
        def _(sp):
            for t in range(TT):
                sp.dma_start(X[:, t, :], a["x"][0, t * P:(t + 1) * P, :]).then_inc(x_in[t], 16)

            def load(g, slot, src, ks, n):
                if not isinstance(g, int) or g >= 2:
                    sp.wait_ge(w_lo, 2 * (g - 1))
                dst = W_raw[:, slot, 0:ks * n].rearrange("p (k n) -> p k n", k=ks)
                sp.dma_start(dst, src).then_inc(raw_full[slot], 16)

            for st in stages:
                g0, n, kind = st["g"], st["n"], st["kind"]
                w_ = st.get("w")
                slots = (g0 % 2, (g0 + 1) % 2)
                if kind == "up":
                    def body(i, ss=(0, 1)):
                        for s in ss:
                            load(g0 + 2 * i + s, slots[s],
                                 w_[:, :, bass.ds(st["col"] + (2 * i + s) * TCOLS, TCOLS)], KD, TCOLS)
                    repeat(sp, n // 2, body)
                    if n % 2:
                        body(n // 2, (0,))
                elif kind in ("norm", "final") and st["fill"]:
                    f = st["fill"]
                    col = (512 if f["what"] == "v" else 0) + f["c"] * TCOLS
                    load(g0, slots[0], w_[:, :, col:col + TCOLS], KD, TCOLS)
                elif kind == "glu":
                    def body(i):
                        for s in range(2):
                            load(g0 + 2 * i + s, slots[s],
                                 w_[:, :, bass.ds(s * FF2 + i * TCOLS, TCOLS)], KD, TCOLS)
                    repeat(sp, n // 2, body)
                elif kind == "natural":
                    for b in range(st["blocks"]):
                        for c in range(2):
                            col = st["col"] + b * 512
                            load(g0 + 2 * b + c, slots[c],
                                 w_[:, 4 * c:4 * c + 4, col:col + st["ncols"]], 4, st["ncols"])
                elif kind == "dilated_in":
                    def body(i):
                        for c in range(2):
                            load(g0 + 2 * i + c, slots[c],
                                 w_[:, 4 * c:4 * c + 4, bass.ds(i * 512, 512)], 4, 512)
                    repeat(sp, n // 2, body)
                elif kind == "conv":
                    for c in range(4):
                        for part in range(3):
                            col = part * D + c * TCOLS
                            load(g0 + 3 * c + part, (g0 + 3 * c + part) % 2,
                                 w_[:, :, col:col + TCOLS], KD, TCOLS)
                elif kind == "forget":
                    load(g0, slots[0], w_[:, :, st["col"]:st["col"] + 8], KD, 8)
                elif kind == "down":
                    ks = st["ks"]

                    def body(i):
                        for s in range(2):
                            load(g0 + 2 * i + s, slots[s],
                                 w_[:, bass.ds((2 * i + s) * ks, ks), :], ks, st["ncols"])
                    repeat(sp, n // 2, body)
                    if n % 2:
                        load(g0 + n - 1, (g0 + n - 1) % 2, w_[:, (n - 1) * ks:n * ks, :], ks,
                             st["ncols"])
            for t in range(TT):
                sp.wait_ge(x_new, x_count - 4 + 2 * (t + 1))
                sp.dma_start(out[0, t * P:(t + 1) * P, :], X[:, t, :]).then_inc(out_done, 16)
            sp.wait_ge(out_done, 16 * TT)

        @block.tensor
        def _(pe):
            mm, tr = nc.tensor.matmul, nc.tensor.transpose

            def chunk_ready(g):
                pe.wait_ge(w_lo, 2 * g + 2)

            def acc_free(u):
                if not isinstance(u, int) or u >= 2:
                    pe.wait_ge(acc_read, u - 1)

            def wT(tile, slot, k, fb):
                return tile[:, slot, k * TCOLS + fb * P:k * TCOLS + (fb + 1) * P]

            both_halves = lambda xn, k: xn[:, k, :, :].rearrange("p a t -> p (a t)")

            def up_chunk(g, u, slot, pair, xn=XN, first=True, between=None,
                         at=(1, 3)):
                chunk_ready(g)
                acc_free(u)
                if xn is XM:
                    pe.wait_ge(xm_done, 4)
                for fb in range(2):
                    bank = PS[:, 2 * pair + fb, :]
                    for k in range(KD):
                        if between and (fb, k) == at:
                            between()
                        if fb == 0 and first and xn is XN and k % 2 == 0:
                            pe.wait_ge(n_lo, xn_ready + k // 2 + 1)
                        both = both_halves(xn, k)
                        if k == 0:
                            mm(bank, wT(W_hi, slot, k, fb), both, start=True, stop=False)
                            mm(bank[:, S:], wT(W_lo, slot, k, fb), xn[:, k, 0, :],
                               start=False, stop=False)
                        else:
                            mm(bank[:, S:], wT(W_lo, slot, k, fb), xn[:, k, 0, :],
                               start=False, stop=False)
                            last = mm(bank, wT(W_hi, slot, k, fb), both, start=False,
                                      stop=k == KD - 1)
                last.then_inc(chunk_done, 1)

            def three(bank, xh, xl, wh, wl, start, stop):
                mm(bank, xh, wh, start=start, stop=False)
                mm(bank, xh, wl, start=False, stop=False)
                return mm(bank, xl, wh, start=False, stop=stop)

            def natural_chunk(g, slot, pair, c, ncols, between=None, at=0):
                chunk_ready(g)
                for t in range(TT):
                    if between and t == at:
                        between()
                    for ks in range(4):
                        k, n = 4 * c + ks, slice(ks * ncols, (ks + 1) * ncols)
                        if t == 0 and k % 2 == 0:
                            pe.wait_ge(n_lo, xn_ready + k // 2 + 1)
                        last = three(PS[:, 2 * pair + t, 0:ncols],
                                     XN[:, k, 0, t * P:(t + 1) * P], XN[:, k, 1, t * P:(t + 1) * P],
                                     W_hi[:, slot, n], W_lo[:, slot, n], k == 0, k == KD - 1)
                last.then_inc(chunk_done, 1)

            def fill_chunk(st, between=None):
                g, u = st["g"], st["u"]
                if st["fill"]["what"] == "k":
                    up_chunk(g, u, g % 2, u % 2, XM, between=between)
                    return
                chunk_ready(g)
                acc_free(u)
                pe.wait_ge(xm_done, 4)
                for t in range(TT):
                    for k in range(KD):
                        if between and (t, k) == (1, 3):
                            between()
                        n = slice(k * TCOLS, (k + 1) * TCOLS)
                        last = three(PS[:, 2 * (u % 2) + t, 0:TCOLS],
                                     XM[:, k, 0, t * P:(t + 1) * P], XM[:, k, 1, t * P:(t + 1) * P],
                                     W_hi[:, g % 2, n], W_lo[:, g % 2, n], k == 0, k == KD - 1)
                last.then_inc(chunk_done, 1)

            def down_chunk(st, g, staged, slot, first, final):
                chunk_ready(g)
                pe.wait_ge(st_lo, staged)
                ncols, ks_n = st["ncols"], st["ks"]
                for t in range(TT):
                    if first and t == 1 and st["src"] == "h" and not st["each"]:
                        pe.wait_ge(h_done, st["h0"])
                    steps = [(ks, b) for ks in range(ks_n) for b in range(2)]
                    for ks, b in sorted(steps, key=lambda x: x[1]) if final else steps:
                        x = slice(ks * S + t * P, ks * S + (t + 1) * P)
                        lo, hi = b * 512, min(ncols, b * 512 + 512)
                        n = slice(ks * ncols + lo, ks * ncols + hi)
                        last = three(PS[:, 4 + 2 * t + b, 0:hi - lo],
                                     SX[:, slot, 0, x], SX[:, slot, 1, x],
                                     W_hi[:, slot, n], W_lo[:, slot, n],
                                     first and ks == 0, final and ks == ks_n - 1)
                        if final and ks == ks_n - 1 and (t, b) != (1, 1):
                            last.then_inc(tile_done, 1)
                last.then_inc(chunk_done, 1)

            def turn_xs(bank, blocks):
                for b in blocks:
                    for k in (2 * b, 2 * b + 1):
                        for t in range(TT):
                            at = (k % 2) * S + t * P
                            last = tr(PS[:, bank + b, at:at + P], XS[:, t, k * P:(k + 1) * P], ident)
                    last.then_inc(n_tr, 1)

            def scores(n):
                e = heads[n]
                for prev in e["score_prev"]:
                    if heads[prev]["bias"]:
                        pe.wait_ge(s_read, heads[prev]["read"] + 1)
                    else:
                        pe.wait_ge(s_exp, 2 * prev + 2)
                for t in range(TT):
                    for g in range(e["G"]):
                        at = e["cols"][t].start + (S + (g - 1) * P if g else 0)
                        keys = (slice(t * P, (t + 1) * P) if g else
                                slice(0, min(S, e["cols"][t].stop - at)))
                        last = mm(e["scores"][:, at:at + keys.stop - keys.start],
                                  e["q"][g][:, t * P:(t + 1) * P], e["k"][g][:, keys],
                                  start=True, stop=True)
                last.then_inc(s_score, 1)

            def transposes(n):
                e = heads[n]
                pe.wait_ge(s_norm, n + 1)
                for part in range(e["parts"]):
                    if e["pt_prev"][part]:
                        pe.wait_ge(s_pte, e["pt_prev"][part])
                    for i in range(2):
                        for t in range(TT):
                            at = e["cols"][t].start + part * S + i * P
                            if at >= e["cols"][t].stop:
                                continue
                            last = tr(PS[:, e["pt_banks"][part],
                                         i * S + t * P:i * S + (t + 1) * P],
                                      e["probs"][:, at:at + P], ident)
                    last.then_inc(s_pt, 1)

            def values(n):
                e = heads[n]
                if n >= 2:
                    pe.wait_ge(h_done, e_out_done(n - 2))
                d = 64 if e["pb"] or e["bias"] in ("na", "dil") or e["scale"] == 96 ** -0.5 else P
                o = PS[e["pb"]:e["pb"] + d, 2 + n % 2, 0:S]
                pe.wait_ge(s_pte, e["group0"] + 1)
                for kt in range(TT):
                    skip = P if kt and e["bias"] == "fox" else 0
                    last = mm(o[:, skip:], e["v"](0, kt), e["ptile"][0][:, kt * S + skip:(kt + 1) * S],
                              start=kt == 0, stop=kt == TT - 1 and e["parts"] == 1)
                if e["parts"] == 2:
                    pe.wait_ge(s_pte, e["group0"] + 2)
                    for g in (1, 2):
                        for t in range(TT):
                            at = (g - 1) * S + t * P
                            last = mm(o[:, t * P:(t + 1) * P], e["v"](g, t),
                                      e["ptile"][1][:, at:at + P], start=False,
                                      stop=g == 2 and t == TT - 1)
                last.then_inc(s_pv, 1)

            def open_attention(st):
                pe.wait_ge(acc_read, st["u"] - 1)
                if st["name"] == "dilated":
                    pe.wait_ge(rope_kept, 4 * DIL_G)
                if st["name"] == "even":
                    pe.wait_ge(mla_a, 2)
                for n in range(opened(st)):
                    scores(st["a0"] + n)

            def turn_memory():
                pe.wait_ge(n_scaled, 4)
                pe.wait_ge(h_done, 3)
                turn_xs(4, range(4))

            def turn_heads(src, bank, hs):
                for h in hs:
                    for t in range(TT):
                        at = (h % 2) * S + t * P
                        last = tr(PS[0:96, bank + h // 2, at:at + P],
                                  region(src + t * 768 + h * 96, 96), ident)
                last.then_inc(mla_t, 1)

            pe.wait_ge(warm, 1)
            for _ in range(7):
                mm(PS[:, 0, :], T[:, 0:P], T[:, 0:512], start=True, stop=True)
            staged = 0
            pe.wait_ge(first_in, 32)
            for st in stages:
                g0, u0, n, kind = st["g"], st["u"], st["n"], st["kind"]
                slots, pairs = (g0 % 2, (g0 + 1) % 2), (u0 % 2, (u0 + 1) % 2)
                if kind == "sums":
                    pe.wait_ge(consts_in, 16)
                if kind == "norm":
                    i = st["i"]
                    def turn():
                        pe.wait_ge(n_scaled, 2 * st["i"] + 2)
                        turn_xs(4, range(4))
                    if st["fill"] and not st["again"]:
                        fill_chunk(st, turn)
                    else:
                        if st["x0"] and not st["fill"]:
                            acc_free(u0)
                            for _ in range(12):
                                mm(PS[:, 2 * pairs[0], :], XN[:, 0, 0, 0:P], both_halves(XN, 0),
                                   start=True, stop=True)
                        turn()
                        if st["fill"]:
                            fill_chunk(st)
                    xn_ready = 4 * st["k"]
                elif kind == "final" and st["fill"]:
                    fill_chunk(st)
                elif kind in ("up", "glu"):
                    def body(i, ss=(0, 1)):
                        for s in ss:
                            opens = s == 1 and st.get("next_attend")
                            between = opens and (lambda: open_attention(opens))
                            if st.get("memory"):
                                between = turn_memory
                            up_chunk(g0 + 2 * i + s, u0 + 2 * i + s, slots[s], pairs[s], first=s == 0,
                                     between=between, at=(0, 4))
                    repeat(pe, n // 2, body)
                    if n % 2:
                        body(n // 2, (0,))
                elif kind == "conv":
                    for c in range(n):
                        up_chunk(g0 + c, u0 + c, (g0 + c) % 2, (u0 + c) % 2, first=c == 0)
                elif kind == "natural":
                    for b in range(st["blocks"]):
                        acc_free(u0 + b)
                        for c in range(2):
                            if st["dest"] == "na_v" and c == 1:
                                pe.wait_ge(mla_p, 3)
                                turn_heads(R["mla_qn"], 4, range(8))
                            opens = c == 1 and st.get("next_attend")
                            natural_chunk(g0 + 2 * b + c, slots[c], (u0 + b) % 2, c, st["ncols"],
                                          opens and (lambda: open_attention(opens)), at=1)
                elif kind == "dilated_in":
                    def turn(i, b, q):
                        pe.wait_ge(rope_sum, 4 * i + b + 1)
                        if q >= 2:
                            pe.wait_ge(rope_kept, 4 * i + b - 1)
                        for pr in range(4):
                            for t in range(TT):
                                last = tr(PS[:, 4 + 2 * (b % 2) + pr // 2,
                                             (pr % 2) * S + t * P:(pr % 2) * S + (t + 1) * P],
                                          rope_out[:, b % 2, t * 512 + pr * P:t * 512 + (pr + 1) * P],
                                          ident)
                        last.then_inc(rope_tr, 1)

                    def body(i, opens=None):
                        for b in range(6):
                            acc_free(u0 + 6 * i + b)
                            for c in range(2):
                                natural_chunk(g0 + 12 * i + 2 * b + c, slots[c], (u0 + b) % 2, c, 512,
                                              opens and (b, c) == (5, 1)
                                              and (lambda: open_attention(opens)))
                            if 1 <= b <= 4:
                                turn(i, b - 1, b - 1)
                    repeat(pe, DIL_G - 1, body)
                    body(DIL_G - 1, st["next_attend"])
                elif kind == "forget":
                    chunk_ready(g0)
                    acc_free(u0)
                    for t in range(TT):
                        for k in range(KD):
                            f = slice(k * 8, k * 8 + 8)
                            last = three(PS[:, 2 * pairs[0] + t, 0:8], XN[:, k, 0, t * P:(t + 1) * P],
                                         XN[:, k, 1, t * P:(t + 1) * P], W_hi[:, slots[0], f],
                                         W_lo[:, slots[0], f], k == 0, k == KD - 1)
                    last.then_inc(chunk_done, 1)
                elif kind == "sums":
                    pe.wait_ge(f_v, 2)
                    acc_free(u0)
                    pe.wait_ge(n_lo, xn_ready + 4)
                    tri, ls = const("tri"), T1[:, 80:96]
                    for q in range(TT):
                        for t in range(TT):
                            mm(PS[:, 2 * pairs[0], q * 8:q * 8 + 8],
                               tri[:, t * S + q * P:t * S + (q + 1) * P],
                               ls[:, t * 8:t * 8 + 8], start=t == 0, stop=t == TT - 1)
                    for h in range(8):
                        for t in range(TT):
                            last = mm(PS[:, 4 + h // 2, (h % 2) * S:(h % 2 + 1) * S],
                                      ls[:, t * 8 + h:t * 8 + h + 1].to_broadcast([P, P]),
                                      tri[:, t * S:(t + 1) * S], start=t == 0, stop=t == TT - 1)
                    last.then_inc(f_t, 1)
                elif kind == "down":
                    for j in (0,) if n > 1 else ():
                        down_chunk(st, g0, staged + 1, g0 % 2, True, False)
                    if n == 1:
                        if st["name"] == "ukv":
                            pe.wait_ge(xm_done, 4)
                        if st["name"] == "uq":
                            pe.wait_ge(x_new, st["x0"])
                        down_chunk(st, g0, staged + 1, g0 % 2, True, True)
                    mid = max(n - 2, 0)

                    def body(i):
                        for s in range(2):
                            down_chunk(st, g0 + 1 + 2 * i + s, staged + 2 + 2 * i + s,
                                       (g0 + 1 + s) % 2, False, False)
                    repeat(pe, mid // 2, body)
                    for j in range(1 + mid // 2 * 2, n):
                        down_chunk(st, g0 + j, staged + j + 1, (g0 + j) % 2, False, j == n - 1)
                    staged += n
                elif kind == "mla_turn":
                    pe.wait_ge(mla_p, 1)
                    lat = region(R["lat_s"], 768)
                    for b in range(3):
                        for t in range(TT):
                            last = tr(PS[:, 4 + b // 2, (b % 2) * S + t * P:(b % 2) * S + (t + 1) * P],
                                      lat[:, t * 384 + b * P:t * 384 + (b + 1) * P], ident)
                    last.then_inc(mla_t, 1)
                elif kind == "mla_k":
                    pe.wait_ge(mla_p, 2)
                    for b in range(2):
                        acc_free(u0 + b)
                        turn_heads(R["mla_kn"], 2 * pairs[b] - 2 * b, range(4 * b, 4 * b + 4))
                elif kind == "attend":
                    a0, m = st["a0"], len(st["what"])

                    pe.wait_ge(acc_read, u0)
                    for n_ in range(opened(st), 3):
                        scores(a0 + n_)
                    for n_ in range(a0, a0 + m):
                        transposes(n_)
                        if n_ + 3 < a0 + m:
                            scores(n_ + 3)
                        values(n_)

        @block.scalar
        def _(act):
            A = nc.scalar.activation

            def split_hi(g, slot):
                if not isinstance(g, int) or g >= 2:
                    act.wait_ge(chunk_done, g - 1)
                act.wait_ge(raw_full[slot], raw_count(g, slot))
                for h in range(2):
                    A(W_hi[:, slot, halves(h)], W_raw[:, slot, halves(h)],
                      ACT.Copy).then_inc(w_hi, 1)

            def ahead(g, slot):
                if not isinstance(g, int) or g + 1 < G_TOTAL:
                    split_hi(g + 1, 1 - slot)

            def cross(g, u, pair):
                act.wait_ge(chunk_done, g + 1)
                if not isinstance(u, int) or u >= 2:
                    act.wait_ge(acc_read, u - 1)
                A(T0[:, pair, :].rearrange("p (f t) -> p f t", f=2),
                  PS[:, 2 * pair:2 * pair + 2, S:2 * S], ACT.Copy).then_inc(cross_out, 1)

            def square(st, t):
                if st["kind"] == "mem_scale":
                    act.wait_ge(mem_in, 16)
                elif st["x0"] == 0:
                    act.wait_ge(x_in[t], 16)
                src = MEM if st["kind"] == "mem_scale" else X
                for b in range(2):
                    n = slice(b * 512, b * 512 + 512)
                    if st["kind"] != "mem_scale" and st["x0"]:
                        act.wait_ge(x_new, st["x0"] - 3 + 2 * t + b)
                    if st["i"]:
                        act.wait_ge(n_scaled, 2 * st["i"])
                    A(XS[:, t, n], src[:, t, n], ACT.Square, scale=D ** -0.5,
                      accum_out=ST[:, 2 * t + b:2 * t + b + 1]).then_inc(n_sq, 1)

            def round_xs(st, dst, bank, blocks):
                for b in blocks:
                    act.wait_ge(n_tr, 4 * st["turn"] + b + 1)
                    for k in (2 * b, 2 * b + 1):
                        last = A(tokens_out(st, dst[:, k, 0, :]),
                                 tokens_in(st, PS[:, bank + b, (k % 2) * S:(k % 2 + 1) * S]),
                                 ACT.Copy, scale=G[:, st["gain"] + k:st["gain"] + k + 1])
                    last.then_inc(n_hi, 1)

            def stage_early(st):
                for j in range(min(2, st["n"])):
                    stage_hi(st, j, st["g"] + j, (st["g"] + j) % 2, True)

            def stage_hi(st, j, g, slot, early=False):
                if st["src"] == "c":
                    act.wait_ge(h_done, st["h0"])
                elif st["each"]:
                    act.wait_ge(h_done, st["h0"] - st["n"] + j + 1)
                elif early:
                    act.wait_ge(conv_done, 4) if st["name"] == "a_out" else act.wait_ge(
                        h_done, st["h0"] - before_heads(st) + 8)
                else:
                    act.wait_ge(h_done, st["h0"])
                if not early or st["src"] == "c":
                    act.wait_ge(chunk_done, g - 1)
                A(SX[:, slot, 0, 0:st["ks"] * S], down_src(st, j), ACT.Copy).then_inc(st_hi, 1)

            def exps(n):
                e = heads[n]
                act.wait_ge(s_soft, n + 1)
                for t in range(TT):
                    src = e["probs"] if e["bias"] else e["scores"]
                    A(e["probs"][:, e["cols"][t]], src[:, e["cols"][t]], ACT.Exp,
                      bias=e["mx"][:, t:t + 1], scale=1.0 if e["bias"] else e["scale"],
                      accum_out=e["z"][:, t:t + 1]).then_inc(s_exp, 1)

            def keep_pt(n):
                e = heads[n]
                for g in range(e["parts"]):
                    act.wait_ge(s_pt, e["group0"] + g + 1)
                    if n > 1:
                        act.wait_ge(s_pv, n - 1)
                    A(e["ptile"][g], PS[:, e["pt_banks"][g], :], ACT.Copy).then_inc(s_pte, 1)

            mem_scale = next(st for st in stages if st["kind"] == "mem_scale")
            act.dma_start(K[:, 0:FIRST], a["const"][:, 0:FIRST]).then_inc(first_in, 16)
            act.dma_start(G[:], a["gains"]).then_inc(first_in, 16)
            act.wait_ge(first_in, 32)
            for st in stages:
                g0, u0, n, kind = st["g"], st["u"], st["n"], st["kind"]
                slots, pairs = (g0 % 2, (g0 + 1) % 2), (u0 % 2, (u0 + 1) % 2)
                if kind in ("norm", "final"):
                    for t in () if st.get("again") else range(TT):
                        square(st, t)
                    if g0 == 0:
                        act.wait_ge(raw_tail, 1)
                        split_hi(0, 0)
                    if st.get("fill"):
                        ahead(g0, slots[0])
                    if kind == "norm":
                        act.wait_ge(chunk_done, g0) if g0 else None
                        round_xs(st, XN, 4, range(4))
                    if st.get("fill") and st["fill"]["what"] == "k":
                        cross(g0, u0, pairs[0])
                elif kind == "mem_turn":
                    round_xs(st, XM, 4, range(4))
                elif kind in ("up", "conv", "natural"):
                    def body(i, ss=(0, 1)):
                        for s in ss:
                            if st.get("dest") == "na_v" and s == 1:
                                act.wait_ge(mla_t, 4)
                                A(region(R["mla_qT"], 2048)[0:96, :],
                                  PS[0:96, 4:8, :].rearrange("p b n -> p (b n)"),
                                  ACT.Copy).then_inc(mla_a, 1)
                            ahead(g0 + 2 * i + s, slots[s])
                            if kind == "up" and s == 1 and st.get("next_attend"):
                                exps(st["next_attend"]["a0"])
                            if kind != "natural":
                                cross(g0 + 2 * i + s, u0 + 2 * i + s, pairs[s])
                            if st.get("dest") == "latent" and s == 0:
                                for t in range(TT):
                                    square(mem_scale, t)
                    early = st.get("next_down")
                    repeat(act, n // 2 - bool(early and n > 1), body, straight=g0 == 0)
                    if early:
                        stage_early(early)
                        if n > 1:
                            body(n // 2 - 1)
                    if n % 2:
                        body(n // 2, (0,))
                elif kind == "glu":
                    def body(i):
                        for s in range(2):
                            ahead(g0 + 2 * i + s, slots[s])
                            if s == 1:
                                act.wait_ge(acc_read, st["u"] + 2 * i + 1)
                                act.wait_ge(h_done, st["h0"] + i)
                                A(T3, T1, ACT.Silu).then_inc(silu_out, 1)
                            cross(g0 + 2 * i + s, u0 + 2 * i + s, pairs[s])
                    A(ST[:, 60:61], G[:, 0:1], ACT.Silu)
                    repeat(act, n // 2 - 1, body)
                    stage_early(st["next_down"])
                    body(n // 2 - 1)
                elif kind == "dilated_in":
                    def keep(i, b):
                        act.wait_ge(rope_tr, 4 * i + b + 1)
                        at = i * DIL_SIZE + (DIL0 + (b // 2) * 2048 + (b % 2) * 1024)
                        A(U[:, bass.ds(at, 1024)],
                          PS[:, 4 + 2 * (b % 2):6 + 2 * (b % 2), :].rearrange("p b n -> p (b n)"),
                          ACT.Copy).then_inc(rope_kept, 1)

                    def body(i):
                        for b in range(6):
                            for c in range(2):
                                ahead(g0 + 12 * i + 2 * b + c, slots[c])
                                if c == 0 and b >= 2:
                                    keep(i, b - 2)
                    repeat(act, DIL_G, body)
                elif kind == "down":
                    def body(i):
                        for s in range(2):
                            ahead(g0 + 2 * i + s, slots[s])
                            stage_hi(st, 2 * i + s + 2, g0 + 2 * i + s + 2, slots[s])
                    rounds = max(n - 2, 0) // 2
                    repeat(act, rounds, body)
                    for j in range(2 * rounds, n):
                        ahead(g0 + j, (g0 + j) % 2)
                        if j + 2 < n:
                            stage_hi(st, j + 2, g0 + j + 2, (g0 + j) % 2)
                elif kind == "forget":
                    ahead(g0, slots[0])
                    act.wait_ge(f_v, 1)
                    A(T1[:, 32:48], T1[:, 16:32], ACT.Exp, scale=-1.0).then_inc(f_a, 1)
                    act.wait_ge(f_a, 1)
                    A(T1[:, 48:64], T1[:, 32:48], ACT.Ln, bias=1.0).then_inc(f_a, 1)
                elif kind == "mla_in":
                    act.wait_ge(acc_read, st["u"])
                    lat = region(R["latent"], 832)
                    for t in range(TT):
                        A(T1[:, t * 256:(t + 1) * 256], lat[:, t * 416:t * 416 + 256], ACT.Square,
                          accum_out=ST[:, 4 + t:5 + t])
                        last = A(T2[:, t * 256:t * 256 + P], lat[:, t * 416 + 256:t * 416 + 384],
                                 ACT.Square, accum_out=ST[:, 6 + t:7 + t])
                    last.then_inc(mla_a, 1)
                elif kind == "mla_k":
                    stage_early(st["next_down"])
                elif kind == "attend":
                    a0, m = st["a0"], len(st["what"])

                    if stages[stages.index(st) - 1]["kind"] != "up":
                        exps(a0)
                    exps(a0 + 1)
                    for n_ in range(a0, a0 + m):
                        keep_pt(n_)
                        if n_ + 2 < a0 + m:
                            exps(n_ + 2)
                        if n_ == a0 + m - 3:
                            stage_early(st["next_down"])

        @block.vector
        def _(dve):
            V = nc.vector
            chain = Count(dve_chain)
            V.memset(T[:, 0:512], 0.0).then_inc(warm, 1)

            def link(ins):
                chain.inc(ins)
                dve.wait_ge(dve_chain, chain.value())

            def split_lo(g, slot):
                for h in range(2):
                    dve.wait_ge(w_hi, 2 * g + h + 1)
                    V.tensor_tensor(W_lo[:, slot, halves(h)], W_raw[:, slot, halves(h)],
                                    W_hi[:, slot, halves(h)], ALU.subtract).then_inc(w_lo, 1)

            def ahead(g, slot):
                if not isinstance(g, int) or g + 1 < G_TOTAL:
                    split_lo(g + 1, 1 - slot)

            def add_halves(st, dst, u, pair):
                dve.wait_ge(cross_out, u - st["u"] + st["cross0"] + 1)
                return V.tensor_tensor(dst.rearrange("p (f t) -> p f t", f=2),
                                       PS[:, 2 * pair:2 * pair + 2, 0:S],
                                       T0[:, pair, :].rearrange("p (f t) -> p f t", f=2), ALU.add)

            def rest_xs(st, dst, bank, b):
                dve.wait_ge(n_hi, 4 * st["turn"] + b + 1)
                for k in (2 * b, 2 * b + 1):
                    last = V.scalar_tensor_tensor(
                        tokens_out(st, dst[:, k, 1, :]),
                        tokens_in(st, PS[:, bank, (k % 2) * S:(k % 2 + 1) * S]),
                        G[:, st["gain"] + k:st["gain"] + k + 1], tokens_out(st, dst[:, k, 0, :]),
                        ALU.mult, ALU.subtract)
                return last

            def soft(n):
                e = heads[n]
                dve.wait_ge(s_score, n + 1)
                if n >= 3:
                    back = heads[n - 3]
                    dve.wait_ge(s_pt, back["group0"] + back["parts"])
                sc = e["scores"].rearrange("p (t n) -> p t n", t=2)
                pr = e["probs"].rearrange("p (t n) -> p t n", t=2)
                if e["bias"] is None:
                    link(V.tensor_reduce(e["mx"], sc, AXIS.X, ALU.max, negate=True))
                    V.tensor_scalar(e["mx"], e["mx"], e["scale"], None,
                                    ALU.mult).then_inc(s_soft, 1)
                    return
                if e["bias"] == "dil":
                    V.scalar_tensor_tensor(e["probs"], e["scores"], e["scale"],
                                           const("dil"), ALU.mult, ALU.add
                                           ).then_inc(s_read, 1)
                elif e["bias"] == "na":
                    if e["h"] == 0:
                        dve.wait_ge(bias_ready, 1)
                    for t in range(TT):
                        at = R["na_bias"] + e["h"] * SLOTS * GRID + (2 - 2 * t) * GRID
                        last = V.scalar_tensor_tensor(pr[:, t, :], sc[:, t, :], e["scale"],
                                                      region(at, S), ALU.mult, ALU.add)
                    last.then_inc(s_read, 1)
                else:
                    ck, cols = region(RB["ck"] + e["h"] * S, S), e["cols"]
                    for t in range(TT):
                        n_keys = slice(0, cols[t].stop - cols[t].start)
                        last = V.scalar_tensor_tensor(e["probs"][:, cols[t]], e["scores"][:, cols[t]],
                                                      e["scale"], ck[:, n_keys],
                                                      ALU.mult, ALU.subtract)
                    last.then_inc(s_read, 1)
                    dve.wait_ge(s_read, e["read"] + 1)
                    for t in range(TT):
                        col = 32 + t * 8 + e["h"]
                        n_keys = slice(t * S, t * S + cols[t].stop - cols[t].start)
                        last = V.scalar_tensor_tensor(
                            e["probs"][:, cols[t]], e["probs"][:, cols[t]], ST[:, col:col + 1],
                            const("causal")[:, n_keys], ALU.add, ALU.add)
                    link(last)
                    for t in range(TT):
                        last = V.tensor_reduce(e["mx"][:, t:t + 1], e["probs"][:, cols[t]], AXIS.X,
                                               ALU.max, negate=True)
                    last.then_inc(s_soft, 1)
                    return
                dve.wait_ge(s_read, e["read"] + 1)
                V.tensor_reduce(e["mx"], pr, AXIS.X, ALU.max, negate=True).then_inc(s_soft, 1)

            def normalise(n):
                e = heads[n]
                dve.wait_ge(s_exp, 2 * n + 2)
                link(V.reciprocal(e["rz"], e["z"]))
                for t in range(TT):
                    pr = e["probs"][:, e["cols"][t]]
                    last = V.tensor_scalar(pr, pr, e["rz"][:, t:t + 1], None, ALU.mult)
                last.then_inc(s_norm, 1)

            def output(n):
                e = heads[n]
                dve.wait_ge(s_pv, n + 1)
                d = e["y"].shape[0]
                y, o = e["y"], PS[e["pb"]:e["pb"] + d, 2 + n % 2, 0:S]
                if e["bias"] == "dil":
                    y = y.rearrange("p (j r) -> p r j", r=RES)
                    o = o.rearrange("p (r j) -> p r j", r=RES)
                V.tensor_copy(y, o).then_inc(h_done, 1)

            def open_attention(st):
                if st["name"] == "memory0":
                    dve.wait_ge(conv_cu_done, 4)
                soft(st["a0"])
                soft(st["a0"] + 1)

            def rope32(dst, x, t, h, complete=False):
                cos, sin = const("cosm"), const("sinm")
                m1 = T1[:, 0:h * 32].rearrange("p (h d) -> p h d", h=h)
                m2 = T2[:, 0:h * 32].rearrange("p (h d) -> p h d", h=h)
                tab = lambda c, lo, hi: (c[:, t * 32 + lo:t * 32 + hi].unsqueeze(1)
                                         .to_broadcast([P, h, hi - lo]))
                V.tensor_tensor(m1, x, tab(cos, 0, 32), ALU.mult)
                V.tensor_tensor(m2[:, :, 0:16], x[:, :, 16:32], tab(sin, 0, 16), ALU.mult)
                link(V.tensor_tensor(m2[:, :, 16:32], x[:, :, 0:16], tab(sin, 16, 32), ALU.mult))
                last = V.tensor_tensor(dst, m1, m2, ALU.add)
                last.then_inc(mla_p, 1) if complete else link(last)

            def scale_latents():
                lat = region(R["latent"], 832)
                lat_s = region(R["lat_s"], 768)
                dve.wait_ge(mla_r, 2)
                for t in range(TT):
                    rope32(KPE[:, t * 32:(t + 1) * 32].unsqueeze(1),
                           lat[:, t * 416 + 384:t * 416 + 416].unsqueeze(1), t, 1)
                for t in range(TT):
                    V.tensor_scalar(lat_s[:, t * 384:t * 384 + 256], lat[:, t * 416:t * 416 + 256],
                                    ST[:, 4 + t:5 + t], None, ALU.mult)
                    last = V.tensor_scalar(lat_s[:, t * 384 + 256:t * 384 + 384],
                                           lat[:, t * 416 + 256:t * 416 + 384],
                                           ST[:, 6 + t:7 + t], None, ALU.mult)
                last.then_inc(mla_p, 1)

            dve.wait_ge(first_in, 32)
            for st in stages:
                g0, u0, n, kind = st["g"], st["u"], st["n"], st["kind"]
                slots, pairs = (g0 % 2, (g0 + 1) % 2), (u0 % 2, (u0 + 1) % 2)
                if kind in ("norm", "final", "mem_scale"):
                    i, again = st["i"], st.get("again")
                    src = MEM if kind == "mem_scale" else X
                    if kind == "final":
                        dve.wait_ge(gain_in, 16 * (st["f"] + 1))
                    for t in () if again else range(TT):
                        dve.wait_ge(n_rstd, 2 * i + t + 1)
                        V.tensor_scalar(XS[:, t, :], src[:, t, :], ST[:, 2 * t:2 * t + 1], None,
                                        ALU.mult).then_inc(n_scaled, 1)
                        if kind == "final":
                            dve.wait_ge(n_scaled, 2 * i + t + 1)
                            for b in range(2):
                                h = slice(b * 512, b * 512 + 512)
                                V.tensor_tensor(X[:, t, h], XS[:, t, h], GF[:, h],
                                                ALU.mult).then_inc(x_new, 1)
                    if i == 0:
                        split_lo(0, 0)
                    if st.get("fill"):
                        ahead(g0, slots[0])
                    if kind == "norm":
                        for b in range(4):
                            rest_xs(st, XN, 4 + b, b).then_inc(n_lo, 1)
                    if st.get("fill"):
                        f = st["fill"]
                        at = RB[f"mem_{f['what']}{f['l']}"]
                        if f["what"] == "k":
                            add_halves(st, region(at + f["c"] * 512, 512), u0, pairs[0]
                                       ).then_inc(acc_read, 1)
                        else:
                            dve.wait_ge(chunk_done, g0 + 1)
                            dst = region(at, 1024).rearrange("p (t n) -> p t n", t=2)
                            V.tensor_copy(dst[:, :, f["c"] * TCOLS:(f["c"] + 1) * TCOLS],
                                          PS[:, 2 * pairs[0]:2 * pairs[0] + 2, 0:TCOLS]
                                          ).then_inc(acc_read, 1)
                elif kind == "mem_turn":
                    for b in range(4):
                        rest_xs(st, XM, 4 + b, b).then_inc(xm_done, 1)
                elif kind == "up":
                    at = dest_at[st["dest"]] + st.get("at", 0)

                    def body(i, ss=(0, 1)):
                        for s in ss:
                            g, c = g0 + 2 * i + s, 2 * i + s
                            ahead(g, slots[s])
                            if st.get("latents"):
                                scale_latents()
                            if s == 1 and st.get("next_attend"):
                                open_attention(st["next_attend"])
                            dve.wait_ge(chunk_done, g + 1)
                            dst = U[:, bass.ds(at + c * 512, 512)]
                            if st["post"] == "copy":
                                add_halves(st, dst, u0 + c, pairs[s]).then_inc(acc_read, 1)
                            else:
                                dve.wait_ge(h_done, st["h0"] + c)
                                add_halves(st, T1, u0 + c, pairs[s]).then_inc(acc_read, 1)
                                dve.wait_ge(acc_read, u0 + c + 1)
                                V.scalar_tensor_tensor(dst, T1, 0.0, T1, ALU.max,
                                                       ALU.mult).then_inc(h_done, 1)
                    repeat(dve, n // 2, body)
                    if n % 2:
                        body(n // 2, (0,))
                elif kind == "glu":
                    def body(i):
                        ahead(g0 + 2 * i, slots[0])
                        dve.wait_ge(chunk_done, g0 + 2 * i + 1)
                        dve.wait_ge(h_done, st["h0"] + i)
                        add_halves(st, T1, u0 + 2 * i, pairs[0]).then_inc(acc_read, 1)
                        ahead(g0 + 2 * i + 1, slots[1])
                        dve.wait_ge(chunk_done, g0 + 2 * i + 2)
                        add_halves(st, T2, u0 + 2 * i + 1, pairs[1]).then_inc(acc_read, 1)
                        dve.wait_ge(acc_read, u0 + 2 * i + 2)
                        dve.wait_ge(silu_out, st["silu0"] + i + 1)
                        V.tensor_tensor(U[:, bass.ds(H0 + i * 512, 512)], T3, T2,
                                        ALU.mult).then_inc(h_done, 1)
                    repeat(dve, n // 2, body)
                elif kind == "natural":
                    ncols = st["ncols"]
                    for b in range(st["blocks"]):
                        for c in range(2):
                            ahead(g0 + 2 * b + c, slots[c])
                        if st.get("next_attend"):
                            open_attention(st["next_attend"])
                        dve.wait_ge(chunk_done, g0 + 2 * b + 2)
                        p = (u0 + b) % 2
                        at = dest_at[st["dest"]] + b * 1024
                        V.tensor_copy(region(at, 2 * ncols).rearrange("p (t n) -> p t n", t=2),
                                      PS[:, 2 * p:2 * p + 2, 0:ncols]).then_inc(acc_read, 1)
                elif kind == "dilated_in":
                    dve.wait_ge(consts_in, 16)
                    cosd, sind = const("cosd"), const("sind")

                    def wide(table, t, lo, hi):
                        return table[:, t * 64 + lo:t * 64 + hi].unsqueeze(1).to_broadcast([P, 8, hi - lo])

                    def body(i, opens=None):
                        for b in range(6):
                            for c in range(2):
                                ahead(g0 + 12 * i + 2 * b + c, slots[c])
                            if opens and b == 5:
                                open_attention(opens)
                            dve.wait_ge(chunk_done, g0 + 12 * i + 2 * b + 2)
                            p = (u0 + b) % 2
                            if b >= 4:
                                at = i * DIL_SIZE + (DIL0 + 4096 + (b - 4) * 1024)
                                V.tensor_copy(U[:, bass.ds(at, 1024)],
                                              PS[:, 2 * p:2 * p + 2, :].rearrange("p b n -> p (b n)")
                                              ).then_inc(acc_read, 1)
                                continue
                            if b:
                                dve.wait_ge(rope_sum, 4 * i + b)
                            for t in range(TT):
                                x = PS[:, 2 * p + t, :].rearrange("p (h d) -> p h d", h=8)
                                m1 = rope_m1[:, t * 512:(t + 1) * 512].rearrange("p (h d) -> p h d", h=8)
                                m2 = rope_m2[:, t * 512:(t + 1) * 512].rearrange("p (h d) -> p h d", h=8)
                                V.tensor_tensor(m1, x, wide(cosd, t, 0, 64), ALU.mult)
                                V.tensor_tensor(m2[:, :, 0:32], x[:, :, 32:64],
                                                wide(sind, t, 0, 32), ALU.mult)
                                last = V.tensor_tensor(m2[:, :, 32:64], x[:, :, 0:32],
                                                       wide(sind, t, 32, 64), ALU.mult)
                            last.then_inc(acc_read, 1)
                    repeat(dve, DIL_G - 1, body)
                    body(DIL_G - 1, st["next_attend"])
                elif kind == "conv":
                    for c in range(4):
                        for part in range(3):
                            j = 3 * c + part
                            ahead(g0 + j, (g0 + j) % 2)
                            if part == 0 and c >= 2:
                                dve.wait_ge(conv_done, c - 1)
                            if part and c:
                                dve.wait_ge(conv_cu_done, c)
                            dst = (conv_b[:, c % 2, :], T1, T2)[part]
                            add_halves(st, dst, u0 + j, (u0 + j) % 2).then_inc(acc_read, 1)
                elif kind == "down":
                    def body(i):
                        for s in range(2):
                            ahead(g0 + 2 * i + s, slots[s])
                    repeat(dve, n // 2, body)
                    if n % 2:
                        ahead(g0 + n - 1, (g0 + n - 1) % 2)
                    done = 3 * st["down"]
                    for t in range(TT):
                        y = PS[:, 4 + 2 * t:6 + 2 * t, :].rearrange("p b n -> p (b n)")
                        if st["after"] == "x":
                            for b in range(2):
                                if (t, b) != (1, 1):
                                    dve.wait_ge(tile_done, done + 2 * t + b + 1)
                                else:
                                    dve.wait_ge(chunk_done, g0 + n)
                                h = slice(b * 512, b * 512 + 512)
                                V.scalar_tensor_tensor(X[:, t, h], y[:, h], st["scale"], X[:, t, h],
                                                       ALU.mult, ALU.add).then_inc(x_new, 1)
                            continue
                        if t == 0:
                            dve.wait_ge(tile_done, done + 2)
                        else:
                            dve.wait_ge(chunk_done, g0 + n)
                        if st["after"] == "q":
                            V.tensor_copy(region(R["mla_qn"] + t * 768, 768),
                                          y[:, 0:768]).then_inc(x_new, 2)
                        else:
                            yh = y.rearrange("p (h d) -> p h d", h=8)
                            kn = region(R["mla_kn"] + t * 768, 768).rearrange("p (h d) -> p h d", h=8)
                            V.tensor_copy(kn[:, :, 0:64], yh[:, :, 0:64])
                            V.tensor_copy(region(R["mla_v"] + t * 512, 512)
                                          .rearrange("p (h d) -> p h d", h=8),
                                          yh[:, :, 64:128]).then_inc(x_new, 2)
                    if st["after"] == "q":
                        dve.wait_ge(x_new, st["x0"] + 4)
                        for t in range(TT):
                            q = region(R["mla_qn"] + t * 768, 768).rearrange("p (h d) -> p h d", h=8)
                            rope32(q[:, :, 64:96], q[:, :, 64:96], t, 8, t == TT - 1)
                    if st["after"] == "kv":
                        for t in range(TT):
                            kn = region(R["mla_kn"] + t * 768, 768).rearrange("p (h d) -> p h d", h=8)
                            last = V.tensor_copy(kn[:, :, 64:96], KPE[:, t * 32:(t + 1) * 32]
                                                 .unsqueeze(1).to_broadcast([P, 8, 32]))
                        last.then_inc(mla_p, 1)
                elif kind == "mla_turn":
                    dve.wait_ge(mla_t, 1)
                    for b in range(3):
                        col = GAINS["q_norm"] + b if b < 2 else GAINS["ckv_norm"]
                        V.tensor_scalar(region(R["c"] + b * S, S),
                                        PS[:, 4 + b // 2, (b % 2) * S:(b % 2 + 1) * S],
                                        G[:, col:col + 1], None, ALU.mult).then_inc(h_done, 1)
                elif kind == "mla_k":
                    for b in range(2):
                        dve.wait_ge(mla_t, 2 + b)
                        V.tensor_copy(region(R["mla_kT"] + b * 1024, 1024)[0:96, :],
                                      PS[0:96, 2 * pairs[b]:2 * pairs[b] + 2, :]
                                      .rearrange("p b n -> p (b n)")).then_inc(acc_read, 1)
                elif kind == "forget":
                    ahead(g0, slots[0])
                    dve.wait_ge(chunk_done, g0 + 1)
                    p = pairs[0]
                    for t in range(TT):
                        last = V.tensor_tensor(T1[:, t * 8:t * 8 + 8], PS[:, 2 * p + t, 0:8],
                                               G[:, GAINS["b_f"]:GAINS["b_f"] + 8], ALU.add)
                    last.then_inc(acc_read, 1)
                    dve.wait_ge(acc_read, u0 + 1)
                    link(V.tensor_scalar(T1[:, 16:32], T1[:, 0:16], -1.0, None, ALU.mult))
                    V.tensor_tensor(T1[:, 16:32], T1[:, 0:16], T1[:, 16:32], ALU.max).then_inc(f_v, 1)
                    link(V.tensor_scalar(T1[:, 64:80], T1[:, 0:16], 0.0, None, ALU.min))
                elif kind == "sums":
                    dve.wait_ge(f_a, 2)
                    V.tensor_tensor(T1[:, 80:96], T1[:, 64:80], T1[:, 48:64],
                                    ALU.subtract).then_inc(f_v, 1)
                    dve.wait_ge(f_t, 1)
                    V.tensor_copy(ST[:, 32:48], PS[:, 2 * pairs[0], 0:16]).then_inc(acc_read, 1)
                    link(V.tensor_copy(region(RB["ck"], 2048),
                                       PS[:, 4:8, :].rearrange("p b n -> p (b n)")))
                elif kind == "attend":
                    a0, m = st["a0"], len(st["what"])

                    normalise(a0)
                    soft(a0 + 2)
                    for n_ in range(a0, a0 + m):
                        if n_ + 1 < a0 + m:
                            normalise(n_ + 1)
                        if n_ > a0:
                            output(n_ - 1)
                        if n_ + 3 < a0 + m:
                            soft(n_ + 3)
                    output(a0 + m - 1)

        @block.gpsimd
        def _(pool):
            chain = Count(pool_chain)
            nc.gpsimd.memset(W_raw[:, :, 4 * 416:], 0.0).then_inc(raw_tail, 1)
            chain.inc(nc.gpsimd.memset(ST[:, 62:64], -0.5))
            gains = (a["norm_final"], a["final_norm_2"])
            wide = lambda v: v.rearrange("(o n) -> o n", o=1).to_broadcast([P, D])

            def rstd(cols, width, done):
                chain.inc(nc.gpsimd.tensor_scalar(cols, cols, 1.0 / width, EPS, ALU.mult, ALU.add))
                power(cols, done)

            def power(cols, done):
                pool.wait_ge(pool_chain, chain.value())
                nc.gpsimd.tensor_tensor(cols, cols, ST[:, 62:62 + cols.shape[1]], ALU.pow).then_inc(done, 1)

            pool.wait_ge(x_in[1], 16)
            pool.dma_start(MEM, a["mem_2"][0].rearrange("(t p) n -> p t n", p=P)).then_inc(mem_in, 16)
            for st in stages:
                g0, n, kind = st["g"], st["n"], st["kind"]
                if kind in ("norm", "final", "mem_scale") and not st.get("again"):
                    for t in range(TT):
                        pool.wait_ge(n_sq, 4 * st["i"] + 2 * t + 2)
                        chain.inc(nc.gpsimd.tensor_scalar(ST[:, 2 * t:2 * t + 1], ST[:, 2 * t:2 * t + 1],
                                                          ST[:, 2 * t + 1:2 * t + 2], EPS,
                                                          ALU.add, ALU.add))
                        power(ST[:, 2 * t:2 * t + 1], n_rstd)
                if kind == "mla_in":
                    pool.wait_ge(mla_a, 1)
                    rstd(ST[:, 4:6], 256, mla_r)
                    rstd(ST[:, 6:8], 128, mla_r)
                if st["name"] == "na_v":
                    bias = region(R["na_bias"], NA_H * SLOTS * GRID)
                    pool.dma_start(bias, a["na_bias"]).then_inc(bias_in, 16)
                    pool.dma_start(K[:, FIRST:], a["const"][:, FIRST:]).then_inc(consts_in, 16)
                    pool.wait_ge(first_in, 32)
                    pool.wait_ge(bias_in, 16)
                    rows = NA_H * SLOTS
                    view = bias.rearrange("p (r n) -> p r n", r=rows)
                    window = const("window").unsqueeze(1).to_broadcast([P, rows, GRID])
                    nc.gpsimd.tensor_tensor(view, view, window, ALU.add).then_inc(bias_ready, 1)
                if kind == "down":
                    def body(i, js=(0, 1)):
                        for s in js:
                            j, slot = 2 * i + s, (g0 + s) % 2
                            pool.wait_ge(st_hi, st["staged0"] + j + 1)
                            nc.gpsimd.tensor_tensor(SX[:, slot, 1, 0:st["ks"] * S], down_src(st, j),
                                                    SX[:, slot, 0, 0:st["ks"] * S],
                                                    ALU.subtract).then_inc(st_lo, 1)
                    repeat(pool, n // 2, body)
                    if n % 2:
                        body(n // 2, (0,))
                    if st["name"] in ("od_o", "b_out"):
                        pool.wait_ge(x_new, st["x0"] + 4)
                        pool.dma_start(GF, wide(gains[st["name"] == "b_out"])).then_inc(gain_in, 16)
                elif kind == "conv":
                    Pg = nc.gpsimd
                    T2v = [t.rearrange("p (f t) -> p f t", f=2) for t in (T1, T2)]

                    def step(ins):
                        chain.inc(ins)
                        pool.wait_ge(pool_chain, chain.value())

                    step(Pg.memset(conv_cu[:, :, 0:2], 0.0))
                    for c in range(4):
                        pool.wait_ge(acc_read, st["u"] + 3 * c + 3)
                        Pg.tensor_tensor(conv_cu[:, :, 2:S + 2], T2v[0], T2v[1],
                                         ALU.mult).then_inc(conv_cu_done, 1)
                        pool.wait_ge(conv_cu_done, c + 1)
                        for tap in (2, 1, 0):
                            dst = conv_acc if tap == 2 else conv_tap
                            for f in range(2):
                                col = GAINS["conv"] + tap * KD + 2 * c + f
                                last = Pg.tensor_scalar(dst[:, f, :], conv_cu[:, f, tap:tap + S],
                                                        G[:, col:col + 1], None, ALU.mult)
                            step(last)
                            if tap != 2:
                                step(Pg.tensor_tensor(conv_acc, conv_acc, conv_tap, ALU.add))
                        Pg.tensor_tensor(region(H0 + c * 512, 512),
                                         conv_acc.rearrange("p f t -> p (f t)"),
                                         conv_b[:, c % 2, :], ALU.mult).then_inc(conv_done, 1)
                        pool.wait_ge(conv_done, c + 1)
                elif kind == "dilated_in":
                    def body(i):
                        for b in range(4):
                            pool.wait_ge(acc_read, st["u"] + 6 * i + b + 1)
                            if b >= 2:
                                pool.wait_ge(rope_tr, 4 * i + b - 1)
                            nc.gpsimd.tensor_tensor(rope_out[:, b % 2, :], rope_m1, rope_m2,
                                                    ALU.add).then_inc(rope_sum, 1)
                    repeat(pool, DIL_G, body)


def _constants():
    p, k = np.arange(P), np.arange(S)
    tokens = np.arange(S).reshape(TT, P)
    out = np.zeros((P, NCONST), np.float32)

    def put(name, value):
        lo, hi = CONST[name]
        out[:, lo:hi] = np.asarray(value, np.float32).reshape(P, hi - lo)

    put("ident", np.eye(P))
    q = tokens.T[:, :, None]
    far = k[None, None, :] - q
    order = np.arange(S).reshape(-1, RES).T.reshape(-1)
    tiles = order.reshape(TT, P)
    far_all = order[None, None, :] - tiles.T[:, :, None]
    far_own = tiles[None, :, :] - tiles.T[:, :, None]
    put("dil", np.concatenate([np.where(ok, 0.0, NEG) for ok in
                               (np.abs(far_all) <= 64, far_own % 4 == 0, far_own % 16 == 0)], axis=2))
    put("causal", np.where(far <= 0, 0.0, NEG))
    c = p % GRID
    start = np.clip(c - 8, 0, GRID - 16)[:, None]
    col = np.arange(GRID)[None, :]
    put("window", np.where((col >= start) & (col < start + 16), 0.0, NEG))
    for name, dim in (("d", 64), ("m", 32)):
        inv = np.float32(1.0) / np.float32(10000.0) ** (np.arange(0, dim, 2, dtype=np.float32)
                                                        / np.float32(dim))
        pos = (order if name == "d" else np.arange(S)).astype(np.float32)
        ang = pos[:, None] * inv[None, :].astype(np.float32)
        cos, sin = np.cos(ang).astype(np.float32), np.sin(ang).astype(np.float32)
        cos = np.concatenate([cos, cos], 1).reshape(TT, P, dim).transpose(1, 0, 2)
        sin = np.concatenate([-sin, sin], 1).reshape(TT, P, dim).transpose(1, 0, 2)
        put("cos" + name, cos)
        put("sin" + name, sin)
    put("tri", (tokens.T[:, :, None] <= k[None, None, :]))
    return out


_WEIGHTS = ["x", "norm_final", "ev_w_in", "ev_w_uq", "ev_w_ukv", "ev_w_o", "od_w_in", "od_w_o",
            "mlp_w1", "mlp_w2", "mem_2", "ffn_w_gate_up_2", "ffn_w_down_2", "mem_w_kv_2",
            "a_w_in_2", "a_w_out_2", "w_kvf_2", "b_w_q_2", "b_w_out_2", "final_norm_2"]


def kernel(**inputs):
    import concourse.bacc as bacc
    from concourse.bass_utils import run_bass_kernel_spmd

    x = {k: np.asarray(v) for k, v in inputs.items()}
    cols = lambda v: v.reshape(-1, P).T
    gains = np.concatenate(
        [cols(x["norm_mix"][0]), cols(x["norm_mix"][1]), cols(x["norm_mlp"][0]),
         cols(x["norm_mlp"][1])]
        + [cols(x["ffn_norm_2"][l, i]) for l in range(2) for i in range(2)]
        + [cols(x["mix_norm_2"][0]), cols(x["mix_norm_2"][1]), cols(x["mem_norm_2"]),
           cols(x["kv_norm_2"]), cols(x["ev_q_norm"][0]), cols(x["ev_kv_norm"][0])]
        + [cols(x["a_conv_w_2"][0, j]) for j in range(3)]
        + [np.broadcast_to(x["b_f_2"], (P, 8))], axis=1)
    rel = np.clip(np.arange(GRID)[None, :] - np.arange(GRID)[:, None] + 15, 0, 30)
    rpb = x["ev_rpb"][0]
    na = [np.take(rpb[:, first:first + SLOTS], rel, axis=2).transpose(2, 0, 1, 3)
          for first in (5, 4)]
    arrays = {k: np.ascontiguousarray(x[k]) for k in _WEIGHTS}
    arrays["gains"] = np.ascontiguousarray(gains)
    arrays["na_bias"] = np.ascontiguousarray(np.concatenate(na, axis=0).reshape(P, -1))
    arrays["const"] = _constants()

    nc = bacc.Bacc("TRN2", target_bir_lowering=False, num_devices=1)
    handles = {k: nc.dram_tensor(f"in_{k}", v.shape, mybir.dt.from_np(v.dtype),
                                 kind="ExternalInput").ap() for k, v in arrays.items()}
    out = nc.dram_tensor("out_x", (1, S, D), F32, kind="ExternalOutput").ap()
    build_program(nc, handles, out)
    r = run_bass_kernel_spmd(nc, [{f"in_{k}": v for k, v in arrays.items()}], core_ids=[0])
    return r.results[0]["out_x"]
```
